# Optimizing a Trainium2 kernel written in Bass

```python
import functools
import jax
import jax.numpy as jnp
from jax import lax
import numpy as np

D_MODEL = 1024
BATCH = 1
SEQ = 1024
DEPTH = 2
DEC_BATCH = 8
DEC_SEQ = 4
PAST_LEN = 4096
PAGE_SIZE = 128

N_META = 16
N_AB = (DEPTH + 1) // 2
N_POOL = DEPTH // 2
H_A = 8
Q_LORA = 384
KV_LORA = 256
NOPE_DIM = 64
ROPE_DIM = 32
V_DIM = 64
ROPE_BASE = 10000.0
Q_BLOCK = 128
SM_SCALE = (NOPE_DIM + ROPE_DIM) ** -0.5
H_B = 8
N_B = 64
D_B = H_B * N_B
DECAY_LORA = 64
AAA_LORA = 64
GATE_LORA = 160
RWKV_IN = 3 * D_B + DECAY_LORA + AAA_LORA + GATE_LORA
MLA_IN = Q_LORA + KV_LORA + ROPE_DIM
N_IN = MLA_IN + RWKV_IN
D_MIX = H_A * V_DIM + D_B
GN_EPS = 64e-5
POOL_WINDOWS = (2, 4, 8, 16)
N_POOL_GROUPS = 4
POOL_GC = D_MODEL // N_POOL_GROUPS
W_MAX = 16
D_FF = 4 * D_MODEL
RMS_EPS = 1e-6

kernel_name = 'hybrid_mla_rwkv7_pool_step'

def rms_norm(x, g):
    xf = x.astype(jnp.float32)
    y = xf * lax.rsqrt(jnp.mean(xf * xf, axis=-1, keepdims=True) + RMS_EPS)
    return (y * g.astype(jnp.float32)).astype(x.dtype)

def rope_angles(pos):
    half = ROPE_DIM // 2
    inv = ROPE_BASE ** (-jnp.arange(half, dtype=jnp.float32) / half)
    ang = pos[:, None] * inv[None, :]
    return jnp.cos(ang), jnp.sin(ang)

def apply_rope(x, cos, sin):
    half = ROPE_DIM // 2
    xf = x.astype(jnp.float32)
    x1, x2 = xf[..., :half], xf[..., half:]
    return jnp.concatenate([x1 * cos - x2 * sin, x2 * cos + x1 * sin], axis=-1).astype(x.dtype)

def ab_project(h, cos, sin, w_in, g_q, w_uq, g_kv, w_uk):
    b, t, _ = h.shape
    z = h @ w_in
    zq = z[..., :Q_LORA]
    zkv = z[..., Q_LORA:Q_LORA + KV_LORA]
    zpe = z[..., Q_LORA + KV_LORA:MLA_IN]
    zb = z[..., MLA_IN:]
    q = (rms_norm(zq, g_q) @ w_uq).reshape(b, t, H_A, NOPE_DIM + ROPE_DIM)
    q_nope = q[..., :NOPE_DIM]
    q_pe = apply_rope(q[..., NOPE_DIM:], cos[:, None, :], sin[:, None, :])
    q_lat = jnp.einsum('bthn,rhn->bthr', q_nope, w_uk)
    c_kv = rms_norm(zkv, g_kv)
    k_pe = apply_rope(zpe, cos, sin)
    return q_lat, q_pe, c_kv, k_pe, zb

def mla_attend_prompt(q_lat, q_pe, c_kv, k_pe):
    b, seq = c_kv.shape[0], c_kv.shape[1]
    n_blk = -(-seq // Q_BLOCK)
    lp = n_blk * Q_BLOCK

    def to_blocks(u):
        u = jnp.pad(u, ((0, 0), (0, lp - seq), (0, 0), (0, 0)))
        return jnp.swapaxes(u.reshape((b, n_blk, Q_BLOCK) + u.shape[2:]), 0, 1)

    key_pos = jnp.arange(seq)

    def block(args):
        ql, qp, i = args
        q_pos = i * Q_BLOCK + jnp.arange(Q_BLOCK)
        s = jnp.einsum('bqhr,bkr->bhqk', ql, c_kv) + jnp.einsum('bqhp,bkp->bhqk', qp, k_pe)
        s = jnp.where(key_pos[None, :] <= q_pos[:, None], s.astype(jnp.float32) * SM_SCALE, -jnp.inf)
        p = jax.nn.softmax(s, axis=-1).astype(c_kv.dtype)
        return jnp.einsum('bhqk,bkr->bqhr', p, c_kv)

    out = lax.map(block, (to_blocks(q_lat), to_blocks(q_pe), jnp.arange(n_blk)))
    return jnp.swapaxes(out, 0, 1).reshape(b, lp, H_A, KV_LORA)[:, :seq]

def mla_attend_sample(q_lat, q_pe, c_new, kpe_new, *, ckv_pool, kpe_pool, page_table):
    db, n_pages = page_table.shape
    c_past = ckv_pool[page_table].reshape(db, n_pages * PAGE_SIZE, KV_LORA)
    k_past = kpe_pool[page_table].reshape(db, n_pages * PAGE_SIZE, ROPE_DIM)
    t = q_lat.shape[1]
    s_past = jnp.einsum('bqhr,bkr->bhqk', q_lat, c_past) + jnp.einsum('bqhp,bkp->bhqk', q_pe, k_past)
    s_new = jnp.einsum('bqhr,bkr->bhqk', q_lat, c_new) + jnp.einsum('bqhp,bkp->bhqk', q_pe, kpe_new)
    causal = jnp.arange(t)[None, :] <= jnp.arange(t)[:, None]
    s_new = jnp.where(causal, s_new.astype(jnp.float32) * SM_SCALE, -jnp.inf)
    s = jnp.concatenate([s_past.astype(jnp.float32) * SM_SCALE, s_new], axis=-1)
    p = jax.nn.softmax(s, axis=-1).astype(c_new.dtype)
    n_past = c_past.shape[1]
    return (jnp.einsum('bhqk,bkr->bqhr', p[..., :n_past], c_past)
            + jnp.einsum('bhqk,bkr->bqhr', p[..., n_past:], c_new))

def rwkv7_mix(zb, prev_row, s0, mu, w0, w2, a0, a2, g2, k_k, k_a, r_k, ln_w, ln_b):
    b, t, _ = zb.shape
    prev = jnp.concatenate([prev_row[:, None, :].astype(zb.dtype), zb[:, :-1]], axis=1)
    xm = zb + (prev - zb) * mu
    o1, o2, o3 = D_B, 2 * D_B, 3 * D_B
    o4 = o3 + DECAY_LORA
    o5 = o4 + AAA_LORA
    r, k, v = xm[..., :o1], xm[..., o1:o2], xm[..., o2:o3]
    xw, xa, xg = xm[..., o3:o4], xm[..., o4:o5], xm[..., o5:]
    w_log = -jax.nn.softplus(-(w0 + jnp.tanh(xw) @ w2).astype(jnp.float32)) - 0.5
    decay = jnp.exp(-jnp.exp(w_log))
    a = jax.nn.sigmoid((a0 + xa @ a2).astype(jnp.float32))
    g = jax.nn.sigmoid(xg) @ g2

    def heads(u):
        return u.reshape(b, t, H_B, N_B)

    kf = k.astype(jnp.float32)
    kk = heads(kf * k_k)
    kk = kk / jnp.maximum(jnp.sqrt(jnp.sum(kk * kk, axis=-1, keepdims=True)), 1e-12)
    k_eff = heads(kf * (1.0 + (a - 1.0) * k_a))
    a_h = heads(a)
    rf = heads(r.astype(jnp.float32))
    vf = heads(v.astype(jnp.float32))
    dec = heads(decay)

    def step(S, inp):
        r_t, w_t, k_t, v_t, kk_t, a_t = inp
        sa = jnp.einsum('bhvk,bhk->bhv', S, kk_t)
        S = (S * w_t[:, :, None, :] - sa[..., None] * (kk_t * a_t)[:, :, None, :]
             + v_t[..., None] * k_t[:, :, None, :])
        return S, jnp.einsum('bhvk,bhk->bhv', S, r_t)

    xs_t = (jnp.moveaxis(rf, 1, 0), jnp.moveaxis(dec, 1, 0), jnp.moveaxis(k_eff, 1, 0),
            jnp.moveaxis(vf, 1, 0), jnp.moveaxis(kk, 1, 0), jnp.moveaxis(a_h, 1, 0))
    s_fin, y = lax.scan(step, s0.astype(jnp.float32), xs_t)
    y = jnp.moveaxis(y, 0, 1)
    mean = jnp.mean(y, axis=-1, keepdims=True)
    var = jnp.mean(jnp.square(y - mean), axis=-1, keepdims=True)
    y = ((y - mean) * lax.rsqrt(var + GN_EPS)).reshape(b, t, D_B) * ln_w + ln_b
    bonus = jnp.sum(rf * k_eff * r_k, axis=-1, keepdims=True) * vf
    out = (y + bonus.reshape(b, t, D_B)) * g.astype(jnp.float32)
    return out.astype(zb.dtype), s_fin.astype(s0.dtype), zb[:, -1]

def ab_mixer(h, cos, sin, attend, prev_row, s0, proj, rw):
    w_in, g_q, w_uq, g_kv, w_uk, w_uv, w_out = proj
    b, t, _ = h.shape
    q_lat, q_pe, c_kv, k_pe, zb = ab_project(h, cos, sin, w_in, g_q, w_uq, g_kv, w_uk)
    o_lat = attend(q_lat, q_pe, c_kv, k_pe)
    o_a = jnp.einsum('bthr,rhv->bthv', o_lat, w_uv).reshape(b, t, H_A * V_DIM)
    o_b, s_fin, last = rwkv7_mix(zb, prev_row, s0, *rw)
    y = jnp.concatenate([o_a, o_b], axis=-1) @ w_out
    return y, c_kv, k_pe, s_fin, last

def pool_mixer(h, prefix, pos0, w_pool, pool_scale):
    b, t, d = h.shape
    p = prefix.shape[1]
    full = jnp.concatenate([prefix.astype(h.dtype), h], axis=1)
    cs = jnp.cumsum(jnp.pad(full.astype(jnp.float32), ((0, 0), (W_MAX, 0), (0, 0))), axis=1)
    end = cs[:, p + W_MAX:p + W_MAX + t]
    hf = h.astype(jnp.float32)
    pos = pos0 + jnp.arange(t)
    outs = []
    for gi, w in enumerate(POOL_WINDOWS):
        sl = slice(gi * POOL_GC, (gi + 1) * POOL_GC)
        cnt = jnp.minimum(pos + 1, w).astype(jnp.float32)[:, None]
        win = end[..., sl] - cs[:, p + W_MAX - w:p + W_MAX - w + t, sl]
        outs.append(win / cnt - hf[..., sl])
    pooled = jnp.concatenate(outs, axis=-1).astype(h.dtype).reshape(b, t, N_POOL_GROUPS, POOL_GC)
    y = jnp.einsum('btgc,gcd->btgd', pooled, w_pool).reshape(b, t, d) * pool_scale
    return y, full[:, -(W_MAX - 1):]

def channel_mixer(x, g_pre, g_post, w_up, w_down):
    h = rms_norm(x, g_pre)
    y = jnp.square(jax.nn.relu(h @ w_up)) @ w_down
    return x + rms_norm(y, g_post)

def setup_inputs(seed: int = 0) -> dict:
    key = jax.random.key(seed)
    ks = jax.random.split(key, 40)
    f32 = jnp.float32

    def nrm(k, shape, scale=1.0):
        return jax.random.normal(k, shape, f32) * scale

    def gain(k, shape):
        return 1.0 + nrm(k, shape, 0.05)

    n_pages = PAST_LEN // PAGE_SIZE
    n_used = DEC_BATCH * n_pages
    n_pool_pages = n_used + n_used // 4
    page_table = jax.random.permutation(ks[0], n_pool_pages)[:n_used].reshape(DEC_BATCH, n_pages).astype(jnp.int32)
    return {
        'x_prompt': nrm(ks[1], (BATCH, SEQ, D_MODEL)),
        'x_sample': nrm(ks[2], (DEC_BATCH, DEC_SEQ, D_MODEL)),
        'cache_ckv': nrm(ks[3], (N_AB, n_pool_pages, PAGE_SIZE, KV_LORA)),
        'cache_kpe': nrm(ks[4], (N_AB, n_pool_pages, PAGE_SIZE, ROPE_DIM)),
        'page_table': page_table,
        'state_wkv': nrm(ks[5], (N_AB, DEC_BATCH, H_B, N_B, N_B), 0.3),
        'state_shift': nrm(ks[6], (N_AB, DEC_BATCH, RWKV_IN)),
        'state_pool': nrm(ks[7], (N_POOL, DEC_BATCH, W_MAX - 1, D_MODEL)),
        'meta_tokens': nrm(ks[8], (N_META, D_MODEL)),
        'g_mix_pre': gain(ks[9], (DEPTH, D_MODEL)),
        'g_mix_post': gain(ks[10], (DEPTH, D_MODEL)),
        'g_ffn_pre': gain(ks[11], (DEPTH, D_MODEL)),
        'g_ffn_post': gain(ks[12], (DEPTH, D_MODEL)),
        'w_in': nrm(ks[13], (N_AB, D_MODEL, N_IN), D_MODEL ** -0.5),
        'g_q': gain(ks[14], (N_AB, Q_LORA)),
        'w_uq': nrm(ks[15], (N_AB, Q_LORA, H_A * (NOPE_DIM + ROPE_DIM)), Q_LORA ** -0.5),
        'g_kv': gain(ks[16], (N_AB, KV_LORA)),
        'w_uk': nrm(ks[17], (N_AB, KV_LORA, H_A, NOPE_DIM), KV_LORA ** -0.5),
        'w_uv': nrm(ks[18], (N_AB, KV_LORA, H_A, V_DIM), KV_LORA ** -0.5),
        'mu_shift': jax.random.uniform(ks[19], (N_AB, RWKV_IN), f32),
        'w0': jax.random.uniform(ks[20], (N_AB, D_B), f32, minval=-6.0, maxval=1.0),
        'w2': nrm(ks[21], (N_AB, DECAY_LORA, D_B), 0.1),
        'a0': nrm(ks[22], (N_AB, D_B), 0.5),
        'a2': nrm(ks[23], (N_AB, AAA_LORA, D_B), 0.5 * AAA_LORA ** -0.5),
        'g2': nrm(ks[24], (N_AB, GATE_LORA, D_B), GATE_LORA ** -0.5),
        'k_k': 0.85 + nrm(ks[25], (N_AB, D_B), 0.05),
        'k_a': 1.0 + nrm(ks[26], (N_AB, D_B), 0.05),
        'r_k': nrm(ks[27], (N_AB, H_B, N_B), 0.1),
        'ln_w': gain(ks[28], (N_AB, D_B)),
        'ln_b': nrm(ks[29], (N_AB, D_B), 0.01),
        'w_out': nrm(ks[30], (N_AB, D_MIX, D_MODEL), D_MIX ** -0.5),
        'w_pool': nrm(ks[31], (N_POOL, N_POOL_GROUPS, POOL_GC, POOL_GC), POOL_GC ** -0.5),
        'pool_scale': 1.0 + nrm(ks[32], (N_POOL, D_MODEL), 0.1),
        'w_up': nrm(ks[33], (DEPTH, D_MODEL, D_FF), D_MODEL ** -0.5),
        'w_down': nrm(ks[34], (DEPTH, D_FF, D_MODEL), D_FF ** -0.5),
    }

def reference(x_prompt, x_sample, cache_ckv, cache_kpe, page_table, state_wkv, state_shift, state_pool,
              meta_tokens, g_mix_pre, g_mix_post, g_ffn_pre, g_ffn_post,
              w_in, g_q, w_uq, g_kv, w_uk, w_uv, mu_shift, w0, w2, a0, a2, g2, k_k, k_a, r_k,
              ln_w, ln_b, w_out, w_pool, pool_scale, w_up, w_down):
    f32 = jnp.float32
    bp = x_prompt.shape[0]
    meta = jnp.broadcast_to(meta_tokens[None].astype(x_prompt.dtype), (bp, N_META, D_MODEL))
    xp = jnp.concatenate([meta, x_prompt], axis=1)
    xs = x_sample
    seq_p = xp.shape[1]
    t_s = xs.shape[1]
    past = page_table.shape[1] * PAGE_SIZE
    cos_p, sin_p = rope_angles(jnp.arange(seq_p, dtype=f32))
    cos_s, sin_s = rope_angles(past + jnp.arange(t_s, dtype=f32))

    ckv_p, kpe_p, wkv_p, shift_p, pool_p = [], [], [], [], []
    ckv_s, kpe_s, wkv_s, shift_s, pool_s = [], [], [], [], []
    for l in range(DEPTH):
        if l % 2 == 0:
            e = l // 2
            proj = (w_in[e], g_q[e], w_uq[e], g_kv[e], w_uk[e], w_uv[e], w_out[e])
            rw = (mu_shift[e], w0[e], w2[e], a0[e], a2[e], g2[e], k_k[e], k_a[e], r_k[e], ln_w[e], ln_b[e])
            y, c, kp, s_fin, last = ab_mixer(
                rms_norm(xp, g_mix_pre[l]), cos_p, sin_p, mla_attend_prompt,
                jnp.zeros((bp, RWKV_IN), xp.dtype), jnp.zeros((bp, H_B, N_B, N_B), xp.dtype), proj, rw)
            xp = xp + rms_norm(y, g_mix_post[l])
            ckv_p.append(c)
            kpe_p.append(kp)
            wkv_p.append(s_fin)
            shift_p.append(last)
            attend_s = functools.partial(mla_attend_sample, ckv_pool=cache_ckv[e], kpe_pool=cache_kpe[e],
                                         page_table=page_table)
            y, c, kp, s_fin, last = ab_mixer(
                rms_norm(xs, g_mix_pre[l]), cos_s, sin_s, attend_s, state_shift[e], state_wkv[e], proj, rw)
            xs = xs + rms_norm(y, g_mix_post[l])
            ckv_s.append(c)
            kpe_s.append(kp)
            wkv_s.append(s_fin)
            shift_s.append(last)
        else:
            o = l // 2
            h = rms_norm(xp, g_mix_pre[l])
            y, buf = pool_mixer(h, h[:, :0], 0, w_pool[o], pool_scale[o])
            xp = xp + rms_norm(y, g_mix_post[l])
            pool_p.append(buf)
            y, buf = pool_mixer(rms_norm(xs, g_mix_pre[l]), state_pool[o], past, w_pool[o], pool_scale[o])
            xs = xs + rms_norm(y, g_mix_post[l])
            pool_s.append(buf)
        xp = channel_mixer(xp, g_ffn_pre[l], g_ffn_post[l], w_up[l], w_down[l])
        xs = channel_mixer(xs, g_ffn_pre[l], g_ffn_post[l], w_up[l], w_down[l])

    y_prompt = xp[:, N_META:]
    y_sample = xs
    new_ckv_p = jnp.stack(ckv_p)
    new_kpe_p = jnp.stack(kpe_p)
    new_wkv_p = jnp.stack(wkv_p)
    new_shift_p = jnp.stack(shift_p)
    new_pool_p = jnp.stack(pool_p)
    new_ckv_s = jnp.stack(ckv_s)
    new_kpe_s = jnp.stack(kpe_s)
    new_wkv_s = jnp.stack(wkv_s)
    new_shift_s = jnp.stack(shift_s)
    new_pool_s = jnp.stack(pool_s)
    return (y_prompt, y_sample, new_ckv_p, new_kpe_p, new_wkv_p, new_shift_p, new_pool_p,
            new_ckv_s, new_kpe_s, new_wkv_s, new_shift_s, new_pool_s)


_drawn_inputs = setup_inputs


def setup_inputs(seed=0):
    import zlib

    import numpy as np

    out = dict(_drawn_inputs(seed))
    spreads = {}
    factors = {'cache_kpe': 2.789, 'g_q': 7.438, 'ln_b': 7.952}
    for name, (base, spread) in spreads.items():
        noise = np.random.default_rng([zlib.crc32(name.encode()), seed]).standard_normal(out[name].shape)
        drawn = base * np.exp(spread * noise) if base else spread * noise
        out[name] = jnp.asarray(drawn.astype(out[name].dtype))
    for name, factor in factors.items():
        out[name] = (out[name] * factor).astype(out[name].dtype)
    return out
```

```python
from contextlib import ExitStack

import numpy as np

import concourse.bass as bass
from concourse import mybir
from concourse.alu_op_type import AluOpType as ALU

F32 = mybir.dt.float32
ACT = mybir.ActivationFunctionType
AX = mybir.AxisListType

P = 128
D = 1024
KC = D // P
N_META, SEQ = 16, 1024
NP = N_META + SEQ
DB, DS = 8, 4
NS = DB * DS
PAD = 16
S0 = NP + PAD
TP = S0 + NS
TILES = [(0, 364), (364, 362), (726, 362)]
assert sum(n for _, n in TILES) == TP

Q_LORA, KV_LORA, ROPE = 384, 256, 32
H, HD, PAIRS = 8, 64, 4
NOPE = 64
D_B = H * HD
RW_IN = 3 * D_B + 64 + 64 + 160
PAGE, N_PAGES, POOL_PAGES = 128, 32, 320
SM_SCALE = float((NOPE + ROPE) ** -0.5)
WMAX, WINDOWS = 16, (2, 4, 8, 16)
RMS_EPS, GN_EPS = 1e-6, 64e-5
NEG = -1e30

Z_Q, Z_KV, Z_PE, Z_R, Z_K, Z_V, Z_WA, Z_G, NZ = 0, 3, 5, 6, 10, 14, 18, 19, 20
N_FB = 4
SLABS = 2 * N_FB * KC
RING = 4

VECS = {}
_at = 0
for _name, _n in (("g_mix_pre", 16), ("g_mix_post", 16), ("g_ffn_pre", 16), ("g_ffn_post", 16), ("g_q", 3),
                  ("g_kv", 2), ("mu", 15), ("w0", 4), ("a0", 4), ("k_k", 4), ("k_a", 4), ("r_k", 4),
                  ("ln_w", 4), ("ln_b", 4), ("pool_scale", 8)):
    VECS[_name] = (_at, _n)
    _at += _n
NVEC = _at

CH = 32
RW_LINKS = 22
CONSTS = {}
_at = 0
for _name, _n in (("ident", P), ("ones", P), ("head_ones", P), ("pair_ident", HD), ("grams", 2 * P), ("lower", P),
                  ("level", 5 * P), ("levelT", 5 * P), ("causal", P), ("grams_s", 2 * P), ("lower_s", P),
                  ("resets", P), ("resets_s", HD), ("seq_of", DB), ("new_causal", NS), ("eps", 2),
                  ("ramp", 64)):
    CONSTS[_name] = (_at, _n)
    _at += _n
NCONST = _at


def constants():
    c = np.zeros((P, NCONST), np.float32)

    def put(name, a):
        at, n = CONSTS[name]
        c[:a.shape[0], at:at + n] = a

    s, t = np.arange(P)[:, None], np.arange(P)[None, :]
    put("ident", np.eye(P))
    put("ones", np.ones((P, P)))
    put("head_ones", (s // HD == t // HD))
    put("pair_ident", np.tile(np.eye(HD), (2, 1)))
    same = s // CH == t // CH
    put("grams", np.concatenate([same & (s < t), same & (s <= t)], 1))
    put("lower", same & (s > t))
    put("level", np.concatenate([(s // (2 << l) == t // (2 << l)) & (s >> l & 1 == 1) & (t >> l & 1 == 0) for l in range(5)], 1))
    put("levelT", np.concatenate([(s // (2 << l) == t // (2 << l)) & (t >> l & 1 == 1) & (s >> l & 1 == 0) for l in range(5)], 1))
    put("causal", np.where(s >= t, 0.0, NEG))
    same = (s < CH) & (t < CH) | (s // DS == t // DS) & (s >= CH) & (t >= CH)
    put("grams_s", np.concatenate([same & (s < t), same & (s <= t)], 1))
    put("lower_s", same & (s > t))
    put("resets", np.tile(t % CH != 0, (P, 1)))
    col = np.arange(HD)[None, :]
    put("resets_s", np.tile(np.where(col < CH, col % CH != 0, col % DS != 0), (P, 1)))
    put("seq_of", (np.arange(P)[:, None] - CH) // DS == np.arange(DB)[None, :])
    put("new_causal", np.where(np.arange(DS)[:, None] <= np.arange(NS)[None, :] % DS, 0.0, NEG))
    put("eps", np.tile(np.array([[RMS_EPS, GN_EPS]]), (P, 1)))
    put("ramp", np.tile(np.concatenate([1.0 / np.minimum(np.arange(16) + 1, w) for w in WINDOWS])[None, :], (P, 1)))
    return c


def rotary_tables():
    half = ROPE // 2
    inv = (np.float32(10000.0) ** (-np.arange(half, dtype=np.float32) / np.float32(half))).astype(np.float32)
    pos = np.concatenate([np.arange(NP), np.zeros(PAD), np.tile(N_PAGES * PAGE + np.arange(DS), DB)]).astype(np.float32)
    ang = (inv[:, None] * pos[None, :]).astype(np.float32)
    cos, sin = np.cos(ang).astype(np.float32), np.sin(ang).astype(np.float32)
    return np.tile(np.stack([np.concatenate([cos, cos]), np.concatenate([-sin, sin])], 1), (4, 1, 1))


class Counter:

    def __init__(self, nc, ctx, name):
        self.sem = ctx.enter_context(nc.semaphore(name))
        self.base = 0

    def at(self, n):
        return self.base + n

    def passed(self, n):
        self.base += n


class Chain:

    def __init__(self, engine, counter):
        self.engine, self.counter, self.start, self.n = engine, counter, 0, 0

    def link(self, instruction):
        self.n += 1
        instruction.then_inc(self.counter.sem, 1)
        self.engine.wait_ge(self.counter.sem, self.counter.at(self.start + self.n))

    def iteration(self, i, length):
        self.before, self.length = self.start + self.n, length
        self.start, self.n = self.before + i * length, 0

    def loop_over(self, turns):
        assert self.n == self.length, f"this loop's body links {self.n}"
        self.start, self.n = self.before + turns * self.length, 0

    def close(self):
        self.counter.passed(self.start + self.n)


def build(nc, io, stop_after=99):
    with ExitStack() as top:
        Program(nc, io, top).emit(stop_after)


class Program:
    def __init__(self, nc, io, top):
        self.nc, self.io, self.top = nc, io, top
        self.vec = self.sb(top, "vec", [P, NVEC])
        self.const = self.sb(top, "const", [P, NCONST])
        self.ps = top.enter_context(nc.psum_tensor("ps", [P, 8, 512], F32))
        self.counters = {}

    def sb(self, ctx, name, shape, dt=F32, side="left"):
        return ctx.enter_context(self.nc.sbuf_tensor(name, shape, dt, side=side))

    def counter(self, name):
        if name not in self.counters:
            self.counters[name] = Counter(self.nc, self.top, name)
        return self.counters[name]

    FREED = ("emptied", "relu_done", "y_added", "s_pv")

    def v(self, name, k=0, n=1):
        at = VECS[name][0] + k
        return self.vec[:, at:at + n]

    def c(self, name, rows=slice(0, P), lo=0, hi=None):
        at, n = CONSTS[name]
        return self.const[rows, at + lo:at + (n if hi is None else hi)]

    def load(self):
        nc, io = self.nc, self.io
        loaded = self.counter("loaded")
        with nc.Block() as block:
            @block.sync
            def _(sp):
                for name in self.FREED:
                    sp.sem_inc(self.counter(name).sem, 2)
                    self.counter(name).passed(2)
                sp.dma_start(self.const[:, :], io["const"]).then_inc(loaded.sem, 16)
                sp.dma_start(self.vec[:, :], io["vec"]).then_inc(loaded.sem, 16)
                sp.wait_ge(loaded.sem, loaded.at(32))
        loaded.passed(32)

    def fetch(self, pairs):
        loaded = self.counter("loaded")
        with self.nc.Block() as block:
            @block.sync
            def _(sp):
                for to, of in pairs:
                    sp.dma_start(to, of).then_inc(loaded.sem, 16)
                sp.wait_ge(loaded.sem, loaded.at(16 * len(pairs)))
        loaded.passed(16 * len(pairs))

    def norm(self, name, src, chunks, gain, dst=None):
        nc, ps = self.nc, self.ps
        squared, used, total = (self.counter(n) for n in ("squared", "sq_used", "total"))
        root, scaled, dve_done, pool_done = (self.counter(n) for n in ("root", "scaled", "dve_own", "pool_done"))
        residual = dst is None
        with ExitStack() as ctx:
            sq = self.sb(ctx, f"{name}_sq", [P, 2, TP])
            acc = self.sb(ctx, f"{name}_acc", [P, TP])
            rstd = self.sb(ctx, f"{name}_rstd", [P, TP])
            with nc.Block() as block:
                @block.scalar
                def _(act):
                    for k in range(chunks):
                        if k >= 3:
                            act.wait_ge(used.sem, used.at(k - 2))
                        to = acc[:, :] if k == 0 else sq[:, k % 2, :]
                        nc.scalar.activation(to, src(k), ACT.Square).then_inc(squared.sem, 1)
                    act.wait_ge(total.sem, total.at(1))
                    for n, (at, w) in enumerate(TILES):
                        nc.scalar.activation(rstd[:, at:at + w], ps[:, n, 0:w], ACT.Sqrt, bias=self.c("eps", hi=1),
                                             scale=1.0 / (chunks * P)).then_inc(root.sem, 1)

                @block.tensor
                def _(pe):
                    pe.wait_ge(used.sem, used.at(chunks - 1))
                    for n, (at, w) in enumerate(TILES):
                        last = nc.tensor.matmul(ps[:, n, 0:w], self.c("ones"), acc[:, at:at + w], start=True, stop=True)
                    last.then_inc(total.sem, 1)

                @block.vector
                def _(dve):
                    chain = Chain(dve, dve_done)
                    dve.wait_ge(squared.sem, squared.at(1))
                    for k in range(1, chunks):
                        dve.wait_ge(squared.sem, squared.at(k + 1))
                        if k > 1:
                            dve.wait_ge(used.sem, used.at(k - 1))
                        nc.vector.tensor_tensor(acc[:, :], acc[:, :], sq[:, k % 2, :], ALU.add).then_inc(used.sem, 1)
                    dve.wait_ge(root.sem, root.at(3))
                    chain.link(nc.vector.reciprocal(rstd[:, :], rstd[:, :]))
                    for k in range(chunks):
                        to = src(k) if residual else dst(k)
                        nc.vector.scalar_tensor_tensor(out=to, in0=src(k), scalar=self.v(*gain(k)), in1=rstd[:, :],
                                                       op0=ALU.mult, op1=ALU.mult).then_inc(scaled.sem, 1)
                    dve.wait_ge(scaled.sem, scaled.at(chunks))
                    chain.close()

                if residual:
                    @block.gpsimd
                    def _(pool):
                        for k in range(chunks):
                            pool.wait_ge(scaled.sem, scaled.at(k + 1))
                            nc.gpsimd.tensor_tensor(self.x[:, k, :], self.x[:, k, :], src(k), ALU.add).then_inc(pool_done.sem, 1)
                        pool.wait_ge(pool_done.sem, pool_done.at(chunks))
            squared.passed(chunks), used.passed(chunks - 1)
            total.passed(1), root.passed(3), scaled.passed(chunks)
            if residual:
                pool_done.passed(chunks)

    def gemm(self, name, slabs, n_slabs, rhs, out, vector=None):
        nc, ps = self.nc, self.ps
        product, emptied = (self.counter(n) for n in ("product", "emptied"))
        landed = [self.counter(f"slab_in{r}") for r in range(RING)]
        assert n_slabs % RING == 0
        with ExitStack() as ctx:
            ring = self.sb(ctx, f"{name}_ring", [P, RING, KC, P])
            with nc.Block() as block:
                @block.sync
                def _(sp):
                    def fetch(s, r):
                        sp.dma_start(ring[:, r, :, :], slabs[bass.ds(s, 1)].rearrange("a p k m -> p (a k) m")).then_inc(landed[r].sem, 16)
                    for r in range(RING):
                        fetch(r, r)
                    with sp.Fori(0, n_slabs // RING - 1) as g:
                        for r in range(RING):
                            sp.wait_ge(product.sem, product.at(g * RING + r + 1))
                            fetch(g * RING + RING + r, r)

                @block.tensor
                def _(pe):
                    with pe.Fori(0, n_slabs // RING) as g:
                        for r in range(RING):
                            pe.wait_ge(landed[r].sem, landed[r].at(g * 16 + 16))
                            bank = 3 * (r % 2)
                            pe.wait_ge(emptied.sem, emptied.at(g * RING + r - 1))
                            self.slab_product(pe, ring, r, rhs, bank).then_inc(product.sem, 1)

                @block.scalar
                def _(act):
                    with act.Fori(0, n_slabs // RING) as g:
                        for r in range(RING):
                            act.wait_ge(product.sem, product.at(g * RING + r + 1))
                            bank = 3 * (r % 2)
                            for n, (at, w) in enumerate(TILES):
                                last = nc.scalar.copy(out[:, bass.ds(g * RING + r, 1), at:at + w],
                                                      ps[:, bank + n, 0:w].unsqueeze(1))
                            last.then_inc(emptied.sem, 1)
                    act.wait_ge(emptied.sem, emptied.at(n_slabs))

                if vector is not None:
                    @block.vector
                    def _(dve):
                        vector(dve, emptied)
            for one in landed:
                one.passed(16 * n_slabs // RING)
            product.passed(n_slabs), emptied.passed(n_slabs)

    def slab_product(self, pe, ring, r, rhs, bank):
        for n, (at, w) in enumerate(TILES):
            for k in range(KC):
                last = self.nc.tensor.matmul(self.ps[:, bank + n, 0:w], ring[:, r, k, :], rhs(k)[:, at:at + w],
                                             start=(k == 0), stop=(k == KC - 1))
        return last

    def mlp(self, layer, h, y):
        nc, ps = self.nc, self.ps
        product, relu_done = (self.counter(n) for n in ("product", "relu_done"))
        landed = [self.counter(f"slab_in{r}") for r in range(RING)]
        hidden, y_added, y_zero = (self.counter(n) for n in ("hidden", "y_added", "y_zero"))
        slabs = self.io["w_mlp"]
        first = layer * SLABS
        with ExitStack() as ctx:
            ring = self.sb(ctx, f"mlp{layer}_ring", [P, RING, KC, P])
            u = self.sb(ctx, f"mlp{layer}_u", [P, KC, TP])
            with nc.Block() as block:
                @block.sync
                def _(sp):
                    def fetch(s, r):
                        sp.dma_start(ring[:, r, :, :], slabs[bass.ds(first + s, 1)].rearrange("a p k m -> p (a k) m")).then_inc(landed[r].sem, 16)
                    for r in range(RING):
                        fetch(r, r)
                    with sp.Fori(0, SLABS // RING - 1) as g:
                        for r in range(RING):
                            sp.wait_ge(product.sem, product.at(g * RING + r + 1))
                            fetch(g * RING + RING + r, r)

                @block.tensor
                def _(pe):
                    with pe.Fori(0, N_FB) as fb:
                        with pe.Fori(0, KC // RING) as j:
                            for r in range(RING):
                                pe.wait_ge(landed[r].sem, landed[r].at(fb * (32 * KC // RING) + j * 16 + 16))
                                pe.wait_ge(relu_done.sem, relu_done.at(fb * KC + j * RING + r - 1))
                                pe.wait_ge(y_added.sem, y_added.at(fb * KC + min(r, 1) - 1))
                                self.slab_product(pe, ring, r, lambda k: h[:, k, :], 3 * (r % 2)).then_inc(product.sem, 1)
                        with pe.Fori(0, KC // RING) as j:
                            for r in range(RING):
                                pe.wait_ge(landed[r].sem, landed[r].at(fb * (32 * KC // RING) + j * 16 + 16 * (KC // RING + 1)))
                                pe.wait_ge(hidden.sem, hidden.at(fb * KC + KC))
                                pe.wait_ge(y_added.sem, y_added.at(fb * KC + j * RING + r - 1))
                                self.slab_product(pe, ring, r, lambda k: u[:, k, :], 3 * (r % 2)).then_inc(product.sem, 1)

                @block.scalar
                def _(act):
                    with act.Fori(0, N_FB) as fb:
                        with act.Fori(0, KC // RING) as j:
                            for r in range(RING):
                                act.wait_ge(product.sem, product.at(fb * (2 * KC) + j * RING + r + 1))
                                for n, (at, w) in enumerate(TILES):
                                    last = nc.scalar.activation(u[:, bass.ds(j * RING + r, 1), at:at + w],
                                                                ps[:, 3 * (r % 2) + n, 0:w].unsqueeze(1), ACT.Relu)
                                last.then_inc(relu_done.sem, 1)

                @block.vector
                def _(dve):
                    nc.vector.memset(y[:, :, :], 0.0).then_inc(y_zero.sem, 1)
                    dve.wait_ge(y_zero.sem, y_zero.at(1))
                    with dve.Fori(0, N_FB) as fb:
                        with dve.Fori(0, KC // RING) as j:
                            for r in range(RING):
                                dve.wait_ge(relu_done.sem, relu_done.at(fb * KC + j * RING + r + 1))
                                k = bass.ds(j * RING + r, 1)
                                nc.vector.tensor_tensor(u[:, k, :], u[:, k, :], u[:, k, :], ALU.mult).then_inc(hidden.sem, 1)
                        with dve.Fori(0, KC // RING) as j:
                            for r in range(RING):
                                dve.wait_ge(product.sem, product.at(fb * (2 * KC) + j * RING + r + KC + 1))
                                k = bass.ds(j * RING + r, 1)
                                for n, (at, w) in enumerate(TILES):
                                    last = nc.vector.tensor_tensor(y[:, k, at:at + w], y[:, k, at:at + w],
                                                                   ps[:, 3 * (r % 2) + n, 0:w].unsqueeze(1), ALU.add)
                                last.then_inc(y_added.sem, 1)
                                dve.wait_ge(y_added.sem, y_added.at(fb * KC + j * RING + r + 1))
            for one in landed:
                one.passed(16 * SLABS // RING)
            product.passed(SLABS), y_added.passed(N_FB * KC), y_zero.passed(1)
            relu_done.passed(N_FB * KC), hidden.passed(N_FB * KC)

    def token_shift(self, dve, emptied, z, diff, last, shift):
        nc = self.nc
        chain = Chain(dve, self.counter("dve_own"))

        def chunk(m, zc, rows, mu):
            starts = slice(S0, TP, DS)
            nc.vector.tensor_copy(last[rows, m, 0:1], zc[:, :, NP - 1:NP])
            chain.link(nc.vector.tensor_copy(last[rows, m, 1:1 + DB], zc[:, :, S0 + DS - 1:TP:DS]))
            nc.vector.tensor_scalar(diff[rows, :, 0:1], zc[:, :, 0:1], -1.0, None, ALU.mult)
            chain.link(nc.vector.tensor_tensor(diff[rows, :, 1:TP], zc[:, :, 0:TP - 1], zc[:, :, 1:TP], ALU.subtract))
            chain.link(nc.vector.tensor_tensor(diff[rows, :, starts], shift[rows, m, :], zc[:, :, starts], ALU.subtract))
            chain.link(nc.vector.scalar_tensor_tensor(out=zc, in0=diff[rows], scalar=mu, in1=zc, op0=ALU.mult, op1=ALU.add))

        chain.link(nc.vector.memset(last[:, :, :], 0.0))
        dve.wait_ge(emptied.sem, emptied.at(Z_PE + 1))
        tail = slice(32, 64)
        chunk(slice(14, 15), z[tail, Z_PE:Z_PE + 1, :], tail, self.vec[tail, VECS["mu"][0] + 14:VECS["mu"][0] + 15])
        with dve.Fori(0, NZ - Z_R) as m:
            chain.iteration(m, 4)
            dve.wait_ge(emptied.sem, emptied.at(m + Z_R + 1))
            chunk(bass.ds(m, 1), z[:, bass.ds(m + Z_R, 1), :], slice(0, P), self.vec[:, bass.ds(m + VECS["mu"][0], 1)])
        chain.loop_over(NZ - Z_R)
        chain.close()

    def rwkv(self, z, last):
        nc, ps, io = self.nc, self.ps, self.io
        names = ("rw_loaded", "block_done", "lora_in", "lora_out", "lora_act", "kk_sq", "kk_sum", "kk_root", "cumulated",
                 "exps", "v_in", "scaled_in", "bonus_in", "bonus_sum", "turned", "turned_out", "gram", "gram_out",
                 "level_b", "prod_p", "p_out", "prod_x", "x_out", "prod_mv", "mv_out", "prod_wg", "wg_out",
                 "prod_r", "prod_f", "f_out", "tt_out", "rhat", "y_in", "step", "state", "gn_in", "gn_sum", "gn_c", "gn_sq",
                 "gn_root", "rw_out", "s_masked", "s_prod", "s_tt", "s_fout", "s_step", "s_state")
        g = {n: self.counter(n) for n in names}
        per_block = {"gram": 3, "gram_out": 3, "level_b": 4, "prod_p": 8, "p_out": 8, "prod_x": 8, "x_out": 8, "step": 4, "state": 4}

        def waits(engine):
            def wait(name, i, n=None):
                c = per_block.get(name, 1)
                engine.wait_ge(g[name].sem, g[name].at(i * c + (c if n is None else n)))
            return wait

        B_FULL = NP // P
        N_BLOCKS = B_FULL + 1
        with ExitStack() as ctx:
            def sb(name, shape):
                return self.sb(ctx, "rw_" + name, shape)
            w2a2 = sb("w2a2", [P, D_B])
            g2 = sb("g2", [P, 2, D_B])
            tw, tg, tg2 = sb("tw", [P, P]), sb("tg", [P, P]), sb("tg2", [P, P])
            sw, a, gate = sb("sw", [P, PAIRS, P]), sb("a", [P, PAIRS, P]), sb("gate", [P, PAIRS, P])
            vs, kk, ke = sb("v", [P, PAIRS, P]), sb("kk", [P, PAIRS, P]), sb("ke", [P, PAIRS, P])
            t1, t2 = sb("t1", [P, PAIRS, P]), sb("t2", [P, PAIRS, P])
            cum, cump = sb("cum", [P, PAIRS, P]), sb("cump", [P, PAIRS, P])
            KR, kp, bp = sb("KR", [P, PAIRS, 2, P]), sb("kp", [P, PAIRS, P]), sb("bp", [P, PAIRS, P])
            vt, kt, bt = sb("vt", [P, H, HD]), sb("kt", [P, H, HD]), sb("bt", [P, H, HD])
            rhs, wg = sb("rhs", [P, H, P]), sb("wg", [P, H, P])
            MK, MB, A = sb("MK", [P, H, 2, P]), sb("MB", [P, H, 2, P]), sb("A", [P, H, P])
            X, XT, BT, PM = sb("X", [P, H, P]), sb("XT", [P, H, P]), sb("BT", [P, H, P]), A
            TT, F = BT[:, :, :].rearrange("p h (a k) -> p (h a) k", a=2), X[:, :, :].rearrange("p h (a k) -> p (h a) k", a=2)
            S, tmp = sb("S", [P, PAIRS, HD]), sb("tmp", [P, PAIRS, HD])
            y, bonus = sb("y", [P, PAIRS, P]), sb("bonus", [P, PAIRS, P])
            S_s = sb("S_s", [P, PAIRS, DB, HD])
            bm, vm = ([MK[:, 4 * n + 2 * q:4 * n + 2 * q + 2, :, :].rearrange("p a b c -> p (a b c)") for q in range(2)] for n in range(2))
            wm = [MB[:, 2 * q:2 * q + 2, :, :].rearrange("p a b c -> p (a b c)") for q in range(2)]
            TTs = XT[:, 0:4, :].rearrange("p a (b k) -> p (a b) k", b=2)
            Fs, tmps = (A[:, 4 * n:4 * n + 4, :].rearrange("p a (b k) -> p (a b) k", b=2) for n in range(2))

            def rows(h):
                return slice(HD * (h % 2), HD * (h % 2) + HD)

            def vb(name, W):
                return self.v(name, n=PAIRS).unsqueeze(2).to_broadcast([P, PAIRS, W])

            def zb(c, i, W):
                return z[:, c:c + PAIRS, bass.ds(i * P, W)]

            def nar(t, W):
                return t[:, :, 0:W]

            def pb(bank, n, W):
                return ps[:, bank, 0:n * W].rearrange("p (a w) -> p a w", a=n)

            with nc.Block() as block:
                @block.sync
                def _(sp):
                    sp.dma_start(w2a2[:, :], io["w2a2"]).then_inc(g["rw_loaded"].sem, 16)
                    sp.dma_start(g2[:, :, :], io["g2"]).then_inc(g["rw_loaded"].sem, 16)
                    sp.dma_start(S_s[:, :, :, :], io["state"]).then_inc(g["rw_loaded"].sem, 16)
                    sp.dma_start(io["shift"], last[:, :, :]).then_inc(g["rw_out"].sem, 16)
                    sp.wait_ge(g["block_done"].sem, g["block_done"].at(N_BLOCKS))
                    sp.dma_start(io["wkv_p"], S[:, :, :]).then_inc(g["rw_out"].sem, 16)
                    sp.dma_start(io["wkv_s"], S_s[:, :, :, :]).then_inc(g["rw_out"].sem, 16)
                    sp.wait_ge(g["rw_out"].sem, g["rw_out"].at(48))

                @block.scalar
                def _(act):
                    wait = waits(act)

                    def turn(i, W):
                        act.wait_ge(g["block_done"].sem, g["block_done"].at(i))
                        cols = bass.ds(i * P, W)
                        nc.scalar.activation(tw[0:64, 0:W], z[0:64, Z_WA, cols], ACT.Tanh)
                        nc.scalar.activation(tg[:, 0:W], z[:, Z_G, cols], ACT.Sigmoid)
                        nc.scalar.activation(tg2[32:64, 0:W], z[32:64, Z_PE, cols], ACT.Sigmoid)
                        nc.scalar.copy(tw[64:128, 0:W], z[64:128, Z_WA, cols]).then_inc(g["lora_in"].sem, 1)
                        nc.scalar.copy(nar(vs, W), zb(Z_V, i, W)).then_inc(g["v_in"].sem, 1)
                        wait("lora_out", i)
                        for p in range(PAIRS):
                            nc.scalar.activation(nar(sw, W)[:, p, :], pb(0, PAIRS, W)[:, p, :], ACT.Sigmoid, bias=self.v("w0", p))
                            nc.scalar.activation(nar(a, W)[:, p, :], pb(1, PAIRS, W)[:, p, :], ACT.Sigmoid, bias=self.v("a0", p))
                        nc.scalar.copy(nar(gate, W), pb(2, PAIRS, W)).then_inc(g["lora_act"].sem, 1)
                        wait("kk_sum", i)
                        nc.scalar.activation(nar(t2, W), pb(3, PAIRS, W), ACT.Sqrt).then_inc(g["kk_root"].sem, 1)
                        wait("cumulated", i)
                        nc.scalar.activation(nar(cump, W), nar(cump, W), ACT.Exp)
                        nc.scalar.activation(nar(sw, W), nar(cum, W), ACT.Exp, scale=-1.0)
                        nc.scalar.activation(nar(cum, W), nar(cum, W), ACT.Exp).then_inc(g["exps"].sem, 1)
                        wait("turned", i)
                        for n, to in enumerate((vt, kt, bt)):
                            nc.scalar.copy(to[0:W, :, :], ps[0:W, 4 + n, :].rearrange("p (h c) -> p h c", h=H))
                        nc.scalar.copy(rhs[0:W, :, HD:P], ps[0:W, 7, :].rearrange("p (h c) -> p h c", h=H)).then_inc(g["turned_out"].sem, 1)
                        for level in range(1, 5):
                            for half in range(2):
                                wait("prod_p", i, 2 * (level - 1) + half + 1)
                                nc.scalar.copy(PM[0:W, 4 * half:4 * half + 4, 0:W], pb(3 * half, 4, W)[0:W]).then_inc(g["p_out"].sem, 1)
                        wait("prod_mv", i)
                        nc.scalar.copy(rhs[0:W, :, 0:HD], ps[0:W, 6, :].rearrange("p (h c) -> p h c", h=H)).then_inc(g["mv_out"].sem, 1)
                        wait("prod_wg", i)
                        for half in range(2):
                            last_out = nc.scalar.mul(wg[0:W, 4 * half:4 * half + 4, :], pb(7 * half, 4, P)[0:W], -1.0)
                        last_out.then_inc(g["wg_out"].sem, 1)
                        wait("prod_r", i)
                        nc.scalar.copy(nar(y, W), pb(3, PAIRS, W)).then_inc(g["y_in"].sem, 1)
                        wait("tt_out", i)
                        for j in range(4 if W == P else 1):
                            last_out = nc.scalar.copy(F[:, 4 * j:4 * j + 4, :], pb(4 + j, 8, HD)[:, 4:8, :])
                        last_out.then_inc(g["f_out"].sem, 1)
                        if W < P:
                            for p in range(PAIRS):
                                act.wait_ge(g["s_prod"].sem, g["s_prod"].at(p + 1))
                                nc.scalar.copy(Fs[:, :, :], pb(5, DB, HD)).then_inc(g["s_fout"].sem, 1)
                        wait("gn_sq", i)
                        nc.scalar.activation(nar(t2, W), pb(5, PAIRS, W), ACT.Sqrt, bias=self.c("eps", lo=1), scale=1.0 / HD).then_inc(g["gn_root"].sem, 1)

                    with act.Fori(0, B_FULL) as i:
                        turn(i, P)
                    turn(B_FULL, HD)

                @block.vector
                def _(dve):
                    wait = waits(dve)
                    chain = Chain(dve, self.counter("dve_own"))
                    link = chain.link
                    tt, stt, ts = nc.vector.tensor_tensor, nc.vector.scalar_tensor_tensor, nc.vector.tensor_scalar

                    def turn(i, W):
                        full = W == P
                        k_in, r_in = zb(Z_K, i, W), zb(Z_R, i, W)
                        resets = self.c("resets", hi=P) if full else self.c("resets_s")
                        link(tt(nar(t1, W), k_in, vb("k_k", W), ALU.mult))
                        tt(nar(t2, W), nar(t1, W), nar(t1, W), ALU.mult).then_inc(g["kk_sq"].sem, 1)
                        wait("lora_act", i)
                        link(ts(nar(sw, W), nar(sw, W), -float(np.exp(-0.5)), None, ALU.mult))
                        if not full:
                            link(nc.vector.memset(sw[:, :, NP % P:CH], 0.0))
                        for p in range(PAIRS):
                            last_scan = nc.vector.tensor_tensor_scan(cum[:, p, 0:W], resets, sw[:, p, 0:W], 0.0, ALU.mult, ALU.add)
                        link(last_scan)
                        tt(nar(cump, W), nar(cum, W), nar(sw, W), ALU.subtract).then_inc(g["cumulated"].sem, 1)
                        link(stt(out=nar(ke, W), in0=nar(a, W), scalar=-1.0, in1=vb("k_a", W), op0=ALU.add, op1=ALU.mult))
                        link(stt(out=nar(ke, W), in0=nar(ke, W), scalar=1.0, in1=k_in, op0=ALU.add, op1=ALU.mult))
                        wait("kk_root", i)
                        link(ts(nar(t2, W), nar(t2, W), 1e-12, None, ALU.max))
                        link(nc.vector.reciprocal(nar(t2, W), nar(t2, W)))
                        link(tt(nar(kk, W), nar(t1, W), nar(t2, W), ALU.mult))
                        link(tt(nar(a, W), nar(kk, W), nar(a, W), ALU.mult))
                        if not full:
                            nc.vector.memset(a[:, :, NP % P:CH], 0.0)
                            link(nc.vector.memset(ke[:, :, NP % P:CH], 0.0))
                        wait("exps", i)
                        tt(KR[:, :, 0, 0:W], nar(kk, W), nar(cump, W), ALU.mult)
                        tt(KR[:, :, 1, 0:W], r_in, nar(cum, W), ALU.mult)
                        tt(nar(kp, W), nar(ke, W), nar(sw, W), ALU.mult)
                        tt(nar(bp, W), nar(a, W), nar(sw, W), ALU.mult).then_inc(g["scaled_in"].sem, 1)
                        link(tt(nar(t1, W), r_in, vb("r_k", W), ALU.mult))
                        tt(nar(t1, W), nar(t1, W), nar(ke, W), ALU.mult).then_inc(g["bonus_in"].sem, 1)
                        wait("bonus_sum", i)
                        wait("v_in", i)
                        tt(nar(bonus, W), pb(3, PAIRS, W), nar(vs, W), ALU.mult)
                        grams, lower = ("grams", "lower") if full else ("grams_s", "lower_s")
                        mask = self.c(grams, slice(0, W)).rearrange("p (b w) -> p b w", b=2)[:, :, 0:W]
                        for n, (to, bank) in enumerate(((MK, 4), (MB, 0))):
                            wait("gram", i, n + 1)
                            for q in range(4):
                                for e in range(2):
                                    mm = tt(to[0:W, 4 * (q // 2) + 2 * e + q % 2, :, 0:W], ps[0:W, bank + q, 2 * W * e:2 * W * (e + 1)].rearrange("p (b w) -> p b w", b=2), mask, ALU.mult)
                            mm.then_inc(g["gram_out"].sem, 1)
                        wait("gram", i, 3)
                        low = self.c(lower, slice(0, W), hi=W).unsqueeze(1).to_broadcast([W, 4, W])
                        for q in range(2):
                            mm = tt(A[0:W, q:H:2, 0:W], pb(4 + q, 4, W)[0:W], low, ALU.mult)
                        mm.then_inc(g["gram_out"].sem, 1)
                        dve.wait_ge(g["gram_out"].sem, g["gram_out"].at(i * 3 + 3))

                        def lv(name, level):
                            return self.c(name, slice(0, W), lo=level * P, hi=level * P + W).unsqueeze(1).to_broadcast([W, H, W])
                        ident = self.c("ident", slice(0, W), hi=W).unsqueeze(1).to_broadcast([W, H, W])
                        AT = MB[0:W, :, 0, 0:W]
                        stt(out=X[0:W, :, 0:W], in0=A[0:W, :, 0:W], scalar=-1.0, in1=lv("level", 0), op0=ALU.mult, op1=ALU.mult)
                        link(stt(out=XT[0:W, :, 0:W], in0=AT, scalar=-1.0, in1=lv("levelT", 0), op0=ALU.mult, op1=ALU.mult))
                        tt(X[0:W, :, 0:W], X[0:W, :, 0:W], ident, ALU.add)
                        link(tt(XT[0:W, :, 0:W], XT[0:W, :, 0:W], ident, ALU.add))
                        for level in range(1, 5):
                            if level > 1:
                                wait("prod_p", i, 2 * (level - 1))
                            tt(BT[0:W, :, 0:W], AT, lv("levelT", level), ALU.mult).then_inc(g["level_b"].sem, 1)
                            for half in range(2):
                                wait("prod_x", i, 2 * (level - 1) + half + 1)
                                hs = slice(4 * half, 4 * half + 4)
                                if level < 4:
                                    tt(X[0:W, hs, 0:W], X[0:W, hs, 0:W], pb(3 * half + 1, 4, W)[0:W], ALU.subtract)
                                tt(XT[0:W, hs, 0:W], XT[0:W, hs, 0:W], pb(3 * half + 2, 4, W)[0:W], ALU.subtract).then_inc(g["x_out"].sem, 1)
                            dve.wait_ge(g["x_out"].sem, g["x_out"].at(i * 8 + 2 * level))
                        wait("prod_r", i)
                        tt(KR[:, :, 1, 0:W], KR[:, :, 1, 0:W], pb(2, PAIRS, W), ALU.add).then_inc(g["rhat"].sem, 1)
                        wait("prod_f", i)
                        chunks = 4 if full else 1
                        eye = self.c("pair_ident").unsqueeze(1)
                        for j in range(chunks):
                            mm = tt(TT[:, 4 * j:4 * j + 4, :], pb(4 + j, 8, HD)[:, 0:4, :], eye.to_broadcast([P, 4, HD]), ALU.add)
                        mm.then_inc(g["tt_out"].sem, 1)
                        wait("f_out", i)
                        wait("y_in", i)
                        for j in range(chunks):
                            b0 = 2 * (j % 2)
                            wait("step", i, j + 1)
                            link(tt(tmp[:, :, :], pb(b0, PAIRS, HD), F[:, 4 * j:4 * j + 4, :], ALU.add))
                            end = cum[:, :, CH * j + CH - 1:CH * j + CH].to_broadcast([P, PAIRS, HD])
                            tt(S[:, :, :], tmp[:, :, :], end, ALU.mult).then_inc(g["state"].sem, 1)
                            cols = slice(CH * j, CH * j + CH)
                            yadd = tt(y[:, :, cols], y[:, :, cols], pb(b0 + 1, PAIRS, CH), ALU.add)
                        if full:
                            yadd.then_inc(g["gn_in"].sem, 1)
                        else:
                            link(yadd)
                            seq = self.c("seq_of", slice(CH, HD)).unsqueeze(2).to_broadcast([CH, DB, HD])
                            rs = slice(CH, HD)
                            for p in range(PAIRS):
                                if p:
                                    dve.wait_ge(g["s_prod"].sem, g["s_prod"].at(p))
                                for e in range(2):
                                    for to, of in ((bm, bt[rs, 2 * p + e, :]), (vm, vt[rs, 2 * p + e, :]), (wm, wg[rs, 2 * p + e, 0:HD])):
                                        mm = tt(to[e][rs, :].rearrange("p (b k) -> p b k", b=DB), of.unsqueeze(1).to_broadcast([CH, DB, HD]), seq, ALU.mult)
                                mm.then_inc(g["s_masked"].sem, 1)
                                dve.wait_ge(g["s_prod"].sem, g["s_prod"].at(p + 1))
                                tt(TTs, pb(4, DB, HD), eye.to_broadcast([P, DB, HD]), ALU.add).then_inc(g["s_tt"].sem, 1)
                                dve.wait_ge(g["s_fout"].sem, g["s_fout"].at(p + 1))
                                dve.wait_ge(g["s_step"].sem, g["s_step"].at(p + 1))
                                link(tt(tmps, pb(6, DB, HD), Fs, ALU.add))
                                end = cum[:, p, CH + DS - 1:HD:DS].unsqueeze(2).to_broadcast([P, DB, HD])
                                tt(S_s[:, p, :, :], tmps, end, ALU.mult)
                                yadd = tt(y[:, p, rs], y[:, p, rs], ps[:, 7, NS * p:NS * p + NS], ALU.add)
                            yadd.then_inc(g["gn_in"].sem, 1)
                        wait("gn_sum", i)
                        link(stt(out=nar(t1, W), in0=pb(4, PAIRS, W), scalar=-1.0 / HD, in1=nar(y, W), op0=ALU.mult, op1=ALU.add))
                        tt(nar(t2, W), nar(t1, W), nar(t1, W), ALU.mult).then_inc(g["gn_c"].sem, 1)
                        wait("gn_root", i)
                        link(nc.vector.reciprocal(nar(t2, W), nar(t2, W)))
                        link(tt(nar(t1, W), nar(t1, W), nar(t2, W), ALU.mult))
                        link(tt(nar(t1, W), nar(t1, W), vb("ln_w", W), ALU.mult))
                        link(tt(nar(t1, W), nar(t1, W), vb("ln_b", W), ALU.add))
                        link(tt(nar(t1, W), nar(t1, W), nar(bonus, W), ALU.add))
                        tt(zb(Z_R, i, W), nar(t1, W), nar(gate, W), ALU.mult).then_inc(g["block_done"].sem, 1)
                        wait("block_done", i)

                    link(nc.vector.memset(S[:, :, :], 0.0))
                    with dve.Fori(0, B_FULL) as i:
                        chain.iteration(i, RW_LINKS)
                        turn(i, P)
                    chain.loop_over(B_FULL)
                    turn(B_FULL, HD)
                    chain.close()

                @block.tensor
                def _(pe):
                    wait = waits(pe)
                    mm = nc.tensor.matmul

                    def turn(i, W):
                        full = W == P
                        heads = [(h, h // 2, rows(h)) for h in range(H)]
                        w = slice(0, W)
                        wait("lora_in", i)
                        for p in range(PAIRS):
                            m = slice(p * P, p * P + P)
                            mm(pb(0, PAIRS, W)[:, p, :], w2a2[0:64, m], tw[0:64, w], start=True, stop=True)
                            mm(pb(1, PAIRS, W)[:, p, :], w2a2[64:128, m], tw[64:128, w], start=True, stop=True)
                            mm(pb(2, PAIRS, W)[:, p, :], g2[:, 0, m], tg[:, w], start=True, stop=False)
                            end = mm(pb(2, PAIRS, W)[:, p, :], g2[32:64, 1, m], tg2[32:64, w], start=False, stop=True)
                        end.then_inc(g["lora_out"].sem, 1)
                        wait("kk_sq", i)
                        mm(pb(3, PAIRS, W), self.c("head_ones"), nar(t2, W), start=True, stop=True).then_inc(g["kk_sum"].sem, 1)
                        wait("v_in", i)
                        wait("scaled_in", i)
                        for n, of in enumerate((nar(vs, W), nar(kp, W), nar(bp, W), KR[:, :, 0, w])):
                            for p in range(PAIRS):
                                end = nc.tensor.transpose(ps[w, 4 + n, p * P:p * P + P], of[:, p, :], self.c("ident"))
                        end.then_inc(g["turned"].sem, 1)
                        wait("bonus_in", i)
                        mm(pb(3, PAIRS, W), self.c("head_ones"), nar(t1, W), start=True, stop=True).then_inc(g["bonus_sum"].sem, 1)
                        wait("turned_out", i)
                        for n, (of, bank) in enumerate(((kp, 4), (bp, 0))):
                            if n:
                                wait("gram_out", i, 1)
                            for h, p, rr in heads:
                                at = 2 * W * (p % 2)
                                end = mm(ps[w, bank + 2 * (h // 4) + h % 2, at:at + 2 * W].rearrange("q (a b) -> q a b", a=2), of[rr, p, w], KR[rr, p, :, w], start=True, stop=True)
                            end.then_inc(g["gram"].sem, 1)
                        for h, p, rr in heads:
                            end = mm(pb(4 + h % 2, 4, W)[w, p, :], KR[rr, p, 0, w], bp[rr, p, w], start=True, stop=True)
                        end.then_inc(g["gram"].sem, 1)
                        for h, p, rr in heads:
                            end = mm(ps[w, 6, h * HD:h * HD + HD], MK[w, h, 0, w], vt[w, h, :], start=True, stop=True)
                        end.then_inc(g["prod_mv"].sem, 1)
                        for level in range(1, 5):
                            wait("level_b", i, level)
                            if level > 1:
                                wait("x_out", i, 2 * (level - 1))
                            for half in range(2):
                                for q in range(4):
                                    h = 4 * half + q
                                    end = mm(pb(3 * half, 4, W)[w, q, :], BT[w, h, w], X[w, h, w], start=True, stop=True)
                                end.then_inc(g["prod_p"].sem, 1)
                            for half in range(2):
                                wait("p_out", i, 2 * (level - 1) + half + 1)
                                for q in range(4):
                                    h = 4 * half + q
                                    if level < 4:
                                        mm(pb(3 * half + 1, 4, W)[w, q, :], XT[w, h, w], PM[w, h, w], start=True, stop=True)
                                    end = mm(pb(3 * half + 2, 4, W)[w, q, :], PM[w, h, w], XT[w, h, w], start=True, stop=True)
                                end.then_inc(g["prod_x"].sem, 1)
                        wait("x_out", i)
                        wait("mv_out", i)
                        for h, p, rr in heads:
                            end = mm(ps[w, 7 * (h // 4), P * (h % 4):P * (h % 4) + P], XT[w, h, w], rhs[w, h, :], start=True, stop=True)
                        end.then_inc(g["prod_wg"].sem, 1)
                        wait("wg_out", i)
                        for h, p, rr in heads:
                            mm(pb(2, PAIRS, W)[rr, p, :], wg[w, h, HD:P], MB[w, h, 1, w], start=True, stop=True)
                        for h, p, rr in heads:
                            mm(pb(3, PAIRS, W)[rr, p, :], vt[w, h, :], MK[w, h, 1, w], start=True, stop=False)
                            end = mm(pb(3, PAIRS, W)[rr, p, :], wg[w, h, 0:HD], MB[w, h, 1, w], start=False, stop=True)
                        end.then_inc(g["prod_r"].sem, 1)
                        chunks = 4 if full else 1
                        for j in range(chunks):
                            c = slice(CH * j, CH * j + CH)
                            for h, p, rr in heads:
                                mm(pb(4 + j, 8, HD)[rr, p, :], wg[c, h, HD:P], bt[c, h, :], start=True, stop=True)
                                mm(pb(4 + j, 8, HD)[rr, PAIRS + p, :], kt[c, h, :], vt[c, h, :], start=True, stop=False)
                                end = mm(pb(4 + j, 8, HD)[rr, PAIRS + p, :], bt[c, h, :], wg[c, h, 0:HD], start=False, stop=True)
                        end.then_inc(g["prod_f"].sem, 1)
                        for j in range(chunks):
                            b0 = 2 * (j % 2)
                            pe.wait_ge(g["rw_loaded"].sem, g["rw_loaded"].at(48))
                            if j:
                                wait("state", i, j)
                            else:
                                wait("tt_out", i)
                                wait("rhat", i)
                                wait("y_in", i)
                            for h, p, rr in heads:
                                mm(pb(b0, PAIRS, HD)[rr, p, :], TT[rr, 4 * j + p, :], S[rr, p, :], start=True, stop=True)
                            for h, p, rr in heads:
                                end = mm(pb(b0 + 1, PAIRS, CH)[rr, p, :], S[rr, p, :], KR[rr, p, 1, CH * j:CH * j + CH], start=True, stop=True)
                            end.then_inc(g["step"].sem, 1)
                        if not full:
                            c = slice(CH, HD)
                            pe.wait_ge(g["rw_loaded"].sem, g["rw_loaded"].at(48))
                            for p in range(PAIRS):
                                pe.wait_ge(g["s_masked"].sem, g["s_masked"].at(p + 1))
                                if p:
                                    pe.wait_ge(g["s_fout"].sem, g["s_fout"].at(p))
                                for e in range(2):
                                    h, rr = 2 * p + e, rows(e)
                                    mm(ps[rr, 4, :], wg[c, h, HD:P], bm[e][c, :], start=True, stop=True)
                                    mm(ps[rr, 5, :], kt[c, h, :], vm[e][c, :], start=True, stop=False)
                                    end = mm(ps[rr, 5, :], bt[c, h, :], wm[e][c, :], start=False, stop=True)
                                end.then_inc(g["s_prod"].sem, 1)
                                pe.wait_ge(g["s_tt"].sem, g["s_tt"].at(p + 1))
                                if p == 0:
                                    wait("f_out", i)
                                for e in range(2):
                                    rr = rows(e)
                                    for b in range(DB):
                                        mm(ps[rr, 6, b * HD:b * HD + HD], TTs[rr, b, :], S_s[rr, p, b, :], start=True, stop=True)
                                        at = NS * p + DS * b
                                        end = mm(ps[rr, 7, at:at + DS], S_s[rr, p, b, :], KR[rr, p, 1, CH + DS * b:CH + DS * b + DS], start=True, stop=True)
                                end.then_inc(g["s_step"].sem, 1)
                        wait("gn_in", i)
                        mm(pb(4, PAIRS, W), self.c("head_ones"), nar(y, W), start=True, stop=True).then_inc(g["gn_sum"].sem, 1)
                        wait("gn_c", i)
                        mm(pb(5, PAIRS, W), self.c("head_ones"), nar(t2, W), start=True, stop=True).then_inc(g["gn_sq"].sem, 1)

                    pe.wait_ge(g["rw_loaded"].sem, g["rw_loaded"].at(48))
                    with pe.Fori(0, B_FULL) as i:
                        turn(i, P)
                    turn(B_FULL, HD)
            for n in names:
                events = per_block.get(n, 1)
                if n in ("step", "state"):
                    g[n].passed(4 * B_FULL + 1)
                elif n in ("rw_loaded", "rw_out"):
                    g[n].passed(48)
                elif n.startswith("s_"):
                    g[n].passed(PAIRS)
                else:
                    g[n].passed(events * N_BLOCKS)

    def prompt_attention(self, z, qsn, qpe, kps):
        nc, ps, io = self.nc, self.ps, self.io
        names = ("rope_in", "kpe_prod", "kpe_done", "pair_w", "proj", "proj_out", "q_rot", "scores", "neg_max", "exp_done", "probs",
                 "flipped", "flip_a", "flip_v", "values", "values_out", "latent_out")
        g = {n: self.counter(n) for n in names}
        NB = -(-NP // P)
        U = 2 * NB
        WQ, WK, WV = 3 * 2 * P, 2 * P, 2 * P
        with ExitStack() as ctx:
            def sb(name, shape):
                return self.sb(ctx, "pa_" + name, shape)
            rope = sb("rope", [P, 2, TP])
            w = sb("w", [P, WQ + WK + WV])
            QT, KT = sb("QT", [P, 2, TP]), sb("KT", [96, 2, TP])
            rot = sb("rot", [P, TP])
            V = sb("V", [P, NB, P])
            E, PT = sb("E", [P, 2, NB * P]), sb("PT", [P, 2, NB, P])
            mx, nm, sums, rs = (sb(n, [P, 2]) for n in ("mx", "nm", "sums", "rs"))
            wq = w[:, 0:WQ].rearrange("p (k m) -> p k m", k=3)
            wk = w[:, WQ:WQ + WK].rearrange("p (k m) -> p k m", k=2)
            wv = w[:, WQ + WK:].rearrange("p (k m) -> p k m", k=2)

            def block_of(u):
                e, i = divmod(u, NB)
                return e, i, min(P, NP - i * P)

            def rr(e):
                return slice(HD * e, HD * e + HD)

            def wide(u):
                return sum(v % NB >= 4 for v in range(u))

            with nc.Block() as block:
                @block.sync
                def _(sp):
                    sp.dma_start(rope[:, :, :], io["rope"]).then_inc(g["rope_in"].sem, 16)
                    sp.dma_start(io["ckv"], z[:, Z_KV:Z_KV + 2, :]).then_inc(g["latent_out"].sem, 16)
                    with sp.Fori(0, PAIRS) as p:
                        sp.wait_ge(g["proj"].sem, g["proj"].at(p * 5))
                        sp.dma_start(w[:, :].unsqueeze(1), io["w_pair"][bass.ds(p, 1)].rearrange("a p m -> p a m")).then_inc(g["pair_w"].sem, 16)
                    sp.wait_ge(g["kpe_done"].sem, g["kpe_done"].at(1))
                    sp.dma_start(io["kpe"], KT[64:96, 0, :]).then_inc(g["latent_out"].sem, 16)
                    sp.wait_ge(g["latent_out"].sem, g["latent_out"].at(32))

                @block.tensor
                def _(pe):
                    mm = nc.tensor.matmul

                    def scores(p, u):
                        e, i, n = block_of(u)
                        if u == 0:
                            pe.wait_ge(g["kpe_done"].sem, g["kpe_done"].at(2))
                        if i == 0:
                            pe.wait_ge(g["q_rot"].sem, g["q_rot"].at(p * 2 + e + 1))
                        q = QT[0:96, e, i * P:i * P + n]
                        bank = 3 * (u % 2)
                        for at in range(0, i * P, 512):
                            c = min(512, i * P - at)
                            mm(ps[0:n, bank + at // 512, 0:c], q, KT[:, e, at:at + c], start=True, stop=True)
                        d = i * P
                        to = ps[0:n, bank + d // 512, d % 512:d % 512 + n]
                        mm(to, q, KT[:, e, d:d + n], start=True, stop=False)
                        mm(to, self.c("ident", hi=n), self.c("causal", hi=n), start=False, stop=True).then_inc(g["scores"].sem, 1)

                    with pe.Fori(0, PAIRS) as p:
                        pe.wait_ge(g["pair_w"].sem, g["pair_w"].at(p * 16 + 16))
                        for e in range(2):
                            for n, (at, c) in enumerate(TILES):
                                for k in range(3):
                                    last = mm(ps[:, 3 * e + n, 0:c], wq[:, k, e * P:e * P + P], z[:, Z_Q + k, at:at + c], start=(k == 0), stop=(k == 2))
                            last.then_inc(g["proj"].sem, 1)
                        for e in range(2):
                            pe.wait_ge(g["proj_out"].sem, g["proj_out"].at(p * 5 + e + 1))
                            for n, (at, c) in enumerate(TILES):
                                for k in range(2):
                                    last = mm(ps[0:64, 3 * e + n, 0:c], wk[:, k, e * HD:e * HD + HD], z[:, Z_KV + k, at:at + c], start=(k == 0), stop=(k == 1))
                            last.then_inc(g["proj"].sem, 1)
                        pe.wait_ge(g["proj_out"].sem, g["proj_out"].at(p * 5 + 3))
                        for i in range(NB):
                            n = min(P, NP - i * P)
                            for k in range(2):
                                last = mm(ps[0:n, i // 4, (i % 4) * P:(i % 4) * P + P], z[:, Z_KV + k, i * P:i * P + n], wv[:, k, :], start=(k == 0), stop=(k == 1))
                        last.then_inc(g["proj"].sem, 1)
                        pe.wait_ge(g["proj_out"].sem, g["proj_out"].at(p * 5 + 5))
                        scores(p, 0)
                        for u in range(U):
                            e, i, n = block_of(u)
                            if u + 1 < U:
                                scores(p, u + 1)
                            probs_at = g["probs"].at(p * U + u + 1)
                            if n < P:
                                probs_at = pe.compute_val(probs_at)
                                pe.wait_ge(g["kpe_done"].sem, g["kpe_done"].at(2))
                            pe.wait_ge(g["probs"].sem, probs_at)
                            for kb in range(i + 1):
                                m = min(P, NP - kb * P)
                                last = nc.tensor.transpose(ps[0:m, 3 * (u % 2) + kb // 4, (kb % 4) * P:(kb % 4) * P + n],
                                                           E[0:n, u % 2, kb * P:kb * P + m], self.c("ident", slice(0, n), hi=n))
                            last.then_inc(g["flipped"].sem, 1)
                            pe.wait_ge(g["flip_a"].sem, g["flip_a"].at(p * U + u + 1))
                            if i >= 4:
                                pe.wait_ge(g["flip_v"].sem, g["flip_v"].at(p * wide(U) + wide(u + 1)))
                            if u >= 2:
                                pe.wait_ge(g["values_out"].sem, g["values_out"].at(p * U + u - 1))
                            for kb in range(i + 1):
                                m = min(P, NP - kb * P)
                                last = mm(ps[rr(e), 6 + u % 2, 0:n], V[0:m, kb, rr(e)], PT[0:m, u % 2, kb, 0:n], start=(kb == 0), stop=(kb == i))
                            last.then_inc(g["values"].sem, 1)
                        pe.wait_ge(g["values_out"].sem, g["values_out"].at(p * U + U))

                @block.scalar
                def _(act):
                    def exp(p, u):
                        e, i, n = block_of(u)
                        act.wait_ge(g["neg_max"].sem, g["neg_max"].at(p * U + u + 1))
                        cols = i * P + n
                        src = ps[0:n, 3 * (u % 2):3 * (u % 2) + 3, :].rearrange("p a b -> p (a b)")[:, 0:cols]
                        nc.scalar.activation(E[0:n, u % 2, 0:cols], src, ACT.Exp, bias=nm[0:n, u % 2:u % 2 + 1], scale=SM_SCALE,
                                             accum_out=sums[0:n, u % 2:u % 2 + 1]).then_inc(g["exp_done"].sem, 1)

                    act.wait_ge(g["kpe_done"].sem, g["kpe_done"].at(1))
                    nc.scalar.copy(KT[64:96, 1, :], KT[64:96, 0, :])
                    nc.scalar.copy(kps[:, :], KT[64:96, 0, S0:TP]).then_inc(g["kpe_done"].sem, 1)
                    with act.Fori(0, PAIRS) as p:
                        for e in range(2):
                            act.wait_ge(g["proj"].sem, g["proj"].at(p * 5 + e + 1))
                            for n, (at, c) in enumerate(TILES):
                                last = nc.scalar.copy(QT[:, e, at:at + c], ps[:, 3 * e + n, 0:c])
                            last.then_inc(g["proj_out"].sem, 1)
                        for e in range(2):
                            act.wait_ge(g["proj"].sem, g["proj"].at(p * 5 + e + 3))
                            for n, (at, c) in enumerate(TILES):
                                last = nc.scalar.copy(KT[0:64, e, at:at + c], ps[0:64, 3 * e + n, 0:c])
                            last.then_inc(g["proj_out"].sem, 1)
                        act.wait_ge(g["proj"].sem, g["proj"].at(p * 5 + 5))
                        for n in range(2):
                            nc.scalar.copy(V[:, 4 * n:4 * n + 4, :], ps[:, n, :].rearrange("p (a b) -> p a b", a=4))
                        nc.scalar.copy(V[0:NP % P, NB - 1, :], ps[0:NP % P, 2, 0:P]).then_inc(g["proj_out"].sem, 1)
                        for e in range(2):
                            act.wait_ge(g["q_rot"].sem, g["q_rot"].at(p * 2 + e + 1))
                            nc.scalar.copy(qsn[rr(e), bass.ds(p, 1), :], QT[0:64, e, S0:TP].unsqueeze(1))
                            nc.scalar.copy(qpe[:, :, bass.ds(p * 2 + e, 1), :],
                                           QT[64:96, e, S0:TP].rearrange("p (b a t) -> p b a t", b=DB, a=1))
                        exp(p, 0)
                        for u in range(U):
                            e, i, n = block_of(u)
                            if u + 1 < U:
                                exp(p, u + 1)
                            act.wait_ge(g["flipped"].sem, g["flipped"].at(p * U + u + 1))
                            for b in range(0, i // 4 + 1, 2):
                                m = min(4, i + 1 - 4 * b)
                                full = min(m, NP // P - 4 * b)
                                if full:
                                    last = nc.scalar.copy(PT[:, u % 2, 4 * b:4 * b + full, 0:n],
                                                          ps[:, 3 * (u % 2) + b, 0:full * P].rearrange("p (a b) -> p a b", a=full)[:, :, 0:n])
                                if full < m:
                                    last = nc.scalar.copy(PT[0:NP % P, u % 2, NB - 1, 0:n], ps[0:NP % P, 3 * (u % 2) + b, 0:n])
                            last.then_inc(g["flip_a"].sem, 1)
                            act.wait_ge(g["values"].sem, g["values"].at(p * U + u + 1))
                            nc.scalar.copy(z[rr(e), bass.ds(p + Z_K, 1), i * P:i * P + n], ps[rr(e), 6 + u % 2, 0:n].unsqueeze(1)).then_inc(g["values_out"].sem, 1)
                    act.wait_ge(g["values_out"].sem, g["values_out"].at(PAIRS * U))

                @block.vector
                def _(dve):
                    chain = Chain(dve, self.counter("dve_own"))
                    link = chain.link
                    tt = nc.vector.tensor_tensor

                    def neg_max(p, u):
                        e, i, n = block_of(u)
                        dve.wait_ge(g["scores"].sem, g["scores"].at(p * U + u + 1))
                        src = ps[0:n, 3 * (u % 2):3 * (u % 2) + 3, :].rearrange("p a b -> p (a b)")[:, 0:i * P + n]
                        c = slice(u % 2, u % 2 + 1)
                        link(nc.vector.tensor_reduce(mx[0:n, c], src, AX.X, ALU.max))
                        nc.vector.tensor_scalar(nm[0:n, c], mx[0:n, c], -SM_SCALE, None, ALU.mult).then_inc(g["neg_max"].sem, 1)

                    def normalise(p, u):
                        e, i, n = block_of(u)
                        c = slice(u % 2, u % 2 + 1)
                        dve.wait_ge(g["exp_done"].sem, g["exp_done"].at(p * U + u + 1))
                        link(nc.vector.reciprocal(rs[0:n, c], sums[0:n, c]))
                        row = E[0:n, u % 2, 0:i * P + n]
                        nc.vector.tensor_scalar(row, row, rs[0:n, c], None, ALU.mult).then_inc(g["probs"].sem, 1)

                    dve.wait_ge(g["rope_in"].sem, g["rope_in"].at(16))
                    tt(rot[64:96, :], z[0:32, Z_PE, :], rope[0:32, 0, :], ALU.mult)
                    link(tt(KT[64:96, 0, :], z[64:96, Z_PE, :], rope[64:96, 1, :], ALU.mult))
                    tt(KT[64:96, 0, :], KT[64:96, 0, :], rot[64:96, :], ALU.add).then_inc(g["kpe_done"].sem, 1)
                    dve.wait_ge(g["kpe_done"].sem, g["kpe_done"].at(1))
                    with dve.Fori(0, PAIRS) as p:
                        chain.iteration(p, 38)
                        for e in range(2):
                            dve.wait_ge(g["proj_out"].sem, g["proj_out"].at(p * 5 + e + 1))
                            tt(rot[64:96, :], QT[96:128, e, :], rope[96:128, 1, :], ALU.mult)
                            link(tt(QT[64:96, e, :], QT[64:96, e, :], rope[64:96, 0, :], ALU.mult))
                            tt(QT[64:96, e, :], QT[64:96, e, :], rot[64:96, :], ALU.add).then_inc(g["q_rot"].sem, 1)
                            dve.wait_ge(g["q_rot"].sem, g["q_rot"].at(p * 2 + e + 1))
                        neg_max(p, 0)
                        normalise(p, 0)
                        for u in range(U):
                            e, i, n = block_of(u)
                            if u + 1 < U:
                                neg_max(p, u + 1)
                            dve.wait_ge(g["flipped"].sem, g["flipped"].at(p * U + u + 1))
                            if i >= 4:
                                if u >= 2:
                                    dve.wait_ge(g["values"].sem, g["values"].at(p * U + u - 1))
                                m = min(4, i - 3)
                                nc.vector.tensor_copy(PT[:, u % 2, 4:4 + m, 0:n], ps[:, 3 * (u % 2) + 1, 0:m * P].rearrange("p (a b) -> p a b", a=m)[:, :, 0:n]).then_inc(g["flip_v"].sem, 1)
                            if u + 1 < U:
                                normalise(p, u + 1)
                    chain.loop_over(PAIRS)
                    chain.close()
            for n, events in (("rope_in", 16), ("kpe_prod", 0), ("kpe_done", 2), ("pair_w", 64), ("proj", 20), ("proj_out", 20), ("q_rot", 8), ("latent_out", 32)):
                g[n].passed(events)
            for n in ("scores", "neg_max", "exp_done", "probs", "flipped", "flip_a", "values", "values_out"):
                g[n].passed(PAIRS * U)
            g["flip_v"].passed(PAIRS * wide(U))

    def sample_attention(self, z, qsn, qpe, kps):
        nc, ps, io = self.nc, self.ps, self.io
        names = ("sa_in", "qlat_prod", "qlat", "new_prod", "new_scores", "q_copied", "turn_c", "turn_a", "turn_v", "s_scores", "s_max",
                 "s_maxT", "s_diag", "s_maxb", "s_shift", "s_exp", "s_sum", "s_sumb", "s_pv", "s_olat", "sa_o", "sa_out")
        g = {n: self.counter(n) for n in names}
        pages_in = [self.counter(f"pages_in{n}") for n in range(2)]
        ROW = KV_LORA + ROPE
        GROUP = 4
        NG = N_PAGES // GROUP
        QR = H * DS
        with ExitStack() as ctx:
            def sb(name, shape, dt=F32):
                return self.sb(ctx, "sa_" + name, shape, dt)
            C = sb("C", [P, 2, N_PAGES, ROW])
            table = sb("table", [1, DB * N_PAGES], mybir.dt.int32)
            wukT, wuv = sb("wukT", [P, PAIRS, KV_LORA]), sb("wuv", [P, 2, H * HD])
            mask = sb("mask", [NS, DB, QR])
            qlat, olat = sb("qlat", [P, 2, DB, QR]), sb("olat", [P, 2, DB, QR])
            ctok, Sn, pn = sb("ctok", [NS, KV_LORA]), sb("Sn", [NS, DB, QR]), sb("pn", [NS, QR])
            cT, kT = sb("cT", [P, 2, GROUP, 2, P]), sb("kT", [ROPE, 2, GROUP, P])
            qb, qpb = sb("qb", [P, 2, 2, QR]), sb("qpb", [ROPE, 2, QR])
            Pb = sb("Pb", [P, N_PAGES, QR])
            mx, mb, sm, rinv = (sb(n, [P, QR]) for n in ("mx", "mb", "sm", "rinv"))
            m1, dg = sb("m1", [QR, 1]), sb("dg", [QR, QR])
            UNITS = 3 * NG

            def by_act(n):
                return n % 2 == 0

            def sg(name, b, c=1, n=None):
                return g[name].at(b * c + (c if n is None else n))

            scored = ps[:, 4:6, :].rearrange("p a (j q) -> p (a j) q", q=QR)

            with nc.Block() as block:
                @block.sync
                def _(sp):
                    sp.dma_start(table[:, :], io["table"]).then_inc(g["sa_in"].sem, 16)
                    sp.dma_start(wukT[:, :, :], io["w_ukT"]).then_inc(g["sa_in"].sem, 16)
                    sp.dma_start(wuv[:, :, :], io["w_uv"]).then_inc(g["sa_in"].sem, 16)
                    sp.dma_start(mask[:, :, :], io["new_mask"]).then_inc(g["sa_in"].sem, 16)
                    sp.wait_ge(g["sa_in"].sem, g["sa_in"].at(64))
                    with sp.Fori(0, DB // 2) as b2:
                        for s in range(2):
                            read_at = sp.compute_val(g["s_pv"].at(b2 * 2 + s - 1))
                            sp.wait_ge(g["sa_in"].sem, g["sa_in"].at(64))
                            sp.wait_ge(g["s_pv"].sem, read_at)
                            with sp.Fori(0, N_PAGES) as j:
                                page = sp.value_load(table[0:1, bass.ds(b2 * (2 * N_PAGES) + s * N_PAGES + j, 1)], min_val=0, max_val=POOL_PAGES - 1)
                                sp.dma_start(C[:, s, bass.ds(j, 1), :], io["pool"][bass.ds(page, 1)].rearrange("a p m -> p a m")).then_inc(pages_in[s].sem, 16)

                @block.tensor
                def _(pe):
                    mm = nc.tensor.matmul
                    pe.wait_ge(g["sa_in"].sem, g["sa_in"].at(64))
                    for h in range(H):
                        p, e = divmod(h, 2)
                        r = slice(HD * e, HD * e + HD)
                        for k in range(2):
                            last = mm(ps[:, e, (2 * p + k) * NS:(2 * p + k + 1) * NS], wukT[r, p, k * P:k * P + P], qsn[r, p, :], start=True, stop=True)
                    for k in range(2):
                        last = nc.tensor.transpose(ps[0:NS, 2, k * P:k * P + P], z[:, Z_KV + k, S0:TP], self.c("ident"))
                    last.then_inc(g["qlat_prod"].sem, 1)
                    pe.wait_ge(g["qlat"].sem, g["qlat"].at(1))
                    for k in range(2):
                        mm(ps[0:NS, 3, 0:DB * QR], z[:, Z_KV + k, S0:TP], qlat[:, k, :, :], start=(k == 0), stop=False)
                    mm(ps[0:NS, 3, 0:DB * QR], kps[:, :], qpe[:, :, :, :], start=False, stop=True).then_inc(g["new_prod"].sem, 1)
                    pe.wait_ge(g["new_scores"].sem, g["new_scores"].at(1))

                    def scores(b, s, grp):
                        n = 3 * grp + 2
                        pe.wait_ge(g["turn_a"].sem, g["turn_a"].at(b * (UNITS // 2) + (n + 2) // 2))
                        pe.wait_ge(g["turn_v"].sem, g["turn_v"].at(b * (UNITS // 2) + (n + 1) // 2))
                        for q in range(GROUP):
                            j = GROUP * grp + q
                            for k in range(2):
                                mm(scored[:, j, :], cT[:, grp % 2, q, k, :], qb[:, s, k, :], start=(k == 0), stop=False)
                            last = mm(scored[:, j, :], kT[:, grp % 2, q, :], qpb[:, s, :], start=False, stop=True)
                        return last

                    def pages_wait(b2, s):
                        return pages_in[s].at(b2 * (16 * N_PAGES) + 16 * N_PAGES)

                    with pe.Fori(0, DB // 2) as b2:
                        for s in range(2):
                            b = b2 * 2 + s
                            pe.wait_ge(pages_in[s].sem, pages_wait(b2, s))
                            pe.wait_ge(g["q_copied"].sem, sg("q_copied", b))
                            for grp in range(NG + 1):
                                if grp < NG:
                                    for v in range(3):
                                        n = 3 * grp + v
                                        if n >= 4:
                                            name = "turn_a" if by_act(n) else "turn_v"
                                            pe.wait_ge(g[name].sem, g[name].at(b * (UNITS // 2) + (n - 4) // 2 + 1))
                                        for q in range(4):
                                            if v < 2:
                                                j, k = GROUP * grp + 2 * v + q // 2, q % 2
                                                last = nc.tensor.transpose(ps[:, n % 4, q * P:q * P + P], C[:, s, j, k * P:k * P + P], self.c("ident"))
                                            else:
                                                j = GROUP * grp + q
                                                last = nc.tensor.transpose(ps[0:ROPE, n % 4, q * P:q * P + P], C[:, s, j, KV_LORA:ROW], self.c("ident"))
                                        last.then_inc(g["turn_c"].sem, 1)
                                if grp:
                                    last = scores(b, s, grp - 1)
                                    last.then_inc(g["s_scores"].sem, 1)
                            pe.wait_ge(g["s_max"].sem, sg("s_max", b))
                            nc.tensor.transpose(ps[0:QR, 6, 0:P], mx[:, :], self.c("ident")).then_inc(g["s_maxT"].sem, 1)
                            pe.wait_ge(g["s_diag"].sem, sg("s_diag", b))
                            mm(ps[:, 6, P:P + QR], self.c("ones", slice(0, QR)), dg[:, :], start=True, stop=True).then_inc(g["s_maxb"].sem, 1)
                            pe.wait_ge(g["s_exp"].sem, sg("s_exp", b))
                            for k in range(2):
                                for j in range(N_PAGES):
                                    mm(ps[:, 7, k * QR:k * QR + QR], C[:, s, j, k * P:k * P + P], Pb[:, j, :], start=(j == 0), stop=False)
                                last = mm(ps[:, 7, k * QR:k * QR + QR], ctok[:, k * P:k * P + P], pn[:, :], start=False, stop=True)
                            last.then_inc(g["s_pv"].sem, 1)
                            pe.wait_ge(g["s_sum"].sem, sg("s_sum", b))
                            mm(ps[:, 6, 2 * P:2 * P + QR], self.c("ones"), sm[:, :], start=True, stop=True).then_inc(g["s_sumb"].sem, 1)
                            pe.wait_ge(g["s_olat"].sem, sg("s_olat", b))
                    for h in range(H):
                        p, e = divmod(h, 2)
                        r = slice(HD * e, HD * e + HD)
                        for k in range(2):
                            last = mm(ps[r, 0, p * NS:p * NS + NS], wuv[:, k, h * HD:h * HD + HD],
                                      olat[:, k, :, h * DS:h * DS + DS], start=(k == 0), stop=(k == 1))
                    last.then_inc(g["sa_o"].sem, 1)

                def leave(eng, copy, b, n, name):
                    grp, v = divmod(n, 3)
                    if grp >= 2:
                        eng.wait_ge(g["s_scores"].sem, g["s_scores"].at(b * NG + grp - 1))
                    eng.wait_ge(g["turn_c"].sem, g["turn_c"].at(b * UNITS + n + 1))
                    if v < 2:
                        last = copy(cT[:, grp % 2, 2 * v:2 * v + 2, :, :], ps[:, n % 4, :].rearrange("p (a k c) -> p a k c", a=2, k=2))
                    else:
                        last = copy(kT[:, grp % 2, :, :], ps[0:ROPE, n % 4, :].rearrange("p (a c) -> p a c", a=4))
                    last.then_inc(g[name].sem, 1)

                @block.scalar
                def _(act):
                    act.wait_ge(g["qlat_prod"].sem, g["qlat_prod"].at(1))
                    for h in range(H):
                        p, e = divmod(h, 2)
                        nc.scalar.copy(qlat[:, :, :, h * DS:h * DS + DS],
                                       ps[:, e, 2 * p * NS:(2 * p + 2) * NS].rearrange("p (k b t) -> p k b t", k=2, b=DB))
                    nc.scalar.copy(ctok[:, :], ps[0:NS, 2, 0:KV_LORA]).then_inc(g["qlat"].sem, 1)
                    act.wait_ge(g["qlat"].sem, g["qlat"].at(1))
                    with act.Fori(0, DB // 2) as b2:
                        for s in range(2):
                            b = b2 * 2 + s
                            nc.scalar.copy(qb[:, s, :, :].unsqueeze(2), qlat[:, :, bass.ds(b, 1), :])
                            nc.scalar.copy(qpb[:, s, :].rearrange("p (a h t) -> p a h t", a=1, h=H), qpe[:, bass.ds(b, 1), :, :]).then_inc(g["q_copied"].sem, 1)
                            for n in range(UNITS):
                                if by_act(n):
                                    leave(act, nc.scalar.copy, b, n, "turn_a")
                            act.wait_ge(g["s_shift"].sem, sg("s_shift", b))
                            nc.scalar.activation(pn[:, :], pn[:, :], ACT.Exp, scale=SM_SCALE)
                            nc.scalar.activation(Pb[:, :, :], Pb[:, :, :], ACT.Exp, scale=SM_SCALE).then_inc(g["s_exp"].sem, 1)
                    act.wait_ge(g["sa_o"].sem, g["sa_o"].at(1))
                    nc.scalar.copy(z[:, Z_K:Z_K + PAIRS, S0:TP], ps[:, 0, 0:PAIRS * NS].rearrange("p (a b) -> p a b", a=PAIRS)).then_inc(g["sa_out"].sem, 1)
                    act.wait_ge(g["sa_out"].sem, g["sa_out"].at(1))

                @block.vector
                def _(dve):
                    chain = Chain(dve, self.counter("dve_own"))
                    link = chain.link
                    tt = nc.vector.tensor_tensor
                    dve.wait_ge(g["new_prod"].sem, g["new_prod"].at(1))
                    dve.wait_ge(g["sa_in"].sem, g["sa_in"].at(64))
                    tt(Sn[:, :, :], ps[0:NS, 3, 0:DB * QR].rearrange("p (b q) -> p b q", b=DB), mask[:, :, :], ALU.add).then_inc(g["new_scores"].sem, 1)
                    dve.wait_ge(g["new_scores"].sem, g["new_scores"].at(1))
                    with dve.Fori(0, DB // 2) as b2:
                        chain.iteration(b2, 10)
                        for s in range(2):
                            b = b2 * 2 + s
                            for n in range(UNITS):
                                if not by_act(n):
                                    leave(dve, nc.vector.tensor_copy, b, n, "turn_v")
                            dve.wait_ge(g["s_scores"].sem, sg("s_scores", b, NG))
                            link(nc.vector.tensor_reduce(mx[:, :], scored.rearrange("p j q -> p q j"), AX.X, ALU.max))
                            tt(mx[0:NS, :].unsqueeze(1), mx[0:NS, :].unsqueeze(1), Sn[:, bass.ds(b, 1), :], ALU.max).then_inc(g["s_max"].sem, 1)
                            dve.wait_ge(g["s_maxT"].sem, sg("s_maxT", b))
                            link(nc.vector.tensor_reduce(m1[:, :], ps[0:QR, 6, 0:P], AX.X, ALU.max))
                            nc.vector.tensor_scalar(dg[:, :], self.c("ident", slice(0, QR), hi=QR), m1[:, 0:1], None, ALU.mult).then_inc(g["s_diag"].sem, 1)
                            dve.wait_ge(g["s_maxb"].sem, sg("s_maxb", b))
                            link(nc.vector.tensor_copy(mb[:, :], ps[:, 6, P:P + QR]))
                            tt(pn[:, :].unsqueeze(1), Sn[:, bass.ds(b, 1), :], mb[0:NS, :].unsqueeze(1), ALU.subtract)
                            tt(Pb[:, :, :], scored, mb[:, :].unsqueeze(1).to_broadcast([P, N_PAGES, QR]), ALU.subtract).then_inc(g["s_shift"].sem, 1)
                            dve.wait_ge(g["s_exp"].sem, sg("s_exp", b))
                            link(nc.vector.tensor_reduce(sm[:, :], Pb[:, :, :].rearrange("p j q -> p q j"), AX.X, ALU.add))
                            tt(sm[0:NS, :], sm[0:NS, :], pn[:, :], ALU.add).then_inc(g["s_sum"].sem, 1)
                            dve.wait_ge(g["s_sumb"].sem, sg("s_sumb", b))
                            link(nc.vector.reciprocal(rinv[:, :], ps[:, 6, 2 * P:2 * P + QR]))
                            dve.wait_ge(g["s_pv"].sem, sg("s_pv", b))
                            (tt(olat[:, :, bass.ds(b, 1), :], ps[:, 7, 0:2 * QR].rearrange("p (k a q) -> p k a q", k=2, a=1),
                                    rinv[:, :].unsqueeze(1).unsqueeze(1).to_broadcast([P, 2, 1, QR]), ALU.mult)
                             .then_inc(g["s_olat"].sem, 1))
                    chain.loop_over(DB // 2)
                    chain.close()
            for n, events in (("sa_in", 64), ("qlat_prod", 1), ("qlat", 1), ("new_prod", 1), ("new_scores", 1), ("turn_c", DB * UNITS),
                              ("turn_a", DB * UNITS // 2), ("turn_v", DB * UNITS // 2), ("s_scores", DB * NG), ("sa_o", 1), ("sa_out", 1)):
                g[n].passed(events)
            for n in ("q_copied", "s_max", "s_maxT", "s_diag", "s_maxb", "s_shift", "s_exp", "s_sum", "s_sumb", "s_pv", "s_olat"):
                g[n].passed(DB)
            for one in pages_in:
                one.passed(16 * N_PAGES * DB // 2)

    def pooling(self, h, y):
        nc, ps, io = self.nc, self.ps, self.io
        names = ("pool_in", "kept", "pooled", "pool_prod", "pool_y", "pool_out")
        g = {n: self.counter(n) for n in names}
        KEPT = WMAX - 1
        with ExitStack() as ctx:
            def sb(name, shape):
                return self.sb(ctx, "pl_" + name, shape)
            wp = sb("wp", [P, 4, 2, 2 * P])
            full = sb("full", [P, KC, DB, KEPT + DS])
            a, b = sb("a", [P, 2, NP]), sb("b", [P, 2, NP])
            sa, sbb = (sb(n, [P, 2, DB, KEPT + DS]) for n in ("sa", "sb"))
            pooled = sb("pooled", [P, KC, TP])
            with nc.Block() as block:
                @block.sync
                def _(sp):
                    sp.dma_start(full[:, :, :, 0:KEPT], io["pool_rows"]).then_inc(g["pool_in"].sem, 16)
                    sp.dma_start(wp[:, :, :, :], io["w_pool"]).then_inc(g["pool_in"].sem, 16)
                    sp.dma_start(io["pool_p"], h[:, :, NP - KEPT:NP]).then_inc(g["pool_out"].sem, 16)
                    sp.wait_ge(g["kept"].sem, g["kept"].at(1))
                    sp.dma_start(io["pool_s"], full[:, :, :, DS:KEPT + DS]).then_inc(g["pool_out"].sem, 16)
                    sp.wait_ge(g["pool_out"].sem, g["pool_out"].at(32))

                @block.vector
                def _(dve):
                    chain = Chain(dve, self.counter("dve_own"))
                    link = chain.link
                    tt, copy = nc.vector.tensor_tensor, nc.vector.tensor_copy
                    link(nc.vector.memset(pooled[:, :, NP:S0], 0.0))
                    dve.wait_ge(g["pool_in"].sem, g["pool_in"].at(32))
                    for k in range(KC):
                        last = copy(full[:, k, :, KEPT:], h[:, k, S0:TP].rearrange("p (b t) -> p b t", b=DB))
                    last.then_inc(g["kept"].sem, 1)
                    dve.wait_ge(g["kept"].sem, g["kept"].at(1))
                    for grp, w in enumerate(WINDOWS):
                        ks = slice(2 * grp, 2 * grp + 2)
                        src, to, other = h[:, ks, 0:NP], a[:, :, :], b[:, :, :]
                        ssrc, sto, sother = full[:, ks], sa[:, :, :, :], sbb[:, :, :, :]
                        shift, valid = 1, 0
                        if grp:
                            dve.wait_ge(g["pooled"].sem, g["pooled"].at(grp))
                        while shift < w:
                            copy(to[:, :, 0:shift], src[:, :, 0:shift])
                            tt(to[:, :, shift:], src[:, :, shift:], src[:, :, 0:NP - shift], ALU.add)
                            for k in range(2):
                                last = tt(sto[:, k, :, valid + shift:], ssrc[:, k, :, valid + shift:], ssrc[:, k, :, valid:KEPT + DS - shift], ALU.add)
                            link(last)
                            src, to, other = to, other, to
                            ssrc, sto, sother = sto, sother, sto
                            valid += shift
                            shift *= 2
                        ramp = self.c("ramp", lo=16 * grp, hi=16 * grp + 16).unsqueeze(1).to_broadcast([P, 2, 16])
                        link(tt(pooled[:, ks, 0:16], src[:, :, 0:16], ramp, ALU.mult))
                        tt(pooled[:, ks, 0:16], pooled[:, ks, 0:16], h[:, ks, 0:16], ALU.subtract)
                        for k in range(2):
                            nc.vector.scalar_tensor_tensor(out=pooled[:, 2 * grp + k, S0:TP].rearrange("p (b t) -> p b t", b=DB), in0=ssrc[:, k, :, KEPT:],
                                                           scalar=1.0 / w, in1=full[:, 2 * grp + k, :, KEPT:], op0=ALU.mult, op1=ALU.subtract)
                        nc.vector.scalar_tensor_tensor(out=pooled[:, ks, 16:NP], in0=src[:, :, 16:NP], scalar=1.0 / w, in1=h[:, ks, 16:NP],
                                                       op0=ALU.mult, op1=ALU.subtract).then_inc(g["pooled"].sem, 1)
                    dve.wait_ge(g["pooled"].sem, g["pooled"].at(4))
                    chain.close()

                @block.tensor
                def _(pe):
                    pe.wait_ge(g["pool_in"].sem, g["pool_in"].at(32))
                    for m in range(KC):
                        grp, half = divmod(m, 2)
                        pe.wait_ge(g["pooled"].sem, g["pooled"].at(grp + 1))
                        if m >= 2:
                            pe.wait_ge(g["pool_y"].sem, g["pool_y"].at(m - 1))
                        for n, (at, c) in enumerate(TILES):
                            for k in range(2):
                                last = nc.tensor.matmul(ps[:, 3 * half + n, 0:c], wp[:, grp, k, half * P:half * P + P], pooled[:, 2 * grp + k, at:at + c],
                                                        start=(k == 0), stop=(k == 1))
                        last.then_inc(g["pool_prod"].sem, 1)

                @block.scalar
                def _(act):
                    for m in range(KC):
                        act.wait_ge(g["pool_prod"].sem, g["pool_prod"].at(m + 1))
                        for n, (at, c) in enumerate(TILES):
                            last = nc.scalar.activation(y[:, m, at:at + c], ps[:, 3 * (m % 2) + n, 0:c], ACT.Copy, scale=self.v("pool_scale", m))
                        last.then_inc(g["pool_y"].sem, 1)
                    act.wait_ge(g["pool_y"].sem, g["pool_y"].at(KC))
            for n, events in (("pool_in", 32), ("kept", 1), ("pooled", 4), ("pool_prod", KC), ("pool_y", KC), ("pool_out", 32)):
                g[n].passed(events)

    def emit(self, stop_after):
        self.load()
        with ExitStack() as mix:
            z = self.sb(mix, "z", [P, NZ, TP])
            last = self.sb(mix, "last", [P, 15, 1 + DB])
            with ExitStack() as inner:
                h = self.sb(inner, "h0", [P, KC, TP])
                diff = self.sb(inner, "diff", [P, 1, TP])
                shift = self.sb(inner, "shift_rows", [P, 15, DB])
                with ExitStack() as first:
                    x0 = self.sb(first, "x0", [P, KC, TP])
                    self.fetch([(x0[:, :, :], self.io["x"]), (shift[:, :, :], self.io["shift_in"])])
                    self.norm("pre0", lambda k: x0[:, k, :], KC, lambda k: ("g_mix_pre", k), lambda k: h[:, k, :])
                self.gemm("in", self.io["w_in"], NZ, lambda k: h[:, k, :], z,
                          lambda dve, emptied: self.token_shift(dve, emptied, z, diff, last, shift))
            if stop_after == 1:
                return
            self.rwkv(z, last)
            if stop_after == 2:
                return
            self.norm("q_lora", lambda k: z[:, Z_Q + k, :], 3, lambda k: ("g_q", k), lambda k: z[:, Z_Q + k, :])
            self.norm("kv_lora", lambda k: z[:, Z_KV + k, :], 2, lambda k: ("g_kv", k), lambda k: z[:, Z_KV + k, :])
            with ExitStack() as inner:
                qsn = self.sb(inner, "qsn", [P, PAIRS, NS])
                qpe = self.sb(inner, "qpe", [ROPE, DB, H, DS])
                kps = self.sb(inner, "kps", [ROPE, NS])
                self.prompt_attention(z, qsn, qpe, kps)
                if stop_after == 3:
                    return
                self.sample_attention(z, qsn, qpe, kps)
                if stop_after == 4:
                    return
            self.x = self.sb(self.top, "x", [P, KC, TP], side="right")
            y = self.sb(self.top, "y", [P, KC, TP], side="right")
            self.fetch([(self.x[:, :, :], self.io["x"])])
            self.gemm("out", self.io["w_out"], KC, lambda k: z[:, (Z_K + k if k < PAIRS else Z_R + k - PAIRS), :], y)
        with ExitStack() as rest:
            h = self.sb(rest, "h", [P, KC, TP])

            def pre(name, gain, layer):
                self.norm(f"{name}{layer}", lambda k: self.x[:, k, :], KC, lambda k: (gain, KC * layer + k), lambda k: h[:, k, :])

            def post(name, gain, layer):
                self.norm(f"{name}{layer}", lambda k: y[:, k, :], KC, lambda k: (gain, KC * layer + k))

            post("mix_post", "g_mix_post", 0)
            pre("ffn_pre", "g_ffn_pre", 0)
            self.mlp(0, h, y)
            post("ffn_post", "g_ffn_post", 0)
            pre("mix_pre", "g_mix_pre", 1)
            self.pooling(h, y)
            post("mix_post", "g_mix_post", 1)
            pre("ffn_pre", "g_ffn_pre", 1)
            self.mlp(1, h, y)
            post("ffn_post", "g_ffn_post", 1)
        self.store()

    def store(self):
        stored = self.counter("stored")
        with self.nc.Block() as block:
            @block.sync
            def _(sp):
                sp.dma_start(self.io["y"], self.x[:, :, :]).then_inc(stored.sem, 16)
                sp.wait_ge(stored.sem, stored.at(16))


def lay_out(i):
    f = {k: np.asarray(a) for k, a in i.items()}
    out = {}

    def cols(a):
        return a.reshape(-1, P).T

    def slabs(w, n):
        return w.reshape(-1, P, n, P).transpose(2, 1, 0, 3)

    tokens = np.zeros((TP, D), np.float32)
    tokens[:N_META], tokens[N_META:NP] = f["meta_tokens"], f["x_prompt"][0]
    tokens[S0:] = f["x_sample"].reshape(NS, D)
    out["x"] = tokens.T.reshape(KC, P, TP).transpose(1, 0, 2)

    half = ROPE // 2
    swap = np.concatenate([np.arange(half, ROPE), np.arange(half)])
    w = f["w_in"][0]
    mla = Q_LORA + KV_LORA + ROPE
    pe, zb = w[:, mla - ROPE:mla], w[:, mla:]
    pad = np.zeros((D, 32), np.float32)
    w = np.concatenate([w[:, :mla - ROPE], pe, zb[:, -32:], pe[:, swap], pad, zb[:, :-32]], 1)
    out["w_in"] = slabs(w, NZ)
    up, down = f["w_up"], f["w_down"]
    parts = []
    for layer in range(2):
        for fb in range(N_FB):
            parts.append(slabs(up[layer][:, fb * D:(fb + 1) * D], KC))
            parts.append(slabs(down[layer][fb * D:(fb + 1) * D], KC))
    out["w_mlp"] = np.concatenate(parts)

    vec = np.zeros((P, NVEC), np.float32)

    def put(name, a):
        at, n = VECS[name]
        vec[:, at:at + n] = a

    for name in ("g_mix_pre", "g_mix_post", "g_ffn_pre", "g_ffn_post", "g_q", "g_kv", "w0", "a0", "k_k", "k_a",
                 "r_k", "ln_w", "ln_b", "pool_scale"):
        put(name, cols(f[name].reshape(-1)))
    mu = f["mu_shift"][0]
    tail = np.zeros(P, np.float32)
    tail[32:64] = mu[-32:]
    put("mu", cols(np.concatenate([mu[:-32], tail])))
    out["vec"] = vec

    def rwkv_rows(a):
        r = np.zeros((15, P, a.shape[0]), np.float32)
        r[:14] = a[:, :-32].T.reshape(14, P, -1)
        r[14, 32:64] = a[:, -32:].T
        return r.transpose(1, 0, 2)

    out["shift_in"] = rwkv_rows(f["state_shift"][0])
    out["w2a2"] = np.concatenate([f["w2"][0], f["a2"][0]])
    g2 = np.zeros((P, 2, D_B), np.float32)
    g2[:, 0], g2[32:64, 1] = f["g2"][0][:P], f["g2"][0][P:]
    out["g2"] = g2
    out["w_out"] = slabs(f["w_out"][0], KC)
    out["w_pool"] = f["w_pool"][0].reshape(4, 2, P, 2 * P).transpose(2, 0, 1, 3)
    out["pool_rows"] = f["state_pool"][0].reshape(DB, WMAX - 1, KC, P).transpose(3, 2, 0, 1)
    out["rope"] = rotary_tables()
    wuq = f["w_uq"][0].reshape(3, P, PAIRS, 2, NOPE + ROPE)
    wq = np.concatenate([wuq, wuq[..., NOPE + swap]], -1)
    wk, wv = (f[n][0].reshape(2, P, PAIRS, 2, HD) for n in ("w_uk", "w_uv"))
    out["w_pair"] = np.concatenate([a.transpose(2, 1, 0, 3, 4).reshape(PAIRS, P, -1) for a in (wq, wk, wv)], 2)
    out["w_ukT"] = wk.transpose(3, 4, 2, 0, 1).reshape(P, PAIRS, KV_LORA)
    out["w_uv"] = f["w_uv"][0].reshape(2, P, H * HD).transpose(1, 0, 2)
    out["pool"] = np.concatenate([f["cache_ckv"][0], f["cache_kpe"][0]], 2)
    out["table"] = f["page_table"].astype(np.int32).reshape(1, DB * N_PAGES)
    key, seq, t = np.arange(NS)[:, None, None], np.arange(DB)[None, :, None], np.arange(H * DS)[None, None, :] % DS
    out["new_mask"] = np.where((key // DS == seq) & (key % DS <= t), 0.0, NEG).astype(np.float32)
    out["state"] = f["state_wkv"][0].reshape(DB, PAIRS, 2, HD, HD).transpose(2, 4, 1, 0, 3).reshape(P, PAIRS, DB, HD)
    out["const"] = constants()
    return {k: np.ascontiguousarray(a) for k, a in out.items()}


OUTS = {"y": (P, KC, TP), "pool_p": (P, KC, WMAX - 1), "pool_s": (P, KC, DB, WMAX - 1), "ckv": (P, 2, TP), "kpe": (ROPE, TP), "shift": (P, 15, 1 + DB), "wkv_p": (P, PAIRS, HD), "wkv_s": (P, PAIRS, DB, HD)}


def kernel(**inputs):
    import concourse.bacc as bacc
    from concourse.bass_utils import run_bass_kernel_spmd

    nc = bacc.Bacc("TRN2", target_bir_lowering=False, num_devices=1)
    arrays = lay_out(inputs)
    io = {k: nc.dram_tensor(k + "_dram", a.shape, mybir.dt.from_np(a.dtype), kind="ExternalInput").ap() for k, a in arrays.items()}
    for k, shape in OUTS.items():
        io[k] = nc.dram_tensor(k + "_dram", shape, F32, kind="ExternalOutput").ap()
    build(nc, io)
    r = run_bass_kernel_spmd(nc, [{k + "_dram": a for k, a in arrays.items()}], core_ids=[0]).results[0]
    return collect({k: r[k + "_dram"] for k in OUTS})


def collect(o):
    def tokens(a):
        rows = a.transpose(2, 1, 0).reshape(TP, -1)
        return rows[:NP], rows[S0:].reshape(DB, DS, -1)

    y_p, y_s = tokens(o["y"])
    ckv_p, ckv_s = tokens(o["ckv"])
    kpe_p, kpe_s = tokens(o["kpe"][:, None, :])
    shift = o["shift"].transpose(2, 1, 0)
    shift = np.concatenate([shift[:, :14].reshape(1 + DB, -1), shift[:, 14, 32:64]], 1)
    wkv_p = o["wkv_p"].reshape(2, HD, PAIRS, HD).transpose(2, 0, 3, 1).reshape(1, 1, H, HD, HD)
    wkv_s = o["wkv_s"].reshape(2, HD, PAIRS, DB, HD).transpose(3, 2, 0, 4, 1).reshape(1, DB, H, HD, HD)
    pool_p = o["pool_p"].transpose(2, 1, 0).reshape(1, 1, WMAX - 1, D)
    pool_s = o["pool_s"].transpose(2, 3, 1, 0).reshape(1, DB, WMAX - 1, D)
    return tuple(np.ascontiguousarray(a) for a in (
        y_p[None, N_META:], y_s, ckv_p[None, None], kpe_p[None, None], wkv_p, shift[None, None, 0], pool_p,
        ckv_s[None], kpe_s[None], wkv_s, shift[None, 1:], pool_s))
```

```python
from contextlib import ExitStack

import numpy as np

import concourse.bass as bass
from concourse import mybir
from concourse.alu_op_type import AluOpType as ALU

F32 = mybir.dt.float32
F32R = mybir.dt.float32r
ACT = mybir.ActivationFunctionType
AX = mybir.AxisListType

P = 128
D = 1024
KC = D // P
N_META, SEQ = 16, 1024
NP = N_META + SEQ
DB, DS = 8, 4
NS = DB * DS
PAD = 16
S0 = NP + PAD
TP = S0 + NS
TILES = [(0, 364), (364, 362), (726, 362)]
assert sum(n for _, n in TILES) == TP

Q_LORA, KV_LORA, ROPE = 384, 256, 32
H, HD, PAIRS = 8, 64, 4
NOPE = 64
D_B = H * HD
RW_IN = 3 * D_B + 64 + 64 + 160
PAGE, N_PAGES, POOL_PAGES = 128, 32, 320
SM_SCALE = float((NOPE + ROPE) ** -0.5)
WMAX, WINDOWS = 16, (2, 4, 8, 16)
RMS_EPS, GN_EPS = 1e-6, 64e-5
NEG = -1e30

Z_Q, Z_KV, Z_PE, Z_R, Z_K, Z_V, Z_WA, Z_G, NZ = 0, 3, 5, 6, 10, 14, 18, 19, 20
N_FB = 8
SLABS = N_FB * 8
RING = 4

VECS = {}
_at = 0
for _name, _n in (("g_mix_pre", 16), ("g_mix_post", 16), ("g_ffn_pre", 16), ("g_ffn_post", 16), ("g_q", 3),
                  ("g_kv", 2), ("mu", 15), ("w0", 4), ("a0", 4), ("k_k", 4), ("k_a", 4), ("r_k", 4),
                  ("ln_w", 4), ("ln_b", 4), ("pool_scale", 8)):
    VECS[_name] = (_at, _n)
    _at += _n
NVEC = _at

CH = 32
RW_LINKS = 22
CONSTS = {}
_at = 0
for _name, _n in (("ident", P), ("head_ones", P), ("pair_ident", HD), ("grams", 2 * P), ("lower", P),
                  ("level", 5 * P), ("levelT", 5 * P), ("causal", P), ("grams_s", 2 * P), ("lower_s", P),
                  ("resets", P), ("resets_s", HD), ("seq_of", DB), ("new_causal", NS), ("ones", P),
                  ("eps", 2), ("ramp", 64)):
    CONSTS[_name] = (_at, _n)
    _at += _n
NCONST, LATE = _at, CONSTS["ones"][0]


def constants():
    c = np.zeros((P, NCONST), np.float32)

    def put(name, a):
        at, n = CONSTS[name]
        c[:a.shape[0], at:at + n] = a

    s, t = np.arange(P)[:, None], np.arange(P)[None, :]
    put("ident", np.eye(P))
    put("ones", np.ones((P, P)))
    put("head_ones", (s // HD == t // HD))
    put("pair_ident", np.tile(np.eye(HD), (2, 1)))
    same = s // CH == t // CH
    put("grams", np.concatenate([same & (s < t), same & (s <= t)], 1))
    put("lower", same & (s > t))
    put("level", np.concatenate([(s // (2 << l) == t // (2 << l)) & (s >> l & 1 == 1) & (t >> l & 1 == 0) for l in range(5)], 1))
    put("levelT", np.concatenate([(s // (2 << l) == t // (2 << l)) & (t >> l & 1 == 1) & (s >> l & 1 == 0) for l in range(5)], 1))
    put("causal", np.where(s >= t, 0.0, NEG))
    same = (s < CH) & (t < CH) | (s // DS == t // DS) & (s >= CH) & (t >= CH)
    put("grams_s", np.concatenate([same & (s < t), same & (s <= t)], 1))
    put("lower_s", same & (s > t))
    put("resets", np.tile(t % CH != 0, (P, 1)))
    col = np.arange(HD)[None, :]
    put("resets_s", np.tile(np.where(col < CH, col % CH != 0, col % DS != 0), (P, 1)))
    put("seq_of", (np.arange(P)[:, None] - CH) // DS == np.arange(DB)[None, :])
    put("new_causal", np.where(np.arange(DS)[:, None] <= np.arange(NS)[None, :] % DS, 0.0, NEG))
    put("eps", np.tile(np.array([[RMS_EPS, GN_EPS]]), (P, 1)))
    put("ramp", np.tile(np.concatenate([1.0 / np.minimum(np.arange(16) + 1, w) for w in WINDOWS])[None, :], (P, 1)))
    return c


def rotary_tables():
    half = ROPE // 2
    inv = (np.float32(10000.0) ** (-np.arange(half, dtype=np.float32) / np.float32(half))).astype(np.float32)
    pos = np.concatenate([np.arange(NP), np.zeros(PAD), np.tile(N_PAGES * PAGE + np.arange(DS), DB)]).astype(np.float32)
    ang = (inv[:, None] * pos[None, :]).astype(np.float32)
    cos, sin = np.cos(ang).astype(np.float32), np.sin(ang).astype(np.float32)
    return np.tile(np.stack([np.concatenate([cos, cos]), np.concatenate([-sin, sin])], 1), (4, 1, 1))


class Counter:

    def __init__(self, nc, ctx, name):
        self.sem = ctx.enter_context(nc.semaphore(name))
        self.base = 0

    def at(self, n):
        return self.base + n

    def passed(self, n):
        self.base += n


class Chain:

    def __init__(self, engine, counter):
        self.engine, self.counter, self.start, self.n = engine, counter, 0, 0

    def link(self, instruction):
        self.n += 1
        instruction.then_inc(self.counter.sem, 1)
        self.engine.wait_ge(self.counter.sem, self.counter.at(self.start + self.n))

    def iteration(self, i, length):
        self.before, self.length = self.start + self.n, length
        self.start, self.n = self.before + i * length, 0

    def loop_over(self, turns):
        assert self.n == self.length, f"this loop's body links {self.n}"
        self.start, self.n = self.before + turns * self.length, 0

    def close(self):
        self.counter.passed(self.start + self.n)


def build(nc, io, stop_after=99):
    with ExitStack() as top:
        Program(nc, io, top).emit(stop_after)


class Program:
    def __init__(self, nc, io, top):
        self.nc, self.io, self.top = nc, io, top
        self.vec = self.sb(top, "vec", [P, NVEC])
        self.late = self.sb(top, "late_const", [P, NCONST - LATE])
        self.ps = top.enter_context(nc.psum_tensor("ps", [P, 8, 512], F32))
        self.counters = {}

    def sb(self, ctx, name, shape, dt=F32, side="left"):
        return ctx.enter_context(self.nc.sbuf_tensor(name, shape, dt, side=side))

    def counter(self, name):
        if name not in self.counters:
            self.counters[name] = Counter(self.nc, self.top, name)
        return self.counters[name]

    FREED = ("emptied", "relu_done", "y_added", "s_pv", "slab_tails", "u_tail", "product")

    def v(self, name, k=0, n=1):
        at = VECS[name][0] + k
        return self.vec[:, at:at + n]

    def c(self, name, rows=slice(0, P), lo=0, hi=None):
        at, n = CONSTS[name]
        of, at = (self.late, at - LATE) if at >= LATE else (self.const, at)
        return of[rows, at + lo:at + (n if hi is None else hi)]

    def load(self):
        nc, io = self.nc, self.io
        loaded = self.counter("loaded")
        with nc.Block() as block:
            @block.sync
            def _(sp):
                for name in self.FREED:
                    sp.sem_inc(self.counter(name).sem, 2)
                    self.counter(name).passed(2)
                sp.dma_start(self.late[:, :], io["const"][:, LATE:]).then_inc(loaded.sem, 16)
                sp.dma_start(self.vec[:, :], io["vec"]).then_inc(loaded.sem, 16)
                sp.wait_ge(loaded.sem, loaded.at(32))
        loaded.passed(32)

    def fetch(self, pairs):
        loaded = self.counter("loaded")
        with self.nc.Block() as block:
            @block.sync
            def _(sp):
                for to, of in pairs:
                    sp.dma_start(to, of).then_inc(loaded.sem, 16)
                sp.wait_ge(loaded.sem, loaded.at(16 * len(pairs)))
        loaded.passed(16 * len(pairs))

    def norm(self, name, src, chunks, gain, dst=None, split=None):
        nc, ps = self.nc, self.ps
        squared, used, total = (self.counter(n) for n in ("squared", "sq_used", "total"))
        root, scaled, dve_done, added = (self.counter(n) for n in ("root", "scaled", "dve_own", "added"))
        residual = dst is None and split is None

        def by_pool(k):
            return k % 3 == 0

        def add(eng, api, k):
            eng.wait_ge(scaled.sem, scaled.at(k + 1))
            api.tensor_tensor(self.x[:, k, :], self.x[:, k, :], src(k), ALU.add).then_inc(added.sem, 1)

        part_head, part_tail = self.counter("part_head"), self.counter("part_tail")
        with ExitStack() as ctx:
            sq = self.sb(ctx, f"{name}_sq", [P, 2, TP])
            acc = self.sb(ctx, f"{name}_acc", [P, TP])
            rstd = self.sb(ctx, f"{name}_rstd", [P, TP])
            with nc.Block() as block:
                @block.scalar
                def _(act):
                    for k in range(chunks):
                        if k >= 3:
                            act.wait_ge(used.sem, used.at(k - 2))
                        to = acc[:, :] if k == 0 else sq[:, k % 2, :]
                        nc.scalar.activation(to, src(k), ACT.Square).then_inc(squared.sem, 1)
                    for n, (at, w) in enumerate(TILES):
                        act.wait_ge(total.sem, total.at(n + 1))
                        nc.scalar.activation(rstd[:, at:at + w], ps[:, n, 0:w], ACT.Sqrt, bias=self.c("eps", hi=1),
                                             scale=1.0 / (chunks * P)).then_inc(root.sem, 1)
                    if split is not None:
                        for k in range(chunks):
                            act.wait_ge(scaled.sem, scaled.at(k + 1))
                            nc.scalar.copy(split[:, 0, k, :], sq[:, k % 2, :]).then_inc(part_head.sem, 1)

                @block.tensor
                def _(pe):
                    pe.wait_ge(used.sem, used.at(chunks - 1))
                    for n, (at, w) in enumerate(TILES):
                        nc.tensor.matmul(ps[:, n, 0:w], self.c("ones"), acc[:, at:at + w], start=True, stop=True).then_inc(total.sem, 1)

                @block.vector
                def _(dve):
                    chain = Chain(dve, dve_done)
                    dve.wait_ge(squared.sem, squared.at(1))
                    for k in range(1, chunks):
                        dve.wait_ge(squared.sem, squared.at(k + 1))
                        if k > 1:
                            dve.wait_ge(used.sem, used.at(k - 1))
                        nc.vector.tensor_tensor(acc[:, :], acc[:, :], sq[:, k % 2, :], ALU.add).then_inc(used.sem, 1)
                    for n, (at, w) in enumerate(TILES):
                        dve.wait_ge(root.sem, root.at(n + 1))
                        last = nc.vector.reciprocal(rstd[:, at:at + w], rstd[:, at:at + w])
                    chain.link(last)

                    def tail_of(k):
                        dve.wait_ge(part_head.sem, part_head.at(k + 1))
                        nc.vector.tensor_tensor(split[:, 1, k, :], sq[:, k % 2, :], split[:, 0, k, :].bitcast(F32), ALU.subtract).then_inc(part_tail.sem, 1)

                    for k in range(chunks):
                        to = src(k) if residual else sq[:, k % 2, :] if split is not None else dst(k)
                        if split is not None and k >= 2:
                            dve.wait_ge(part_tail.sem, part_tail.at(k - 1))
                        nc.vector.scalar_tensor_tensor(out=to, in0=src(k), scalar=self.v(*gain(k)), in1=rstd[:, :],
                                                       op0=ALU.mult, op1=ALU.mult).then_inc(scaled.sem, 1)
                        if split is not None and k:
                            tail_of(k - 1)
                        if residual and k and not by_pool(k - 1):
                            add(dve, nc.vector, k - 1)
                    if split is not None:
                        tail_of(chunks - 1)
                    if residual:
                        add(dve, nc.vector, chunks - 1)
                    dve.wait_ge(scaled.sem, scaled.at(chunks))
                    chain.close()

                if residual:
                    @block.gpsimd
                    def _(pool):
                        for k in filter(by_pool, range(chunks)):
                            add(pool, nc.gpsimd, k)
                        pool.wait_ge(added.sem, added.at(chunks))
            squared.passed(chunks), used.passed(chunks - 1)
            total.passed(3), root.passed(3), scaled.passed(chunks)
            if residual:
                added.passed(chunks)
            if split is not None:
                part_head.passed(chunks), part_tail.passed(chunks)

    def gemm(self, name, slabs, n_slabs, rhs, out, to, of):
        nc, ps = self.nc, self.ps
        product, emptied, loaded = (self.counter(n) for n in ("product", "emptied", "loaded"))
        landed = [self.counter(f"slab_in{r}") for r in range(RING)]
        assert n_slabs % RING == 0
        with ExitStack() as ctx:
            ring = self.sb(ctx, f"{name}_ring", [P, RING, KC, P])
            with nc.Block() as block:
                @block.sync
                def _(sp):
                    def fetch(s, r):
                        sp.dma_start(ring[:, r, :, :], slabs[bass.ds(s, 1)].rearrange("a p k m -> p (a k) m")).then_inc(landed[r].sem, 16)
                    for r in range(RING):
                        fetch(r, r)
                    sp.dma_start(to, of).then_inc(loaded.sem, 16)
                    with sp.Fori(0, n_slabs // RING - 1) as g:
                        for r in range(RING):
                            sp.wait_ge(product.sem, product.at(g * RING + r + 1))
                            fetch(g * RING + RING + r, r)
                    sp.wait_ge(loaded.sem, loaded.at(16))

                @block.tensor
                def _(pe):
                    with pe.Fori(0, n_slabs // RING) as g:
                        for r in range(RING):
                            pe.wait_ge(landed[r].sem, landed[r].at(g * 16 + 16))
                            bank = 3 * (r % 2)
                            pe.wait_ge(emptied.sem, emptied.at(g * RING + r - 1))
                            self.slab_product(pe, ring, r, rhs, bank).then_inc(product.sem, 1)

                @block.scalar
                def _(act):
                    with act.Fori(0, n_slabs // RING) as g:
                        for r in range(RING):
                            act.wait_ge(product.sem, product.at(g * RING + r + 1))
                            bank = 3 * (r % 2)
                            for n, (at, w) in enumerate(TILES):
                                last = nc.scalar.copy(out[:, bass.ds(g * RING + r, 1), at:at + w],
                                                      ps[:, bank + n, 0:w].unsqueeze(1))
                            last.then_inc(emptied.sem, 1)
                    act.wait_ge(emptied.sem, emptied.at(n_slabs))

            for one in landed:
                one.passed(16 * n_slabs // RING)
            loaded.passed(16)
            product.passed(n_slabs), emptied.passed(n_slabs)

    def slab_product(self, pe, ring, r, rhs, bank):
        for n, (at, w) in enumerate(TILES):
            for k in range(KC):
                last = self.nc.tensor.matmul(self.ps[:, bank + n, 0:w], ring[:, r, k, :], rhs(k)[:, at:at + w],
                                             start=(k == 0), stop=(k == KC - 1))
        return last

    def three_passes(self, out, w, k, m, rhs, rk, at, c, start, stop):
        for n, (a, b) in enumerate(((0, 0), (0, 1), (1, 0))):
            last = self.nc.tensor.matmul(out, w[:, a, k, m], rhs[:, b, rk, at:at + c], start=(start and n == 0), stop=(stop and n == 2))
        return last

    def gemm_split(self, name, slabs, n_slabs, h, out, vector):
        nc, ps = self.nc, self.ps
        product, emptied, heads, tails = (self.counter(n) for n in ("product", "emptied", "slab_heads", "slab_tails"))
        landed = [self.counter(f"slab_in{r}") for r in range(2)]
        with ExitStack() as ctx:
            raw = self.sb(ctx, f"{name}_raw", [P, 2, KC, P])
            ring = [self.sb(ctx, f"{name}_split{r}", [P, 2, KC, P], F32R) for r in range(2)]
            with nc.Block() as block:
                @block.sync
                def _(sp):
                    with sp.Fori(0, n_slabs // 2) as g:
                        for r in range(2):
                            sp.wait_ge(tails.sem, tails.at(g * 2 + r - 1))
                            sp.dma_start(raw[:, r, :, :], slabs[bass.ds(g * 2 + r, 1)].rearrange("a p k m -> p (a k) m")).then_inc(landed[r].sem, 16)

                @block.tensor
                def _(pe):
                    with pe.Fori(0, n_slabs // 2) as g:
                        for r in range(2):
                            pe.wait_ge(tails.sem, tails.at(g * 2 + r + 1))
                            pe.wait_ge(emptied.sem, emptied.at(g * 2 + r - 1))
                            for n, (at, c) in enumerate(TILES):
                                for k in range(KC):
                                    last = self.three_passes(ps[:, 3 * r + n, 0:c], ring[r], k, slice(0, P), h, k, at, c, k == 0, k == KC - 1)
                            last.then_inc(product.sem, 1)

                @block.scalar
                def _(act):
                    def head(g, r):
                        act.wait_ge(landed[r].sem, landed[r].at(g * 16 + 16))
                        act.wait_ge(product.sem, product.at(g * 2 + r - 1))
                        nc.scalar.copy(ring[r][:, 0, :, :], raw[:, r, :, :]).then_inc(heads.sem, 1)

                    def turn(g, more):
                        for r in range(2):
                            if r == 0 or more:
                                head(g + r, 1 - r)
                            act.wait_ge(product.sem, product.at(g * 2 + r + 1))
                            for n, (at, c) in enumerate(TILES):
                                last = nc.scalar.copy(out[:, bass.ds(g * 2 + r, 1), at:at + c], ps[:, 3 * r + n, 0:c].unsqueeze(1))
                            last.then_inc(emptied.sem, 1)

                    head(0, 0)
                    with act.Fori(0, n_slabs // 2 - 1) as g:
                        turn(g, True)
                    turn(n_slabs // 2 - 1, False)
                    act.wait_ge(emptied.sem, emptied.at(n_slabs))

                @block.gpsimd
                def _(pool):
                    with pool.Fori(0, n_slabs // 2) as g:
                        for r in range(2):
                            pool.wait_ge(heads.sem, heads.at(g * 2 + r + 1))
                            nc.gpsimd.tensor_tensor(ring[r][:, 1, :, :], raw[:, r, :, :], ring[r][:, 0, :, :].bitcast(F32), ALU.subtract).then_inc(tails.sem, 1)

                @block.vector
                def _(dve):
                    vector(dve, emptied)
            for one in landed:
                one.passed(16 * n_slabs // 2)
            for one in (product, emptied, heads, tails):
                one.passed(n_slabs)

    def mlp(self, layer, h, y):
        nc, ps = self.nc, self.ps
        names = ("product", "relu_done", "y_added", "slab_heads", "slab_tails", "y_zero", "u_squared", "u_head", "u_tail")
        product, relu_done, y_added, heads, tails, y_zero, u_sq, u_head, u_tail = (self.counter(n) for n in names)
        landed = [self.counter(f"slab_in{r}") for r in range(2)]
        slabs = self.io["w_mlp"]
        first = layer * SLABS
        UP, SL = 4, 8
        with ExitStack() as ctx:
            raw = self.sb(ctx, f"mlp{layer}_raw", [P, 2, KC, P])
            ring = [self.sb(ctx, f"mlp{layer}_split{r}", [P, 2, KC, P], F32R) for r in range(2)]
            relu = self.sb(ctx, f"mlp{layer}_relu", [P, 2, TP])
            u = self.sb(ctx, f"mlp{layer}_u", [P, 2, UP, TP], F32R)
            with nc.Block() as block:
                @block.sync
                def _(sp):
                    with sp.Fori(0, SLABS // 2) as g:
                        for r in range(2):
                            sp.wait_ge(tails.sem, tails.at(g * 2 + r - 1))
                            sp.dma_start(raw[:, r, :, :], slabs[bass.ds(g * 2 + first + r, 1)].rearrange("a p k m -> p (a k) m")).then_inc(landed[r].sem, 16)

                @block.tensor
                def _(pe):
                    with pe.Fori(0, N_FB) as g:
                        for r in range(SL):
                            pe.wait_ge(tails.sem, tails.at(g * SL + r + 1))
                            if r < UP:
                                if r < 2:
                                    pe.wait_ge(y_added.sem, y_added.at(g * KC + r - 1))
                                else:
                                    pe.wait_ge(relu_done.sem, relu_done.at(g * UP + r - 1))
                                for k in range(KC):
                                    for n, (at, c) in enumerate(TILES):
                                        last = self.three_passes(ps[:, 3 * (r % 2) + n, 0:c], ring[r % 2], k, slice(0, P), h, k, at, c, k == 0, k == KC - 1)
                                last.then_inc(product.sem, 1)
                                continue
                            for half in range(2):
                                m = 2 * (r - UP) + half
                                if r == UP:
                                    pe.wait_ge(relu_done.sem, relu_done.at(g * UP + 3 + half))
                                else:
                                    pe.wait_ge(y_added.sem, y_added.at(g * KC + m - 1))
                                for k in range(UP):
                                    if m == 0:
                                        pe.wait_ge(u_tail.sem, u_tail.at(g * UP + k + 1))
                                    for n, (at, c) in enumerate(TILES):
                                        last = self.three_passes(ps[:, 3 * half + n, 0:c], ring[r % 2], UP * half + k, slice(0, P), u, k, at, c, k == 0, k == UP - 1)
                                last.then_inc(product.sem, 1)

                def made(r):
                    return r + 1 if r < UP else UP + 2 * (r - UP + 1)

                TURN = made(SL - 1)

                @block.scalar
                def _(act):
                    def head(g, r):
                        act.wait_ge(landed[r % 2].sem, landed[r % 2].at(g * (8 * SL) + 16 * (r // 2 + 1)))
                        act.wait_ge(product.sem, product.at(g * TURN + (made(r - 2) if r > 1 else 2 * r - 2)))
                        nc.scalar.copy(ring[r % 2][:, 0, :, :], raw[:, r % 2, :, :]).then_inc(heads.sem, 1)

                    def turn(g, more):
                        for r in range(SL):
                            if r < SL - 1:
                                head(g, r + 1)
                            elif more:
                                head(g + 1, 0)
                            if r < UP:
                                act.wait_ge(product.sem, product.at(g * TURN + r + 1))
                                act.wait_ge(u_tail.sem, u_tail.at(g * UP + r - 1))
                                for n, (at, c) in enumerate(TILES):
                                    last = nc.scalar.activation(relu[:, r % 2, at:at + c], ps[:, 3 * (r % 2) + n, 0:c], ACT.Relu)
                                last.then_inc(relu_done.sem, 1)
                                act.wait_ge(u_sq.sem, u_sq.at(g * UP + r + 1))
                                nc.scalar.copy(u[:, 0, r, :], relu[:, r % 2, :]).then_inc(u_head.sem, 1)

                    head(0, 0)
                    with act.Fori(0, N_FB - 1) as g:
                        turn(g, True)
                    turn(N_FB - 1, False)

                @block.vector
                def _(dve):
                    tt = nc.vector.tensor_tensor

                    def tail(g, r):
                        dve.wait_ge(heads.sem, heads.at(g * SL + r + 1))
                        tt(ring[r % 2][:, 1, :, :], raw[:, r % 2, :, :], ring[r % 2][:, 0, :, :].bitcast(F32), ALU.subtract).then_inc(tails.sem, 1)

                    def turn(g, more):
                        for r in range(SL):
                            if r < SL - 1:
                                tail(g, r + 1)
                            elif more:
                                tail(g + 1, 0)
                            if r < UP:
                                dve.wait_ge(relu_done.sem, relu_done.at(g * UP + r + 1))
                                tt(relu[:, r % 2, :], relu[:, r % 2, :], relu[:, r % 2, :], ALU.mult).then_inc(u_sq.sem, 1)
                                dve.wait_ge(u_head.sem, u_head.at(g * UP + r + 1))
                                tt(u[:, 1, r, :], relu[:, r % 2, :], u[:, 0, r, :].bitcast(F32), ALU.subtract).then_inc(u_tail.sem, 1)
                                continue
                            for half in range(2):
                                m = 2 * (r - UP) + half
                                dve.wait_ge(product.sem, product.at(g * TURN + UP + m + 1))
                                for n, (at, c) in enumerate(TILES):
                                    last = tt(y[:, m, at:at + c], y[:, m, at:at + c], ps[:, 3 * half + n, 0:c], ALU.add)
                                last.then_inc(y_added.sem, 1)
                        dve.wait_ge(y_added.sem, y_added.at(g * KC + KC))

                    tail(0, 0)
                    nc.vector.memset(y[:, :, :], 0.0).then_inc(y_zero.sem, 1)
                    dve.wait_ge(y_zero.sem, y_zero.at(1))
                    with dve.Fori(0, N_FB - 1) as g:
                        turn(g, True)
                    turn(N_FB - 1, False)
            for one in landed:
                one.passed(16 * SLABS // 2)
            for one, events in ((product, N_FB * TURN), (y_added, N_FB * KC), (heads, SLABS), (tails, SLABS), (y_zero, 1),
                                (relu_done, N_FB * UP), (u_sq, N_FB * UP), (u_head, N_FB * UP), (u_tail, N_FB * UP)):
                one.passed(events)

    def token_shift(self, dve, emptied, z, diff, last, shift):
        nc = self.nc
        chain = Chain(dve, self.counter("dve_own"))

        def chunk(m, zc, rows, mu):
            starts = slice(S0, TP, DS)
            nc.vector.tensor_copy(last[rows, m, 0:1], zc[:, :, NP - 1:NP])
            chain.link(nc.vector.tensor_copy(last[rows, m, 1:1 + DB], zc[:, :, S0 + DS - 1:TP:DS]))
            nc.vector.tensor_scalar(diff[rows, :, 0:1], zc[:, :, 0:1], -1.0, None, ALU.mult)
            chain.link(nc.vector.tensor_tensor(diff[rows, :, 1:TP], zc[:, :, 0:TP - 1], zc[:, :, 1:TP], ALU.subtract))
            chain.link(nc.vector.tensor_tensor(diff[rows, :, starts], shift[rows, m, :], zc[:, :, starts], ALU.subtract))
            chain.link(nc.vector.scalar_tensor_tensor(out=zc, in0=diff[rows], scalar=mu, in1=zc, op0=ALU.mult, op1=ALU.add))

        chain.link(nc.vector.memset(last[:, :, :], 0.0))
        dve.wait_ge(emptied.sem, emptied.at(Z_PE + 1))
        tail = slice(32, 64)
        chunk(slice(14, 15), z[tail, Z_PE:Z_PE + 1, :], tail, self.vec[tail, VECS["mu"][0] + 14:VECS["mu"][0] + 15])
        with dve.Fori(0, NZ - Z_R) as m:
            chain.iteration(m, 4)
            dve.wait_ge(emptied.sem, emptied.at(m + Z_R + 1))
            chunk(bass.ds(m, 1), z[:, bass.ds(m + Z_R, 1), :], slice(0, P), self.vec[:, bass.ds(m + VECS["mu"][0], 1)])
        chain.loop_over(NZ - Z_R)
        chain.close()

    def rwkv(self, z, last):
        nc, ps, io = self.nc, self.ps, self.io
        names = ("rw_loaded", "block_done", "lora_in", "lora_out", "lora_act", "kk_sq", "kk_sum", "kk_root", "cumulated",
                 "exps", "v_in", "scaled_in", "bonus_in", "bonus_sum", "turned", "turned_out", "gram", "gram_out",
                 "level_b", "prod_p", "p_out", "prod_x", "x_out", "prod_mv", "mv_out", "prod_wg", "wg_out",
                 "prod_r", "prod_f", "f_out", "tt_out", "rhat", "y_in", "step", "state", "gn_in", "gn_sum", "gn_c", "gn_sq",
                 "gn_root", "rw_out", "s_masked", "s_prod", "s_tt", "s_fout", "s_step", "s_state")
        g = {n: self.counter(n) for n in names}
        per_block = {"gram": 3, "gram_out": 3, "level_b": 4, "prod_p": 8, "p_out": 8, "prod_x": 8, "x_out": 8, "step": 4, "state": 4}

        def waits(engine):
            def wait(name, i, n=None):
                c = per_block.get(name, 1)
                engine.wait_ge(g[name].sem, g[name].at(i * c + (c if n is None else n)))
            return wait

        B_FULL = NP // P
        N_BLOCKS = B_FULL + 1
        with ExitStack() as ctx:
            def sb(name, shape):
                return self.sb(ctx, "rw_" + name, shape)
            w2a2 = sb("w2a2", [P, D_B])
            g2 = sb("g2", [P, 2, D_B])
            tw, tg, tg2 = sb("tw", [P, P]), sb("tg", [P, P]), sb("tg2", [P, P])
            sw, a, gate = sb("sw", [P, PAIRS, P]), sb("a", [P, PAIRS, P]), sb("gate", [P, PAIRS, P])
            gate_in = sb("gate_in", [P, PAIRS, P])
            vs, kk, ke = sb("v", [P, PAIRS, P]), sb("kk", [P, PAIRS, P]), sb("ke", [P, PAIRS, P])
            t1, t2 = sb("t1", [P, PAIRS, P]), sb("t2", [P, PAIRS, P])
            cum, cump = sb("cum", [P, PAIRS, P]), sb("cump", [P, PAIRS, P])
            KR, kp, bp = sb("KR", [P, PAIRS, 2, P]), sb("kp", [P, PAIRS, P]), sb("bp", [P, PAIRS, P])
            vt, kt, bt = sb("vt", [P, H, HD]), sb("kt", [P, H, HD]), sb("bt", [P, H, HD])
            rhs, wg = sb("rhs", [P, H, P]), sb("wg", [P, H, P])
            MK, MB, A = sb("MK", [P, H, 2, P]), sb("MB", [P, H, 2, P]), sb("A", [P, H, P])
            X, XT, BT, PM = sb("X", [P, H, P]), sb("XT", [P, H, P]), sb("BT", [P, H, P]), A
            TT, F = BT[:, :, :].rearrange("p h (a k) -> p (h a) k", a=2), X[:, :, :].rearrange("p h (a k) -> p (h a) k", a=2)
            S, tmp = sb("S", [P, PAIRS, HD]), sb("tmp", [P, PAIRS, HD])
            y, bonus = sb("y", [P, PAIRS, P]), sb("bonus", [P, PAIRS, P])
            S_s = sb("S_s", [P, PAIRS, DB, HD])
            bm, vm = ([MK[:, 4 * n + 2 * q:4 * n + 2 * q + 2, :, :].rearrange("p a b c -> p (a b c)") for q in range(2)] for n in range(2))
            wm = [MB[:, 2 * q:2 * q + 2, :, :].rearrange("p a b c -> p (a b c)") for q in range(2)]
            TTs = XT[:, 0:4, :].rearrange("p a (b k) -> p (a b) k", b=2)
            Fs, tmps = (A[:, 4 * n:4 * n + 4, :].rearrange("p a (b k) -> p (a b) k", b=2) for n in range(2))

            def rows(h):
                return slice(HD * (h % 2), HD * (h % 2) + HD)

            def vb(name, W):
                return self.v(name, n=PAIRS).unsqueeze(2).to_broadcast([P, PAIRS, W])

            def zb(c, i, W):
                return z[:, c:c + PAIRS, bass.ds(i * P, W)]

            def nar(t, W):
                return t[:, :, 0:W]

            def pb(bank, n, W):
                return ps[:, bank, 0:n * W].rearrange("p (a w) -> p a w", a=n)

            with nc.Block() as block:
                @block.sync
                def _(sp):
                    sp.dma_start(w2a2[:, :], io["w2a2"]).then_inc(g["rw_loaded"].sem, 16)
                    sp.dma_start(g2[:, :, :], io["g2"]).then_inc(g["rw_loaded"].sem, 16)
                    sp.dma_start(S_s[:, :, :, :], io["state"]).then_inc(g["rw_loaded"].sem, 16)
                    sp.dma_start(io["shift"], last[:, :, :]).then_inc(g["rw_out"].sem, 16)
                    sp.wait_ge(g["block_done"].sem, g["block_done"].at(N_BLOCKS))
                    sp.dma_start(io["wkv_p"], S[:, :, :]).then_inc(g["rw_out"].sem, 16)
                    sp.dma_start(io["wkv_s"], S_s[:, :, :, :]).then_inc(g["rw_out"].sem, 16)
                    sp.wait_ge(g["rw_out"].sem, g["rw_out"].at(48))

                @block.scalar
                def _(act):
                    wait = waits(act)

                    def lora_in(i, W):
                        cols = bass.ds(i * P, W)
                        nc.scalar.activation(tw[0:64, 0:W], z[0:64, Z_WA, cols], ACT.Tanh)
                        nc.scalar.activation(tg[:, 0:W], z[:, Z_G, cols], ACT.Sigmoid)
                        nc.scalar.activation(tg2[32:64, 0:W], z[32:64, Z_PE, cols], ACT.Sigmoid)
                        nc.scalar.copy(tw[64:128, 0:W], z[64:128, Z_WA, cols]).then_inc(g["lora_in"].sem, 1)

                    def rates(i, W):
                        wait("lora_out", i)
                        for p in range(PAIRS):
                            nc.scalar.activation(nar(sw, W)[:, p, :], pb(6, PAIRS, W)[:, p, :], ACT.Sigmoid, bias=self.v("w0", p))
                            last_rate = nc.scalar.activation(nar(a, W)[:, p, :], pb(7, PAIRS, W)[:, p, :], ACT.Sigmoid, bias=self.v("a0", p))
                        last_rate.then_inc(g["lora_act"].sem, 1)
                        nc.scalar.copy(nar(gate_in, W), pb(5, PAIRS, W))
                        nc.scalar.copy(nar(vs, W), zb(Z_V, i, W)).then_inc(g["v_in"].sem, 1)

                    def key_root(i, W):
                        wait("kk_sum", i)
                        nc.scalar.activation(nar(cump, W), pb(7, PAIRS, W), ACT.Sqrt).then_inc(g["kk_root"].sem, 1)

                    def exps(i, W):
                        wait("cumulated", i)
                        nc.scalar.activation(nar(cump, W), nar(cump, W), ACT.Exp)
                        nc.scalar.activation(nar(sw, W), nar(cum, W), ACT.Exp, scale=-1.0)
                        nc.scalar.activation(nar(cum, W), nar(cum, W), ACT.Exp).then_inc(g["exps"].sem, 1)

                    def turn(i, W, W_next):
                        wait("turned", i)
                        for n, to in enumerate((vt, kt, bt)):
                            nc.scalar.copy(to[0:W, :, :], ps[0:W, 4 + n, :].rearrange("p (h c) -> p h c", h=H))
                        nc.scalar.copy(rhs[0:W, :, HD:P], ps[0:W, 7, :].rearrange("p (h c) -> p h c", h=H)).then_inc(g["turned_out"].sem, 1)
                        if W_next:
                            lora_in(i + 1, W_next)
                        wait("prod_mv", i)
                        nc.scalar.copy(rhs[0:W, :, 0:HD], ps[0:W, 6, :].rearrange("p (h c) -> p h c", h=H)).then_inc(g["mv_out"].sem, 1)
                        for level in range(1, 5):
                            for half in range(2):
                                wait("prod_p", i, 2 * (level - 1) + half + 1)
                                nc.scalar.copy(PM[0:W, 4 * half:4 * half + 4, 0:W], pb(3 * half, 4, W)[0:W]).then_inc(g["p_out"].sem, 1)
                            if level == 1 and W_next:
                                key_root(i + 1, W_next)
                        wait("prod_wg", i)
                        for half in range(2):
                            last_out = nc.scalar.mul(wg[0:W, 4 * half:4 * half + 4, :], pb(7 * half, 4, P)[0:W], -1.0)
                        last_out.then_inc(g["wg_out"].sem, 1)
                        wait("prod_r", i)
                        nc.scalar.copy(nar(y, W), pb(3, PAIRS, W)).then_inc(g["y_in"].sem, 1)
                        wait("tt_out", i)
                        for j in range(4 if W == P else 1):
                            last_out = nc.scalar.copy(F[:, 4 * j:4 * j + 4, :], pb(4 + j, 8, HD)[:, 4:8, :])
                        last_out.then_inc(g["f_out"].sem, 1)
                        if W < P:
                            for p in range(PAIRS):
                                act.wait_ge(g["s_prod"].sem, g["s_prod"].at(p + 1))
                                nc.scalar.copy(Fs[:, :, :], pb(5, DB, HD)).then_inc(g["s_fout"].sem, 1)
                        if W_next:
                            rates(i + 1, W_next)
                            exps(i + 1, W_next)
                        wait("gn_sq", i)
                        nc.scalar.activation(nar(t2, W), pb(3, PAIRS, W), ACT.Sqrt, bias=self.c("eps", lo=1), scale=1.0 / HD).then_inc(g["gn_root"].sem, 1)

                    lora_in(0, P)
                    rates(0, P)
                    key_root(0, P)
                    exps(0, P)
                    with act.Fori(0, B_FULL - 1) as i:
                        turn(i, P, P)
                    turn(B_FULL - 1, P, HD)
                    turn(B_FULL, HD, 0)

                @block.vector
                def _(dve):
                    wait = waits(dve)
                    chain = Chain(dve, self.counter("dve_own"))
                    link = chain.link
                    tt, stt, ts = nc.vector.tensor_tensor, nc.vector.scalar_tensor_tensor, nc.vector.tensor_scalar

                    def removal_key(i, W):
                        link(tt(nar(kk, W), zb(Z_K, i, W), vb("k_k", W), ALU.mult))
                        tt(nar(cump, W), nar(kk, W), nar(kk, W), ALU.mult).then_inc(g["kk_sq"].sem, 1)

                    def normalise_key(i, W):
                        wait("kk_root", i)
                        link(ts(nar(cump, W), nar(cump, W), 1e-12, None, ALU.max))
                        link(nc.vector.reciprocal(nar(cump, W), nar(cump, W)))
                        link(tt(nar(kk, W), nar(kk, W), nar(cump, W), ALU.mult))

                    def decay(i, W):
                        full = W == P
                        resets = self.c("resets", hi=P) if full else self.c("resets_s")
                        wait("lora_act", i)
                        link(ts(nar(sw, W), nar(sw, W), -float(np.exp(-0.5)), None, ALU.mult))
                        if not full:
                            link(nc.vector.memset(sw[:, :, NP % P:CH], 0.0))
                        for p in range(PAIRS):
                            last_scan = nc.vector.tensor_tensor_scan(cum[:, p, 0:W], resets, sw[:, p, 0:W], 0.0, ALU.mult, ALU.add)
                        link(last_scan)
                        tt(nar(cump, W), nar(cum, W), nar(sw, W), ALU.subtract).then_inc(g["cumulated"].sem, 1)

                    def scale(i, W):
                        full = W == P
                        k_in, r_in = zb(Z_K, i, W), zb(Z_R, i, W)
                        link(stt(out=nar(ke, W), in0=nar(a, W), scalar=-1.0, in1=vb("k_a", W), op0=ALU.add, op1=ALU.mult))
                        link(stt(out=nar(ke, W), in0=nar(ke, W), scalar=1.0, in1=k_in, op0=ALU.add, op1=ALU.mult))
                        link(tt(nar(a, W), nar(kk, W), nar(a, W), ALU.mult))
                        if not full:
                            nc.vector.memset(a[:, :, NP % P:CH], 0.0)
                            link(nc.vector.memset(ke[:, :, NP % P:CH], 0.0))
                        wait("exps", i)
                        tt(KR[:, :, 0, 0:W], nar(kk, W), nar(cump, W), ALU.mult)
                        tt(KR[:, :, 1, 0:W], r_in, nar(cum, W), ALU.mult)
                        tt(nar(kp, W), nar(ke, W), nar(sw, W), ALU.mult)
                        tt(nar(bp, W), nar(a, W), nar(sw, W), ALU.mult).then_inc(g["scaled_in"].sem, 1)

                    def turn(i, W, W_next):
                        full = W == P
                        r_in = zb(Z_R, i, W)
                        grams, lower = ("grams", "lower") if full else ("grams_s", "lower_s")
                        mask = self.c(grams, slice(0, W)).rearrange("p (b w) -> p b w", b=2)[:, :, 0:W]
                        for n, (to, bank) in enumerate(((MB, 0), (MK, 4))):
                            wait("gram", i, n + 1)
                            for q in range(4):
                                for e in range(2):
                                    mm = tt(to[0:W, 4 * (q // 2) + 2 * e + q % 2, :, 0:W], ps[0:W, bank + q, 2 * W * e:2 * W * (e + 1)].rearrange("p (b w) -> p b w", b=2), mask, ALU.mult)
                            mm.then_inc(g["gram_out"].sem, 1)
                        wait("gram", i, 3)
                        low = self.c(lower, slice(0, W), hi=W).unsqueeze(1).to_broadcast([W, 4, W])
                        for q in range(2):
                            mm = tt(A[0:W, q:H:2, 0:W], pb(q, 4, W)[0:W], low, ALU.mult)
                        mm.then_inc(g["gram_out"].sem, 1)
                        dve.wait_ge(g["gram_out"].sem, g["gram_out"].at(i * 3 + 3))

                        def lv(name, level):
                            return self.c(name, slice(0, W), lo=level * P, hi=level * P + W).unsqueeze(1).to_broadcast([W, H, W])
                        ident = self.c("ident", slice(0, W), hi=W).unsqueeze(1).to_broadcast([W, H, W])
                        AT = MB[0:W, :, 0, 0:W]
                        stt(out=X[0:W, :, 0:W], in0=A[0:W, :, 0:W], scalar=-1.0, in1=lv("level", 0), op0=ALU.mult, op1=ALU.mult)
                        link(stt(out=XT[0:W, :, 0:W], in0=AT, scalar=-1.0, in1=lv("levelT", 0), op0=ALU.mult, op1=ALU.mult))
                        tt(X[0:W, :, 0:W], X[0:W, :, 0:W], ident, ALU.add)
                        link(tt(XT[0:W, :, 0:W], XT[0:W, :, 0:W], ident, ALU.add))
                        for level in range(1, 5):
                            if level > 1:
                                wait("prod_p", i, 2 * (level - 1))
                            tt(BT[0:W, :, 0:W], AT, lv("levelT", level), ALU.mult).then_inc(g["level_b"].sem, 1)
                            if level == 1 and W_next:
                                removal_key(i + 1, W_next)
                            if level == 1:
                                link(tt(nar(t1, W), r_in, vb("r_k", W), ALU.mult))
                                tt(nar(t1, W), nar(t1, W), nar(ke, W), ALU.mult).then_inc(g["bonus_in"].sem, 1)
                            if level == 3:
                                wait("bonus_sum", i)
                                wait("v_in", i)
                                link(tt(nar(bonus, W), pb(6, PAIRS, W), nar(vs, W), ALU.mult))
                                link(tt(nar(bonus, W), nar(bonus, W), vb("ln_b", W), ALU.add))
                                tt(nar(bonus, W), nar(bonus, W), nar(gate_in, W), ALU.mult)
                                tt(nar(gate, W), nar(gate_in, W), vb("ln_w", W), ALU.mult)
                            for half in range(2):
                                wait("prod_x", i, 2 * (level - 1) + half + 1)
                                hs = slice(4 * half, 4 * half + 4)
                                if level < 4:
                                    tt(X[0:W, hs, 0:W], X[0:W, hs, 0:W], pb(3 * half + 1, 4, W)[0:W], ALU.subtract)
                                tt(XT[0:W, hs, 0:W], XT[0:W, hs, 0:W], pb(3 * half + 2, 4, W)[0:W], ALU.subtract).then_inc(g["x_out"].sem, 1)
                            dve.wait_ge(g["x_out"].sem, g["x_out"].at(i * 8 + 2 * level))
                        wait("prod_r", i)
                        tt(KR[:, :, 1, 0:W], KR[:, :, 1, 0:W], pb(2, PAIRS, W), ALU.add).then_inc(g["rhat"].sem, 1)
                        if W_next:
                            normalise_key(i + 1, W_next)
                        wait("prod_f", i)
                        chunks = 4 if full else 1
                        eye = self.c("pair_ident").unsqueeze(1)
                        for j in range(chunks):
                            mm = tt(TT[:, 4 * j:4 * j + 4, :], pb(4 + j, 8, HD)[:, 0:4, :], eye.to_broadcast([P, 4, HD]), ALU.add)
                        mm.then_inc(g["tt_out"].sem, 1)
                        wait("f_out", i)
                        wait("y_in", i)
                        for j in range(chunks):
                            b0 = 2 * (j % 2)
                            wait("step", i, j + 1)
                            link(tt(tmp[:, :, :], pb(b0, PAIRS, HD), F[:, 4 * j:4 * j + 4, :], ALU.add))
                            end = cum[:, :, CH * j + CH - 1:CH * j + CH].to_broadcast([P, PAIRS, HD])
                            tt(S[:, :, :], tmp[:, :, :], end, ALU.mult).then_inc(g["state"].sem, 1)
                            cols = slice(CH * j, CH * j + CH)
                            yadd = tt(y[:, :, cols], y[:, :, cols], pb(b0 + 1, PAIRS, CH), ALU.add)
                        if full:
                            yadd.then_inc(g["gn_in"].sem, 1)
                        else:
                            link(yadd)
                            seq = self.c("seq_of", slice(CH, HD)).unsqueeze(2).to_broadcast([CH, DB, HD])
                            rs = slice(CH, HD)
                            for p in range(PAIRS):
                                if p:
                                    dve.wait_ge(g["s_prod"].sem, g["s_prod"].at(p))
                                for e in range(2):
                                    for to, of in ((bm, bt[rs, 2 * p + e, :]), (vm, vt[rs, 2 * p + e, :]), (wm, wg[rs, 2 * p + e, 0:HD])):
                                        mm = tt(to[e][rs, :].rearrange("p (b k) -> p b k", b=DB), of.unsqueeze(1).to_broadcast([CH, DB, HD]), seq, ALU.mult)
                                mm.then_inc(g["s_masked"].sem, 1)
                                dve.wait_ge(g["s_prod"].sem, g["s_prod"].at(p + 1))
                                tt(TTs, pb(4, DB, HD), eye.to_broadcast([P, DB, HD]), ALU.add).then_inc(g["s_tt"].sem, 1)
                                dve.wait_ge(g["s_fout"].sem, g["s_fout"].at(p + 1))
                                dve.wait_ge(g["s_step"].sem, g["s_step"].at(p + 1))
                                link(tt(tmps, pb(6, DB, HD), Fs, ALU.add))
                                end = cum[:, p, CH + DS - 1:HD:DS].unsqueeze(2).to_broadcast([P, DB, HD])
                                tt(S_s[:, p, :, :], tmps, end, ALU.mult)
                                yadd = tt(y[:, p, rs], y[:, p, rs], ps[:, 7, NS * p:NS * p + NS], ALU.add)
                            yadd.then_inc(g["gn_in"].sem, 1)
                        wait("gn_sum", i)
                        link(stt(out=nar(t1, W), in0=pb(4, PAIRS, W), scalar=-1.0 / HD, in1=nar(y, W), op0=ALU.mult, op1=ALU.add))
                        tt(nar(t2, W), nar(t1, W), nar(t1, W), ALU.mult).then_inc(g["gn_c"].sem, 1)
                        if W_next:
                            decay(i + 1, W_next)
                            scale(i + 1, W_next)
                        wait("gn_root", i)
                        link(nc.vector.reciprocal(nar(t2, W), nar(t2, W)))
                        link(tt(nar(t1, W), nar(t1, W), nar(t2, W), ALU.mult))
                        link(tt(nar(t1, W), nar(t1, W), nar(gate, W), ALU.mult))
                        tt(zb(Z_R, i, W), nar(t1, W), nar(bonus, W), ALU.add).then_inc(g["block_done"].sem, 1)
                        wait("block_done", i)

                    link(nc.vector.memset(S[:, :, :], 0.0))
                    removal_key(0, P)
                    normalise_key(0, P)
                    decay(0, P)
                    scale(0, P)
                    with dve.Fori(0, B_FULL - 1) as i:
                        chain.iteration(i, RW_LINKS)
                        turn(i, P, P)
                    chain.loop_over(B_FULL - 1)
                    turn(B_FULL - 1, P, HD)
                    turn(B_FULL, HD, 0)
                    chain.close()

                @block.tensor
                def _(pe):
                    wait = waits(pe)
                    mm = nc.tensor.matmul

                    def lora(i, W, p):
                        if p == 0:
                            wait("lora_in", i)
                        m, w = slice(p * P, p * P + P), slice(0, W)
                        mm(pb(6, PAIRS, W)[:, p, :], w2a2[0:64, m], tw[0:64, w], start=True, stop=True)
                        mm(pb(7, PAIRS, W)[:, p, :], w2a2[64:128, m], tw[64:128, w], start=True, stop=True)
                        mm(pb(5, PAIRS, W)[:, p, :], g2[:, 0, m], tg[:, w], start=True, stop=False)
                        end = mm(pb(5, PAIRS, W)[:, p, :], g2[32:64, 1, m], tg2[32:64, w], start=False, stop=True)
                        if p == PAIRS - 1:
                            end.then_inc(g["lora_out"].sem, 1)

                    def key_sum(i, W):
                        wait("kk_sq", i)
                        mm(pb(7, PAIRS, W), self.c("head_ones"), nar(cump, W), start=True, stop=True).then_inc(g["kk_sum"].sem, 1)

                    def turn(i, W, W_next):
                        full = W == P
                        heads = [(h, h // 2, rows(h)) for h in range(H)]
                        w = slice(0, W)
                        wait("v_in", i)
                        wait("scaled_in", i)
                        for n, of in enumerate((nar(vs, W), nar(kp, W), nar(bp, W), KR[:, :, 0, w])):
                            for p in range(PAIRS):
                                end = nc.tensor.transpose(ps[w, 4 + n, p * P:p * P + P], of[:, p, :], self.c("ident"))
                        end.then_inc(g["turned"].sem, 1)
                        for n, (of, bank) in enumerate(((bp, 0), (kp, 4))):
                            if n:
                                wait("turned_out", i)
                            for h, p, rr in heads:
                                at = 2 * W * (p % 2)
                                end = mm(ps[w, bank + 2 * (h // 4) + h % 2, at:at + 2 * W].rearrange("q (a b) -> q a b", a=2), of[rr, p, w], KR[rr, p, :, w], start=True, stop=True)
                            end.then_inc(g["gram"].sem, 1)
                        wait("gram_out", i, 1)
                        for h, p, rr in heads:
                            end = mm(pb(h % 2, 4, W)[w, p, :], KR[rr, p, 0, w], bp[rr, p, w], start=True, stop=True)
                        end.then_inc(g["gram"].sem, 1)
                        wait("gram_out", i, 2)
                        for h, p, rr in heads:
                            end = mm(ps[w, 6, h * HD:h * HD + HD], MK[w, h, 0, w], vt[w, h, :], start=True, stop=True)
                        end.then_inc(g["prod_mv"].sem, 1)
                        for level in range(1, 5):
                            wait("level_b", i, level)
                            if level > 1:
                                wait("x_out", i, 2 * (level - 1))
                            for half in range(2):
                                for q in range(4):
                                    h = 4 * half + q
                                    end = mm(pb(3 * half, 4, W)[w, q, :], BT[w, h, w], X[w, h, w], start=True, stop=True)
                                end.then_inc(g["prod_p"].sem, 1)
                            for half in range(2):
                                wait("p_out", i, 2 * (level - 1) + half + 1)
                                for q in range(4):
                                    h = 4 * half + q
                                    if level < 4:
                                        mm(pb(3 * half + 1, 4, W)[w, q, :], XT[w, h, w], PM[w, h, w], start=True, stop=True)
                                    end = mm(pb(3 * half + 2, 4, W)[w, q, :], PM[w, h, w], XT[w, h, w], start=True, stop=True)
                                end.then_inc(g["prod_x"].sem, 1)
                            if level == 1 and W_next:
                                key_sum(i + 1, W_next)
                            if level == 2:
                                wait("mv_out", i)
                                wait("bonus_in", i)
                                mm(pb(6, PAIRS, W), self.c("head_ones"), nar(t1, W), start=True, stop=True).then_inc(g["bonus_sum"].sem, 1)
                        wait("x_out", i)
                        wait("mv_out", i)
                        for h, p, rr in heads:
                            end = mm(ps[w, 7 * (h // 4), P * (h % 4):P * (h % 4) + P], XT[w, h, w], rhs[w, h, :], start=True, stop=True)
                        end.then_inc(g["prod_wg"].sem, 1)
                        wait("wg_out", i)
                        for h, p, rr in heads:
                            mm(pb(2, PAIRS, W)[rr, p, :], wg[w, h, HD:P], MB[w, h, 1, w], start=True, stop=True)
                        for h, p, rr in heads:
                            mm(pb(3, PAIRS, W)[rr, p, :], vt[w, h, :], MK[w, h, 1, w], start=True, stop=False)
                            end = mm(pb(3, PAIRS, W)[rr, p, :], wg[w, h, 0:HD], MB[w, h, 1, w], start=False, stop=True)
                        end.then_inc(g["prod_r"].sem, 1)
                        chunks = 4 if full else 1
                        for j in range(chunks):
                            c = slice(CH * j, CH * j + CH)
                            for h, p, rr in heads:
                                mm(pb(4 + j, 8, HD)[rr, p, :], wg[c, h, HD:P], bt[c, h, :], start=True, stop=True)
                                mm(pb(4 + j, 8, HD)[rr, PAIRS + p, :], kt[c, h, :], vt[c, h, :], start=True, stop=False)
                                end = mm(pb(4 + j, 8, HD)[rr, PAIRS + p, :], bt[c, h, :], wg[c, h, 0:HD], start=False, stop=True)
                        end.then_inc(g["prod_f"].sem, 1)
                        for j in range(chunks):
                            b0 = 2 * (j % 2)
                            pe.wait_ge(g["rw_loaded"].sem, g["rw_loaded"].at(48))
                            if j:
                                wait("state", i, j)
                            else:
                                wait("tt_out", i)
                                wait("rhat", i)
                                wait("y_in", i)
                            for h, p, rr in heads:
                                mm(pb(b0, PAIRS, HD)[rr, p, :], TT[rr, 4 * j + p, :], S[rr, p, :], start=True, stop=True)
                            for h, p, rr in heads:
                                end = mm(pb(b0 + 1, PAIRS, CH)[rr, p, :], S[rr, p, :], KR[rr, p, 1, CH * j:CH * j + CH], start=True, stop=True)
                            end.then_inc(g["step"].sem, 1)
                            if W_next:
                                if j == 0:
                                    wait("f_out", i)
                                lora(i + 1, W_next, j)
                        if not full:
                            c = slice(CH, HD)
                            pe.wait_ge(g["rw_loaded"].sem, g["rw_loaded"].at(48))
                            for p in range(PAIRS):
                                pe.wait_ge(g["s_masked"].sem, g["s_masked"].at(p + 1))
                                if p:
                                    pe.wait_ge(g["s_fout"].sem, g["s_fout"].at(p))
                                for e in range(2):
                                    h, rr = 2 * p + e, rows(e)
                                    mm(ps[rr, 4, :], wg[c, h, HD:P], bm[e][c, :], start=True, stop=True)
                                    mm(ps[rr, 5, :], kt[c, h, :], vm[e][c, :], start=True, stop=False)
                                    end = mm(ps[rr, 5, :], bt[c, h, :], wm[e][c, :], start=False, stop=True)
                                end.then_inc(g["s_prod"].sem, 1)
                                pe.wait_ge(g["s_tt"].sem, g["s_tt"].at(p + 1))
                                if p == 0:
                                    wait("f_out", i)
                                for e in range(2):
                                    rr = rows(e)
                                    for b in range(DB):
                                        mm(ps[rr, 6, b * HD:b * HD + HD], TTs[rr, b, :], S_s[rr, p, b, :], start=True, stop=True)
                                        at = NS * p + DS * b
                                        end = mm(ps[rr, 7, at:at + DS], S_s[rr, p, b, :], KR[rr, p, 1, CH + DS * b:CH + DS * b + DS], start=True, stop=True)
                                end.then_inc(g["s_step"].sem, 1)
                        wait("gn_in", i)
                        mm(pb(4, PAIRS, W), self.c("head_ones"), nar(y, W), start=True, stop=True).then_inc(g["gn_sum"].sem, 1)
                        wait("gn_c", i)
                        mm(pb(3, PAIRS, W), self.c("head_ones"), nar(t2, W), start=True, stop=True).then_inc(g["gn_sq"].sem, 1)
                        wait("gn_root", i)

                    pe.wait_ge(g["rw_loaded"].sem, g["rw_loaded"].at(48))
                    for p in range(PAIRS):
                        lora(0, P, p)
                    wait("lora_act", 0)
                    key_sum(0, P)
                    with pe.Fori(0, B_FULL - 1) as i:
                        turn(i, P, P)
                    turn(B_FULL - 1, P, HD)
                    turn(B_FULL, HD, 0)
            for n in names:
                events = per_block.get(n, 1)
                if n in ("step", "state"):
                    g[n].passed(4 * B_FULL + 1)
                elif n in ("rw_loaded", "rw_out"):
                    g[n].passed(48)
                elif n.startswith("s_"):
                    g[n].passed(PAIRS)
                else:
                    g[n].passed(events * N_BLOCKS)

    def prompt_attention(self, z, qsn, qpe, kps):
        nc, ps, io = self.nc, self.ps, self.io
        names = ("rope_in", "kpe_prod", "kpe_done", "pair_w", "proj", "proj_out", "q_rot", "scores", "neg_max", "exp_done", "probs",
                 "flipped", "flip_a", "flip_v", "values", "values_out", "latent_out")
        g = {n: self.counter(n) for n in names}
        NB = -(-NP // P)
        U = 2 * NB
        WQ, WK, WV = 3 * 2 * P, 2 * P, 2 * P
        with ExitStack() as ctx:
            def sb(name, shape):
                return self.sb(ctx, "pa_" + name, shape)
            rope = sb("rope", [P, 2, TP])
            w = sb("w", [P, WQ + WK + WV])
            QT, KT = sb("QT", [P, 2, TP]), sb("KT", [96, 2, TP])
            rot = sb("rot", [P, TP])
            V = sb("V", [P, NB, P])
            E, PT = sb("E", [P, 2, NB * P]), sb("PT", [P, 2, NB, P])
            mx, nm, sums, rs = (sb(n, [P, 2]) for n in ("mx", "nm", "sums", "rs"))
            wq = w[:, 0:WQ].rearrange("p (k m) -> p k m", k=3)
            wk = w[:, WQ:WQ + WK].rearrange("p (k m) -> p k m", k=2)
            wv = w[:, WQ + WK:].rearrange("p (k m) -> p k m", k=2)

            def block_of(u):
                e, i = divmod(u, NB)
                return e, i, min(P, NP - i * P)

            def rr(e):
                return slice(HD * e, HD * e + HD)

            def wide(u):
                return sum(v % NB >= 4 for v in range(u))

            with nc.Block() as block:
                @block.sync
                def _(sp):
                    sp.dma_start(rope[:, :, :], io["rope"]).then_inc(g["rope_in"].sem, 16)
                    sp.dma_start(io["ckv"], z[:, Z_KV:Z_KV + 2, :]).then_inc(g["latent_out"].sem, 16)
                    with sp.Fori(0, PAIRS) as p:
                        sp.wait_ge(g["proj"].sem, g["proj"].at(p * 5))
                        sp.dma_start(w[:, :].unsqueeze(1), io["w_pair"][bass.ds(p, 1)].rearrange("a p m -> p a m")).then_inc(g["pair_w"].sem, 16)
                    sp.wait_ge(g["kpe_done"].sem, g["kpe_done"].at(1))
                    sp.dma_start(io["kpe"], KT[64:96, 0, :]).then_inc(g["latent_out"].sem, 16)
                    sp.wait_ge(g["latent_out"].sem, g["latent_out"].at(32))

                @block.tensor
                def _(pe):
                    mm = nc.tensor.matmul

                    def scores(p, u):
                        e, i, n = block_of(u)
                        if u == 0:
                            pe.wait_ge(g["kpe_done"].sem, g["kpe_done"].at(2))
                        if i == 0:
                            pe.wait_ge(g["q_rot"].sem, g["q_rot"].at(p * 2 + e + 1))
                        q = QT[0:96, e, i * P:i * P + n]
                        bank = 3 * (u % 2)
                        for at in range(0, i * P, 512):
                            c = min(512, i * P - at)
                            mm(ps[0:n, bank + at // 512, 0:c], q, KT[:, e, at:at + c], start=True, stop=True)
                        d = i * P
                        to = ps[0:n, bank + d // 512, d % 512:d % 512 + n]
                        mm(to, q, KT[:, e, d:d + n], start=True, stop=False)
                        mm(to, self.c("ident", hi=n), self.c("causal", hi=n), start=False, stop=True).then_inc(g["scores"].sem, 1)

                    with pe.Fori(0, PAIRS) as p:
                        pe.wait_ge(g["pair_w"].sem, g["pair_w"].at(p * 16 + 16))
                        for e in range(2):
                            for n, (at, c) in enumerate(TILES):
                                for k in range(3):
                                    last = mm(ps[:, 3 * e + n, 0:c], wq[:, k, e * P:e * P + P], z[:, Z_Q + k, at:at + c], start=(k == 0), stop=(k == 2))
                            last.then_inc(g["proj"].sem, 1)
                        for e in range(2):
                            pe.wait_ge(g["proj_out"].sem, g["proj_out"].at(p * 5 + e + 1))
                            for n, (at, c) in enumerate(TILES):
                                for k in range(2):
                                    last = mm(ps[0:64, 3 * e + n, 0:c], wk[:, k, e * HD:e * HD + HD], z[:, Z_KV + k, at:at + c], start=(k == 0), stop=(k == 1))
                            last.then_inc(g["proj"].sem, 1)
                        pe.wait_ge(g["proj_out"].sem, g["proj_out"].at(p * 5 + 3))
                        for i in range(NB):
                            n = min(P, NP - i * P)
                            for k in range(2):
                                last = mm(ps[0:n, i // 4, (i % 4) * P:(i % 4) * P + P], z[:, Z_KV + k, i * P:i * P + n], wv[:, k, :], start=(k == 0), stop=(k == 1))
                        last.then_inc(g["proj"].sem, 1)
                        pe.wait_ge(g["proj_out"].sem, g["proj_out"].at(p * 5 + 5))
                        scores(p, 0)
                        for u in range(U):
                            e, i, n = block_of(u)
                            if u + 1 < U:
                                scores(p, u + 1)
                            probs_at = g["probs"].at(p * U + u + 1)
                            if n < P:
                                probs_at = pe.compute_val(probs_at)
                                pe.wait_ge(g["kpe_done"].sem, g["kpe_done"].at(2))
                            pe.wait_ge(g["probs"].sem, probs_at)
                            for kb in range(i + 1):
                                m = min(P, NP - kb * P)
                                last = nc.tensor.transpose(ps[0:m, 3 * (u % 2) + kb // 4, (kb % 4) * P:(kb % 4) * P + n],
                                                           E[0:n, u % 2, kb * P:kb * P + m], self.c("ident", slice(0, n), hi=n))
                            last.then_inc(g["flipped"].sem, 1)
                            pe.wait_ge(g["flip_a"].sem, g["flip_a"].at(p * U + u + 1))
                            if i >= 4:
                                pe.wait_ge(g["flip_v"].sem, g["flip_v"].at(p * wide(U) + wide(u + 1)))
                            if u >= 2:
                                pe.wait_ge(g["values_out"].sem, g["values_out"].at(p * U + u - 1))
                            for kb in range(i + 1):
                                m = min(P, NP - kb * P)
                                last = mm(ps[rr(e), 6 + u % 2, 0:n], V[0:m, kb, rr(e)], PT[0:m, u % 2, kb, 0:n], start=(kb == 0), stop=(kb == i))
                            last.then_inc(g["values"].sem, 1)
                        pe.wait_ge(g["values_out"].sem, g["values_out"].at(p * U + U))

                @block.scalar
                def _(act):
                    def exp(p, u):
                        e, i, n = block_of(u)
                        act.wait_ge(g["neg_max"].sem, g["neg_max"].at(p * U + u + 1))
                        cols = i * P + n
                        src = ps[0:n, 3 * (u % 2):3 * (u % 2) + 3, :].rearrange("p a b -> p (a b)")[:, 0:cols]
                        nc.scalar.activation(E[0:n, u % 2, 0:cols], src, ACT.Exp, bias=nm[0:n, u % 2:u % 2 + 1], scale=SM_SCALE,
                                             accum_out=sums[0:n, u % 2:u % 2 + 1]).then_inc(g["exp_done"].sem, 1)

                    act.wait_ge(g["kpe_done"].sem, g["kpe_done"].at(1))
                    nc.scalar.copy(KT[64:96, 1, :], KT[64:96, 0, :])
                    nc.scalar.copy(kps[:, :], KT[64:96, 0, S0:TP]).then_inc(g["kpe_done"].sem, 1)
                    with act.Fori(0, PAIRS) as p:
                        for e in range(2):
                            act.wait_ge(g["proj"].sem, g["proj"].at(p * 5 + e + 1))
                            for n, (at, c) in enumerate(TILES):
                                last = nc.scalar.copy(QT[:, e, at:at + c], ps[:, 3 * e + n, 0:c])
                            last.then_inc(g["proj_out"].sem, 1)
                        for e in range(2):
                            act.wait_ge(g["proj"].sem, g["proj"].at(p * 5 + e + 3))
                            for n, (at, c) in enumerate(TILES):
                                last = nc.scalar.copy(KT[0:64, e, at:at + c], ps[0:64, 3 * e + n, 0:c])
                            last.then_inc(g["proj_out"].sem, 1)
                        act.wait_ge(g["proj"].sem, g["proj"].at(p * 5 + 5))
                        for n in range(2):
                            nc.scalar.copy(V[:, 4 * n:4 * n + 4, :], ps[:, n, :].rearrange("p (a b) -> p a b", a=4))
                        nc.scalar.copy(V[0:NP % P, NB - 1, :], ps[0:NP % P, 2, 0:P]).then_inc(g["proj_out"].sem, 1)
                        for e in range(2):
                            act.wait_ge(g["q_rot"].sem, g["q_rot"].at(p * 2 + e + 1))
                            nc.scalar.copy(qsn[rr(e), bass.ds(p, 1), :], QT[0:64, e, S0:TP].unsqueeze(1))
                            nc.scalar.copy(qpe[:, :, bass.ds(p * 2 + e, 1), :],
                                           QT[64:96, e, S0:TP].rearrange("p (b a t) -> p b a t", b=DB, a=1))
                        exp(p, 0)
                        for u in range(U):
                            e, i, n = block_of(u)
                            act.wait_ge(g["flipped"].sem, g["flipped"].at(p * U + u + 1))
                            for b in range(0, i // 4 + 1, 2):
                                m = min(4, i + 1 - 4 * b)
                                full = min(m, NP // P - 4 * b)
                                if full:
                                    last = nc.scalar.copy(PT[:, u % 2, 4 * b:4 * b + full, 0:n],
                                                          ps[:, 3 * (u % 2) + b, 0:full * P].rearrange("p (a b) -> p a b", a=full)[:, :, 0:n])
                                if full < m:
                                    last = nc.scalar.copy(PT[0:NP % P, u % 2, NB - 1, 0:n], ps[0:NP % P, 3 * (u % 2) + b, 0:n])
                            last.then_inc(g["flip_a"].sem, 1)
                            if u + 1 < U:
                                exp(p, u + 1)
                            act.wait_ge(g["values"].sem, g["values"].at(p * U + u + 1))
                            nc.scalar.copy(z[rr(e), bass.ds(p + Z_K, 1), i * P:i * P + n], ps[rr(e), 6 + u % 2, 0:n].unsqueeze(1)).then_inc(g["values_out"].sem, 1)
                    act.wait_ge(g["values_out"].sem, g["values_out"].at(PAIRS * U))

                @block.vector
                def _(dve):
                    chain = Chain(dve, self.counter("dve_own"))
                    link = chain.link
                    tt = nc.vector.tensor_tensor

                    def neg_max(p, u):
                        e, i, n = block_of(u)
                        dve.wait_ge(g["scores"].sem, g["scores"].at(p * U + u + 1))
                        src = ps[0:n, 3 * (u % 2):3 * (u % 2) + 3, :].rearrange("p a b -> p (a b)")[:, 0:i * P + n]
                        c = slice(u % 2, u % 2 + 1)
                        link(nc.vector.tensor_reduce(mx[0:n, c], src, AX.X, ALU.max))
                        nc.vector.tensor_scalar(nm[0:n, c], mx[0:n, c], -SM_SCALE, None, ALU.mult).then_inc(g["neg_max"].sem, 1)

                    def normalise(p, u):
                        e, i, n = block_of(u)
                        c = slice(u % 2, u % 2 + 1)
                        dve.wait_ge(g["exp_done"].sem, g["exp_done"].at(p * U + u + 1))
                        link(nc.vector.reciprocal(rs[0:n, c], sums[0:n, c]))
                        row = E[0:n, u % 2, 0:i * P + n]
                        nc.vector.tensor_scalar(row, row, rs[0:n, c], None, ALU.mult).then_inc(g["probs"].sem, 1)

                    dve.wait_ge(g["rope_in"].sem, g["rope_in"].at(16))
                    tt(rot[64:96, :], z[0:32, Z_PE, :], rope[0:32, 0, :], ALU.mult)
                    link(tt(KT[64:96, 0, :], z[64:96, Z_PE, :], rope[64:96, 1, :], ALU.mult))
                    tt(KT[64:96, 0, :], KT[64:96, 0, :], rot[64:96, :], ALU.add).then_inc(g["kpe_done"].sem, 1)
                    dve.wait_ge(g["kpe_done"].sem, g["kpe_done"].at(1))
                    with dve.Fori(0, PAIRS) as p:
                        chain.iteration(p, 38)
                        for e in range(2):
                            dve.wait_ge(g["proj_out"].sem, g["proj_out"].at(p * 5 + e + 1))
                            tt(rot[64:96, :], QT[96:128, e, :], rope[96:128, 1, :], ALU.mult)
                            link(tt(QT[64:96, e, :], QT[64:96, e, :], rope[64:96, 0, :], ALU.mult))
                            tt(QT[64:96, e, :], QT[64:96, e, :], rot[64:96, :], ALU.add).then_inc(g["q_rot"].sem, 1)
                            dve.wait_ge(g["q_rot"].sem, g["q_rot"].at(p * 2 + e + 1))
                        neg_max(p, 0)
                        normalise(p, 0)
                        for u in range(U):
                            e, i, n = block_of(u)
                            if u + 1 < U:
                                neg_max(p, u + 1)
                            dve.wait_ge(g["flipped"].sem, g["flipped"].at(p * U + u + 1))
                            if i >= 4:
                                if u >= 2:
                                    dve.wait_ge(g["values"].sem, g["values"].at(p * U + u - 1))
                                m = min(4, i - 3)
                                nc.vector.tensor_copy(PT[:, u % 2, 4:4 + m, 0:n], ps[:, 3 * (u % 2) + 1, 0:m * P].rearrange("p (a b) -> p a b", a=m)[:, :, 0:n]).then_inc(g["flip_v"].sem, 1)
                            if u + 1 < U:
                                normalise(p, u + 1)
                    chain.loop_over(PAIRS)
                    chain.close()
            for n, events in (("rope_in", 16), ("kpe_prod", 0), ("kpe_done", 2), ("pair_w", 64), ("proj", 20), ("proj_out", 20), ("q_rot", 8), ("latent_out", 32)):
                g[n].passed(events)
            for n in ("scores", "neg_max", "exp_done", "probs", "flipped", "flip_a", "values", "values_out"):
                g[n].passed(PAIRS * U)
            g["flip_v"].passed(PAIRS * wide(U))

    def sample_attention(self, z, qsn, qpe, kps):
        nc, ps, io = self.nc, self.ps, self.io
        names = ("sa_in", "qlat_prod", "qlat", "new_prod", "new_scores", "q_copied", "turn_c", "turn_a", "turn_v", "s_scores", "s_max",
                 "s_maxT", "s_diag", "s_maxb", "s_shift", "s_exp", "s_sum", "s_sumb", "s_pv", "s_olat", "olat_prod", "olat_done", "sa_o", "sa_out")
        g = {n: self.counter(n) for n in names}
        QUARTERS = 4
        pages_in = [[self.counter(f"pages_in{n}_{q}") for q in range(QUARTERS)] for n in range(2)]
        EVENTS = 16 * N_PAGES // QUARTERS
        ROW = KV_LORA + ROPE
        GROUP = 4
        NG = N_PAGES // GROUP
        QR = H * DS
        with ExitStack() as ctx:
            def sb(name, shape, dt=F32):
                return self.sb(ctx, "sa_" + name, shape, dt)
            C = sb("C", [P, 2, N_PAGES, ROW])
            table = sb("table", [1, DB * N_PAGES], mybir.dt.int32)
            wukT, wuv = sb("wukT", [P, PAIRS, KV_LORA]), sb("wuv", [P, 2, H * HD])
            mask = sb("mask", [NS, DB, QR])
            qlat, olat = sb("qlat", [P, 2, DB, QR]), sb("olat", [P, 2, DB, QR])
            ctok, Sn, pn = sb("ctok", [NS, KV_LORA]), sb("Sn", [NS, DB, QR]), sb("pn", [NS, QR])
            cT, kT = sb("cT", [P, 2, GROUP, 2, P]), sb("kT", [ROPE, 2, GROUP, P])
            qb, qpb = sb("qb", [P, 2, 2, QR]), sb("qpb", [ROPE, 2, QR])
            Pb = sb("Pb", [P, N_PAGES, QR])
            mx, mb, sm = (sb(n, [P, QR]) for n in ("mx", "mb", "sm"))
            rinv = sb("rinv", [QR, 1])
            orow = z[0:QR, Z_Q:Z_Q + 2, :]
            m1, dg = sb("m1", [QR, 1]), sb("dg", [QR, QR])
            UNITS = 3 * NG

            def by_act(n):
                return n % 2 == 0

            def sg(name, b, c=1, n=None):
                return g[name].at(b * c + (c if n is None else n))

            scored = ps[:, 4:6, :].rearrange("p a (j q) -> p (a j) q", q=QR)

            with nc.Block() as block:
                @block.sync
                def _(sp):
                    sp.dma_start(table[:, :], io["table"]).then_inc(g["sa_in"].sem, 16)
                    sp.dma_start(wukT[:, :, :], io["w_ukT"]).then_inc(g["sa_in"].sem, 16)
                    sp.dma_start(wuv[:, :, :], io["w_uv"]).then_inc(g["sa_in"].sem, 16)
                    sp.dma_start(mask[:, :, :], io["new_mask"]).then_inc(g["sa_in"].sem, 16)
                    sp.wait_ge(g["sa_in"].sem, g["sa_in"].at(64))
                    with sp.Fori(0, DB // 2) as b2:
                        for s in range(2):
                            read_at = sp.compute_val(g["s_pv"].at(b2 * 2 + s - 1))
                            sp.wait_ge(g["sa_in"].sem, g["sa_in"].at(64))
                            sp.wait_ge(g["s_pv"].sem, read_at)
                            for quarter in range(QUARTERS):
                                with sp.Fori(0, N_PAGES // QUARTERS // GROUP) as j:
                                    at = [quarter * (N_PAGES // QUARTERS) + j * GROUP + q for q in range(GROUP)]
                                    pages = [sp.value_load(table[0:1, bass.ds(b2 * (2 * N_PAGES) + s * N_PAGES + n, 1)], min_val=0, max_val=POOL_PAGES - 1) for n in at]
                                    for n, page in zip(at, pages):
                                        sp.dma_start(C[:, s, bass.ds(n, 1), :], io["pool"][bass.ds(page, 1)].rearrange("a p m -> p a m")).then_inc(pages_in[s][quarter].sem, 16)

                @block.tensor
                def _(pe):
                    mm = nc.tensor.matmul
                    pe.wait_ge(g["sa_in"].sem, g["sa_in"].at(64))
                    for h in range(H):
                        p, e = divmod(h, 2)
                        r = slice(HD * e, HD * e + HD)
                        for k in range(2):
                            last = mm(ps[:, e, (2 * p + k) * NS:(2 * p + k + 1) * NS], wukT[r, p, k * P:k * P + P], qsn[r, p, :], start=True, stop=True)
                    for k in range(2):
                        last = nc.tensor.transpose(ps[0:NS, 2, k * P:k * P + P], z[:, Z_KV + k, S0:TP], self.c("ident"))
                    last.then_inc(g["qlat_prod"].sem, 1)
                    pe.wait_ge(g["qlat"].sem, g["qlat"].at(1))
                    for k in range(2):
                        mm(ps[0:NS, 3, 0:DB * QR], z[:, Z_KV + k, S0:TP], qlat[:, k, :, :], start=(k == 0), stop=False)
                    mm(ps[0:NS, 3, 0:DB * QR], kps[:, :], qpe[:, :, :, :], start=False, stop=True).then_inc(g["new_prod"].sem, 1)
                    pe.wait_ge(g["new_scores"].sem, g["new_scores"].at(1))

                    def scores(b, s, grp):
                        n = 3 * grp + 2
                        pe.wait_ge(g["turn_a"].sem, g["turn_a"].at(b * (UNITS // 2) + (n + 2) // 2))
                        pe.wait_ge(g["turn_v"].sem, g["turn_v"].at(b * (UNITS // 2) + (n + 1) // 2))
                        for q in range(GROUP):
                            j = GROUP * grp + q
                            for k in range(2):
                                mm(scored[:, j, :], cT[:, grp % 2, q, k, :], qb[:, s, k, :], start=(k == 0), stop=False)
                            last = mm(scored[:, j, :], kT[:, grp % 2, q, :], qpb[:, s, :], start=False, stop=True)
                        return last

                    with pe.Fori(0, DB // 2) as b2:
                        for s in range(2):
                            b = b2 * 2 + s
                            pe.wait_ge(g["q_copied"].sem, sg("q_copied", b))
                            for grp in range(NG + 1):
                                if grp < NG:
                                    if grp % (NG // QUARTERS) == 0:
                                        arrived = pages_in[s][grp // (NG // QUARTERS)]
                                        pe.wait_ge(arrived.sem, arrived.at(b2 * EVENTS + EVENTS))
                                    for v in range(3):
                                        n = 3 * grp + v
                                        if n >= 4:
                                            name = "turn_a" if by_act(n) else "turn_v"
                                            pe.wait_ge(g[name].sem, g[name].at(b * (UNITS // 2) + (n - 4) // 2 + 1))
                                        for q in range(4):
                                            if v < 2:
                                                j, k = GROUP * grp + 2 * v + q // 2, q % 2
                                                last = nc.tensor.transpose(ps[:, n % 4, q * P:q * P + P], C[:, s, j, k * P:k * P + P], self.c("ident"))
                                            else:
                                                j = GROUP * grp + q
                                                last = nc.tensor.transpose(ps[0:ROPE, n % 4, q * P:q * P + P], C[:, s, j, KV_LORA:ROW], self.c("ident"))
                                        last.then_inc(g["turn_c"].sem, 1)
                                if grp:
                                    last = scores(b, s, grp - 1)
                                    last.then_inc(g["s_scores"].sem, 1)
                            pe.wait_ge(g["s_max"].sem, sg("s_max", b))
                            nc.tensor.transpose(ps[0:QR, 6, 0:P], mx[:, :], self.c("ident")).then_inc(g["s_maxT"].sem, 1)
                            pe.wait_ge(g["s_diag"].sem, sg("s_diag", b))
                            mm(ps[:, 6, P:P + QR], self.c("ones", slice(0, QR)), dg[:, :], start=True, stop=True).then_inc(g["s_maxb"].sem, 1)
                            pe.wait_ge(g["s_exp"].sem, sg("s_exp", b))
                            for j in range(N_PAGES):
                                mm(ps[0:QR, 7, 0:KV_LORA], Pb[:, j, :], C[:, s, j, 0:KV_LORA], start=(j == 0), stop=False)
                            mm(ps[0:QR, 7, 0:KV_LORA], pn[:, :], ctok[:, :], start=False, stop=True).then_inc(g["s_pv"].sem, 1)
                            pe.wait_ge(g["s_sum"].sem, sg("s_sum", b))
                            mm(ps[0:QR, 6, 2 * P:2 * P + 1], sm[:, :], self.c("ones", hi=1), start=True, stop=True).then_inc(g["s_sumb"].sem, 1)
                            pe.wait_ge(g["s_olat"].sem, sg("s_olat", b))
                    for k in range(2):
                        for b in range(DB):
                            last = nc.tensor.transpose(ps[:, 0, (k * DB + b) * QR:(k * DB + b + 1) * QR], orow[:, k, b * P:b * P + P], self.c("ident", slice(0, QR), hi=QR))
                    last.then_inc(g["olat_prod"].sem, 1)
                    pe.wait_ge(g["olat_done"].sem, g["olat_done"].at(1))
                    for h in range(H):
                        p, e = divmod(h, 2)
                        r = slice(HD * e, HD * e + HD)
                        for k in range(2):
                            last = mm(ps[r, 0, p * NS:p * NS + NS], wuv[:, k, h * HD:h * HD + HD],
                                      olat[:, k, :, h * DS:h * DS + DS], start=(k == 0), stop=(k == 1))
                    last.then_inc(g["sa_o"].sem, 1)

                def leave(eng, copy, b, n, name):
                    grp, v = divmod(n, 3)
                    if grp >= 2:
                        eng.wait_ge(g["s_scores"].sem, g["s_scores"].at(b * NG + grp - 1))
                    eng.wait_ge(g["turn_c"].sem, g["turn_c"].at(b * UNITS + n + 1))
                    if v < 2:
                        last = copy(cT[:, grp % 2, 2 * v:2 * v + 2, :, :], ps[:, n % 4, :].rearrange("p (a k c) -> p a k c", a=2, k=2))
                    else:
                        last = copy(kT[:, grp % 2, :, :], ps[0:ROPE, n % 4, :].rearrange("p (a c) -> p a c", a=4))
                    last.then_inc(g[name].sem, 1)

                @block.scalar
                def _(act):
                    act.wait_ge(g["qlat_prod"].sem, g["qlat_prod"].at(1))
                    for h in range(H):
                        p, e = divmod(h, 2)
                        nc.scalar.copy(qlat[:, :, :, h * DS:h * DS + DS],
                                       ps[:, e, 2 * p * NS:(2 * p + 2) * NS].rearrange("p (k b t) -> p k b t", k=2, b=DB))
                    nc.scalar.copy(ctok[:, :], ps[0:NS, 2, 0:KV_LORA]).then_inc(g["qlat"].sem, 1)
                    act.wait_ge(g["qlat"].sem, g["qlat"].at(1))
                    with act.Fori(0, DB // 2) as b2:
                        for s in range(2):
                            b = b2 * 2 + s
                            nc.scalar.copy(qb[:, s, :, :].unsqueeze(2), qlat[:, :, bass.ds(b, 1), :])
                            nc.scalar.copy(qpb[:, s, :].rearrange("p (a h t) -> p a h t", a=1, h=H), qpe[:, bass.ds(b, 1), :, :]).then_inc(g["q_copied"].sem, 1)
                            for n in range(UNITS):
                                if by_act(n):
                                    leave(act, nc.scalar.copy, b, n, "turn_a")
                            act.wait_ge(g["s_shift"].sem, sg("s_shift", b))
                            nc.scalar.activation(pn[:, :], pn[:, :], ACT.Exp, scale=SM_SCALE)
                            nc.scalar.activation(Pb[:, :, :], Pb[:, :, :], ACT.Exp, scale=SM_SCALE).then_inc(g["s_exp"].sem, 1)
                    act.wait_ge(g["olat_prod"].sem, g["olat_prod"].at(1))
                    nc.scalar.copy(olat[:, :, :, :], ps[:, 0, :].rearrange("p (k b q) -> p k b q", k=2, b=DB)).then_inc(g["olat_done"].sem, 1)
                    act.wait_ge(g["sa_o"].sem, g["sa_o"].at(1))
                    nc.scalar.copy(z[:, Z_K:Z_K + PAIRS, S0:TP], ps[:, 0, 0:PAIRS * NS].rearrange("p (a b) -> p a b", a=PAIRS)).then_inc(g["sa_out"].sem, 1)
                    act.wait_ge(g["sa_out"].sem, g["sa_out"].at(1))

                @block.vector
                def _(dve):
                    chain = Chain(dve, self.counter("dve_own"))
                    link = chain.link
                    tt = nc.vector.tensor_tensor
                    dve.wait_ge(g["new_prod"].sem, g["new_prod"].at(1))
                    dve.wait_ge(g["sa_in"].sem, g["sa_in"].at(64))
                    tt(Sn[:, :, :], ps[0:NS, 3, 0:DB * QR].rearrange("p (b q) -> p b q", b=DB), mask[:, :, :], ALU.add).then_inc(g["new_scores"].sem, 1)
                    dve.wait_ge(g["new_scores"].sem, g["new_scores"].at(1))
                    with dve.Fori(0, DB // 2) as b2:
                        chain.iteration(b2, 10)
                        for s in range(2):
                            b = b2 * 2 + s
                            for n in range(UNITS):
                                if not by_act(n):
                                    leave(dve, nc.vector.tensor_copy, b, n, "turn_v")
                            dve.wait_ge(g["s_scores"].sem, sg("s_scores", b, NG))
                            link(nc.vector.tensor_reduce(mx[:, :], scored.rearrange("p j q -> p q j"), AX.X, ALU.max))
                            tt(mx[0:NS, :].unsqueeze(1), mx[0:NS, :].unsqueeze(1), Sn[:, bass.ds(b, 1), :], ALU.max).then_inc(g["s_max"].sem, 1)
                            dve.wait_ge(g["s_maxT"].sem, sg("s_maxT", b))
                            link(nc.vector.tensor_reduce(m1[:, :], ps[0:QR, 6, 0:P], AX.X, ALU.max))
                            nc.vector.tensor_scalar(dg[:, :], self.c("ident", slice(0, QR), hi=QR), m1[:, 0:1], None, ALU.mult).then_inc(g["s_diag"].sem, 1)
                            dve.wait_ge(g["s_maxb"].sem, sg("s_maxb", b))
                            link(nc.vector.tensor_copy(mb[:, :], ps[:, 6, P:P + QR]))
                            tt(pn[:, :].unsqueeze(1), Sn[:, bass.ds(b, 1), :], mb[0:NS, :].unsqueeze(1), ALU.subtract)
                            tt(Pb[:, :, :], scored, mb[:, :].unsqueeze(1).to_broadcast([P, N_PAGES, QR]), ALU.subtract).then_inc(g["s_shift"].sem, 1)
                            dve.wait_ge(g["s_exp"].sem, sg("s_exp", b))
                            link(nc.vector.tensor_reduce(sm[:, :], Pb[:, :, :].rearrange("p j q -> p q j"), AX.X, ALU.add))
                            tt(sm[0:NS, :], sm[0:NS, :], pn[:, :], ALU.add).then_inc(g["s_sum"].sem, 1)
                            dve.wait_ge(g["s_sumb"].sem, sg("s_sumb", b))
                            link(nc.vector.reciprocal(rinv[:, :], ps[0:QR, 6, 2 * P:2 * P + 1]))
                            dve.wait_ge(g["s_pv"].sem, sg("s_pv", b))
                            nc.vector.tensor_scalar(orow[:, :, bass.ds(b * P, P)], ps[0:QR, 7, 0:KV_LORA].rearrange("q (k c) -> q k c", k=2), rinv[:, 0:1], None, ALU.mult).then_inc(g["s_olat"].sem, 1)
                    chain.loop_over(DB // 2)
                    chain.close()
            for n, events in (("sa_in", 64), ("qlat_prod", 1), ("qlat", 1), ("new_prod", 1), ("new_scores", 1), ("olat_prod", 1), ("olat_done", 1), ("turn_c", DB * UNITS),
                              ("turn_a", DB * UNITS // 2), ("turn_v", DB * UNITS // 2), ("s_scores", DB * NG), ("sa_o", 1), ("sa_out", 1)):
                g[n].passed(events)
            for n in ("q_copied", "s_max", "s_maxT", "s_diag", "s_maxb", "s_shift", "s_exp", "s_sum", "s_sumb", "s_pv", "s_olat"):
                g[n].passed(DB)
            for one in pages_in[0] + pages_in[1]:
                one.passed(EVENTS * DB // 2)

    def pooling(self, h, y):
        nc, ps, io = self.nc, self.ps, self.io
        names = ("pool_in", "kept", "pooled", "pool_prod", "pool_y", "pool_out")
        g = {n: self.counter(n) for n in names}
        KEPT = WMAX - 1
        with ExitStack() as ctx:
            def sb(name, shape):
                return self.sb(ctx, "pl_" + name, shape)
            wp = sb("wp", [P, 4, 2, 2 * P])
            full = sb("full", [P, KC, DB, KEPT + DS])
            a, b = sb("a", [P, 2, NP]), sb("b", [P, 2, NP])
            sa, sbb = (sb(n, [P, 2, DB, KEPT + DS]) for n in ("sa", "sb"))
            pooled = sb("pooled", [P, KC, TP])
            with nc.Block() as block:
                @block.sync
                def _(sp):
                    sp.dma_start(full[:, :, :, 0:KEPT], io["pool_rows"]).then_inc(g["pool_in"].sem, 16)
                    sp.dma_start(wp[:, :, :, :], io["w_pool"]).then_inc(g["pool_in"].sem, 16)
                    sp.dma_start(io["pool_p"], h[:, :, NP - KEPT:NP]).then_inc(g["pool_out"].sem, 16)
                    sp.wait_ge(g["kept"].sem, g["kept"].at(1))
                    sp.dma_start(io["pool_s"], full[:, :, :, DS:KEPT + DS]).then_inc(g["pool_out"].sem, 16)
                    sp.wait_ge(g["pool_out"].sem, g["pool_out"].at(32))

                @block.vector
                def _(dve):
                    chain = Chain(dve, self.counter("dve_own"))
                    link = chain.link
                    tt, copy = nc.vector.tensor_tensor, nc.vector.tensor_copy
                    link(nc.vector.memset(pooled[:, :, NP:S0], 0.0))
                    dve.wait_ge(g["pool_in"].sem, g["pool_in"].at(32))
                    for k in range(KC):
                        last = copy(full[:, k, :, KEPT:], h[:, k, S0:TP].rearrange("p (b t) -> p b t", b=DB))
                    last.then_inc(g["kept"].sem, 1)
                    dve.wait_ge(g["kept"].sem, g["kept"].at(1))
                    for grp, w in enumerate(WINDOWS):
                        ks = slice(2 * grp, 2 * grp + 2)
                        src, to, other = h[:, ks, 0:NP], a[:, :, :], b[:, :, :]
                        ssrc, sto, sother = full[:, ks], sa[:, :, :, :], sbb[:, :, :, :]
                        shift, valid = 1, 0
                        if grp:
                            dve.wait_ge(g["pooled"].sem, g["pooled"].at(grp))
                        while shift < w:
                            copy(to[:, :, 0:shift], src[:, :, 0:shift])
                            tt(to[:, :, shift:], src[:, :, shift:], src[:, :, 0:NP - shift], ALU.add)
                            for k in range(2):
                                last = tt(sto[:, k, :, valid + shift:], ssrc[:, k, :, valid + shift:], ssrc[:, k, :, valid:KEPT + DS - shift], ALU.add)
                            link(last)
                            src, to, other = to, other, to
                            ssrc, sto, sother = sto, sother, sto
                            valid += shift
                            shift *= 2
                        ramp = self.c("ramp", lo=16 * grp, hi=16 * grp + 16).unsqueeze(1).to_broadcast([P, 2, 16])
                        link(tt(pooled[:, ks, 0:16], src[:, :, 0:16], ramp, ALU.mult))
                        tt(pooled[:, ks, 0:16], pooled[:, ks, 0:16], h[:, ks, 0:16], ALU.subtract)
                        for k in range(2):
                            nc.vector.scalar_tensor_tensor(out=pooled[:, 2 * grp + k, S0:TP].rearrange("p (b t) -> p b t", b=DB), in0=ssrc[:, k, :, KEPT:],
                                                           scalar=1.0 / w, in1=full[:, 2 * grp + k, :, KEPT:], op0=ALU.mult, op1=ALU.subtract)
                        nc.vector.scalar_tensor_tensor(out=pooled[:, ks, 16:NP], in0=src[:, :, 16:NP], scalar=1.0 / w, in1=h[:, ks, 16:NP],
                                                       op0=ALU.mult, op1=ALU.subtract).then_inc(g["pooled"].sem, 1)
                    dve.wait_ge(g["pooled"].sem, g["pooled"].at(4))
                    chain.close()

                @block.tensor
                def _(pe):
                    pe.wait_ge(g["pool_in"].sem, g["pool_in"].at(32))
                    for m in range(KC):
                        grp, half = divmod(m, 2)
                        pe.wait_ge(g["pooled"].sem, g["pooled"].at(grp + 1))
                        if m >= 2:
                            pe.wait_ge(g["pool_y"].sem, g["pool_y"].at(m - 1))
                        for n, (at, c) in enumerate(TILES):
                            for k in range(2):
                                last = nc.tensor.matmul(ps[:, 3 * half + n, 0:c], wp[:, grp, k, half * P:half * P + P], pooled[:, 2 * grp + k, at:at + c],
                                                        start=(k == 0), stop=(k == 1))
                        last.then_inc(g["pool_prod"].sem, 1)

                @block.scalar
                def _(act):
                    for m in range(KC):
                        act.wait_ge(g["pool_prod"].sem, g["pool_prod"].at(m + 1))
                        for n, (at, c) in enumerate(TILES):
                            last = nc.scalar.activation(y[:, m, at:at + c], ps[:, 3 * (m % 2) + n, 0:c], ACT.Copy, scale=self.v("pool_scale", m))
                        last.then_inc(g["pool_y"].sem, 1)
                    act.wait_ge(g["pool_y"].sem, g["pool_y"].at(KC))
            for n, events in (("pool_in", 32), ("kept", 1), ("pooled", 4), ("pool_prod", KC), ("pool_y", KC), ("pool_out", 32)):
                g[n].passed(events)

    def emit(self, stop_after):
        self.load()
        with ExitStack() as mix:
            self.const = self.sb(mix, "const", [P, LATE])
            last = self.sb(mix, "last", [P, 15, 1 + DB])
            with ExitStack() as inner:
                h = self.sb(inner, "h0", [P, 2, KC, TP], F32R, side="right")
                shift = self.sb(inner, "shift_rows", [P, 15, DB], side="right")
                with ExitStack() as start:
                    x0 = self.sb(start, "x0", [P, KC, TP])
                    self.fetch([(x0[:, :, :], self.io["x"]), (shift[:, :, :], self.io["shift_in"]), (self.const[:, :], self.io["const"][:, 0:LATE])])
                    self.norm("pre0", lambda k: x0[:, k, :], KC, lambda k: ("g_mix_pre", k), split=h)
                z = self.sb(mix, "z", [P, NZ, TP])
                diff = self.sb(inner, "diff", [P, 1, TP], side="right")
                self.gemm_split("in", self.io["w_in"], NZ, h, z,
                                lambda dve, emptied: self.token_shift(dve, emptied, z, diff, last, shift))
            if stop_after == 1:
                return
            self.rwkv(z, last)
            if stop_after == 2:
                return
            self.norm("q_lora", lambda k: z[:, Z_Q + k, :], 3, lambda k: ("g_q", k), lambda k: z[:, Z_Q + k, :])
            self.norm("kv_lora", lambda k: z[:, Z_KV + k, :], 2, lambda k: ("g_kv", k), lambda k: z[:, Z_KV + k, :])
            with ExitStack() as inner:
                qsn = self.sb(inner, "qsn", [P, PAIRS, NS])
                qpe = self.sb(inner, "qpe", [ROPE, DB, H, DS])
                kps = self.sb(inner, "kps", [ROPE, NS])
                self.prompt_attention(z, qsn, qpe, kps)
                if stop_after == 3:
                    return
                self.sample_attention(z, qsn, qpe, kps)
                if stop_after == 4:
                    return
            self.x = self.sb(self.top, "x", [P, KC, TP], side="right")
            y = self.sb(self.top, "y", [P, KC, TP], side="right")
            self.gemm("out", self.io["w_out"], KC, lambda k: z[:, (Z_K + k if k < PAIRS else Z_R + k - PAIRS), :], y,
                      self.x[:, :, :], self.io["x"])
        def post(name, gain, layer):
            self.norm(f"{name}{layer}", lambda k: y[:, k, :], KC, lambda k: (gain, KC * layer + k))

        for layer in range(2):
            if layer == 1:
                with ExitStack() as rest:
                    h = self.sb(rest, "h", [P, KC, TP])
                    self.norm("mix_pre1", lambda k: self.x[:, k, :], KC, lambda k: ("g_mix_pre", KC + k), lambda k: h[:, k, :])
                    self.pooling(h, y)
            post("mix_post", "g_mix_post", layer)
            with ExitStack() as rest:
                h = self.sb(rest, f"h_ffn{layer}", [P, 2, KC, TP], F32R)
                self.norm(f"ffn_pre{layer}", lambda k: self.x[:, k, :], KC, lambda k: ("g_ffn_pre", KC * layer + k), split=h)
                self.mlp(layer, h, y)
            post("ffn_post", "g_ffn_post", layer)
        self.store()

    def store(self):
        stored = self.counter("stored")
        with self.nc.Block() as block:
            @block.sync
            def _(sp):
                sp.dma_start(self.io["y"], self.x[:, :, :]).then_inc(stored.sem, 16)
                sp.wait_ge(stored.sem, stored.at(16))


def lay_out(i):
    f = {k: np.asarray(a) for k, a in i.items()}
    out = {}

    def cols(a):
        return a.reshape(-1, P).T

    def slabs(w, n):
        return w.reshape(-1, P, n, P).transpose(2, 1, 0, 3)

    tokens = np.zeros((TP, D), np.float32)
    tokens[:N_META], tokens[N_META:NP] = f["meta_tokens"], f["x_prompt"][0]
    tokens[S0:] = f["x_sample"].reshape(NS, D)
    out["x"] = tokens.T.reshape(KC, P, TP).transpose(1, 0, 2)

    half = ROPE // 2
    swap = np.concatenate([np.arange(half, ROPE), np.arange(half)])
    w = f["w_in"][0]
    mla = Q_LORA + KV_LORA + ROPE
    pe, zb = w[:, mla - ROPE:mla], w[:, mla:]
    pad = np.zeros((D, 32), np.float32)
    w = np.concatenate([w[:, :mla - ROPE], pe, zb[:, -32:], pe[:, swap], pad, zb[:, :-32]], 1)
    out["w_in"] = slabs(w, NZ)
    up, down = f["w_up"], f["w_down"]
    parts = []
    for layer in range(2):
        for fb in range(N_FB):
            hidden = slice(fb * 4 * P, (fb + 1) * 4 * P)
            parts.append(slabs(up[layer][:, hidden], 4))
            parts.append(down[layer][hidden].reshape(4, P, 4, 2, P).transpose(2, 1, 3, 0, 4).reshape(4, P, KC, P))
    out["w_mlp"] = np.concatenate(parts)

    vec = np.zeros((P, NVEC), np.float32)

    def put(name, a):
        at, n = VECS[name]
        vec[:, at:at + n] = a

    for name in ("g_mix_pre", "g_mix_post", "g_ffn_pre", "g_ffn_post", "g_q", "g_kv", "w0", "a0", "k_k", "k_a",
                 "r_k", "ln_w", "ln_b", "pool_scale"):
        put(name, cols(f[name].reshape(-1)))
    mu = f["mu_shift"][0]
    tail = np.zeros(P, np.float32)
    tail[32:64] = mu[-32:]
    put("mu", cols(np.concatenate([mu[:-32], tail])))
    out["vec"] = vec

    def rwkv_rows(a):
        r = np.zeros((15, P, a.shape[0]), np.float32)
        r[:14] = a[:, :-32].T.reshape(14, P, -1)
        r[14, 32:64] = a[:, -32:].T
        return r.transpose(1, 0, 2)

    out["shift_in"] = rwkv_rows(f["state_shift"][0])
    out["w2a2"] = np.concatenate([f["w2"][0], f["a2"][0]])
    g2 = np.zeros((P, 2, D_B), np.float32)
    g2[:, 0], g2[32:64, 1] = f["g2"][0][:P], f["g2"][0][P:]
    out["g2"] = g2
    out["w_out"] = slabs(f["w_out"][0], KC)
    out["w_pool"] = f["w_pool"][0].reshape(4, 2, P, 2 * P).transpose(2, 0, 1, 3)
    out["pool_rows"] = f["state_pool"][0].reshape(DB, WMAX - 1, KC, P).transpose(3, 2, 0, 1)
    out["rope"] = rotary_tables()
    wuq = f["w_uq"][0].reshape(3, P, PAIRS, 2, NOPE + ROPE)
    wq = np.concatenate([wuq, wuq[..., NOPE + swap]], -1)
    wk, wv = (f[n][0].reshape(2, P, PAIRS, 2, HD) for n in ("w_uk", "w_uv"))
    out["w_pair"] = np.concatenate([a.transpose(2, 1, 0, 3, 4).reshape(PAIRS, P, -1) for a in (wq, wk, wv)], 2)
    out["w_ukT"] = wk.transpose(3, 4, 2, 0, 1).reshape(P, PAIRS, KV_LORA)
    out["w_uv"] = f["w_uv"][0].reshape(2, P, H * HD).transpose(1, 0, 2)
    out["pool"] = np.concatenate([f["cache_ckv"][0], f["cache_kpe"][0]], 2)
    out["table"] = f["page_table"].astype(np.int32).reshape(1, DB * N_PAGES)
    key, seq, t = np.arange(NS)[:, None, None], np.arange(DB)[None, :, None], np.arange(H * DS)[None, None, :] % DS
    out["new_mask"] = np.where((key // DS == seq) & (key % DS <= t), 0.0, NEG).astype(np.float32)
    out["state"] = f["state_wkv"][0].reshape(DB, PAIRS, 2, HD, HD).transpose(2, 4, 1, 0, 3).reshape(P, PAIRS, DB, HD)
    out["const"] = constants()
    return {k: np.ascontiguousarray(a) for k, a in out.items()}


OUTS = {"y": (P, KC, TP), "pool_p": (P, KC, WMAX - 1), "pool_s": (P, KC, DB, WMAX - 1), "ckv": (P, 2, TP), "kpe": (ROPE, TP), "shift": (P, 15, 1 + DB), "wkv_p": (P, PAIRS, HD), "wkv_s": (P, PAIRS, DB, HD)}


def kernel(**inputs):
    import concourse.bacc as bacc
    from concourse.bass_utils import run_bass_kernel_spmd

    nc = bacc.Bacc("TRN2", target_bir_lowering=False, num_devices=1)
    arrays = lay_out(inputs)
    io = {k: nc.dram_tensor(k + "_dram", a.shape, mybir.dt.from_np(a.dtype), kind="ExternalInput").ap() for k, a in arrays.items()}
    for k, shape in OUTS.items():
        io[k] = nc.dram_tensor(k + "_dram", shape, F32, kind="ExternalOutput").ap()
    build(nc, io)
    r = run_bass_kernel_spmd(nc, [{k + "_dram": a for k, a in arrays.items()}], core_ids=[0]).results[0]
    return collect({k: r[k + "_dram"] for k in OUTS})


def collect(o):
    def tokens(a):
        rows = a.transpose(2, 1, 0).reshape(TP, -1)
        return rows[:NP], rows[S0:].reshape(DB, DS, -1)

    y_p, y_s = tokens(o["y"])
    ckv_p, ckv_s = tokens(o["ckv"])
    kpe_p, kpe_s = tokens(o["kpe"][:, None, :])
    shift = o["shift"].transpose(2, 1, 0)
    shift = np.concatenate([shift[:, :14].reshape(1 + DB, -1), shift[:, 14, 32:64]], 1)
    wkv_p = o["wkv_p"].reshape(2, HD, PAIRS, HD).transpose(2, 0, 3, 1).reshape(1, 1, H, HD, HD)
    wkv_s = o["wkv_s"].reshape(2, HD, PAIRS, DB, HD).transpose(3, 2, 0, 4, 1).reshape(1, DB, H, HD, HD)
    pool_p = o["pool_p"].transpose(2, 1, 0).reshape(1, 1, WMAX - 1, D)
    pool_s = o["pool_s"].transpose(2, 3, 1, 0).reshape(1, DB, WMAX - 1, D)
    return tuple(np.ascontiguousarray(a) for a in (
        y_p[None, N_META:], y_s, ckv_p[None, None], kpe_p[None, None], wkv_p, shift[None, None, 0], pool_p,
        ckv_s[None], kpe_s[None], wkv_s, shift[None, 1:], pool_s))
```
